# Optimizing a Trainium2 kernel written in Bass

```python
import jax, jax.numpy as jnp
from jax import lax
import numpy as np
import math

D_MODEL = 1024
BATCH = 1
SEQ = 512
DEPTH = 2

HEAD_DIM = 64
NSA_HEADS = 8
NSA_KV_GROUPS = 2
NSA_HPG = NSA_HEADS // NSA_KV_GROUPS
CMP_LEN = 32
CMP_STRIDE = 16
CMP_HIDDEN = 256
SEL_BLOCK = 64
SEL_TOPK = 16
WINDOW = 512
NSA_QBLOCK = 64
FORCE_BONUS = 1e4
GLA_HEADS = 4
GLA_DK = 32
GLA_DV = 64
GLA_RANK = 16
GLA_TAU = 16.0
GLA_CHUNK = 64
SG_GROUPS = 4
SG_CH = 64
SG_CHUNK = 128
NSA_W = NSA_HEADS * HEAD_DIM
GLA_W = GLA_HEADS * GLA_DV
SG_W = SG_GROUPS * SG_CH
D_MIX = NSA_W + GLA_W + SG_W
KV_W = NSA_KV_GROUPS * HEAD_DIM
IN_SIZES = (NSA_W, KV_W, KV_W, KV_W, KV_W, KV_W, KV_W, NSA_HEADS * 3,
            GLA_HEADS * GLA_DK, GLA_HEADS * GLA_DK, GLA_W, GLA_RANK, GLA_W, 2 * SG_W)
D_IN = sum(IN_SIZES)
D_FF = -(-8 * D_MODEL // (3 * 256)) * 256
ROPE_THETA = 10000.0
NORM_EPS = 1e-6


def rmsnorm(x, g):
    xf = x.astype(jnp.float32)
    y = xf * lax.rsqrt(jnp.mean(xf * xf, axis=-1, keepdims=True) + NORM_EPS)
    return (y * g.astype(jnp.float32)).astype(x.dtype)

def layernorm(x, g, b):
    xf = x.astype(jnp.float32)
    mu = jnp.mean(xf, axis=-1, keepdims=True)
    var = jnp.mean(jnp.square(xf - mu), axis=-1, keepdims=True)
    y = (xf - mu) * lax.rsqrt(var + NORM_EPS)
    return (y * g.astype(jnp.float32) + b.astype(jnp.float32)).astype(x.dtype)

def rope(x, pos):
    half = x.shape[-1] // 2
    inv = 1.0 / (ROPE_THETA ** (jnp.arange(half, dtype=jnp.float32) / half))
    ang = pos[:, None] * inv[None, :]
    cos = jnp.cos(ang)[None, :, None, :]
    sin = jnp.sin(ang)[None, :, None, :]
    xf = x.astype(jnp.float32)
    x1, x2 = xf[..., :half], xf[..., half:]
    return jnp.concatenate([x1 * cos - x2 * sin, x2 * cos + x1 * sin], axis=-1).astype(x.dtype)

def masked_softmax(s, mask):
    s = jnp.where(mask, s.astype(jnp.float32), -jnp.inf)
    m = jnp.max(s, axis=-1, keepdims=True)
    m = jnp.where(jnp.isfinite(m), m, 0.0)
    e = jnp.exp(s - m)
    d = jnp.sum(e, axis=-1, keepdims=True)
    return e / jnp.where(d > 0, d, 1.0)

def compress_blocks(k_raw, pos_emb, w1, w2):
    B, S, G, hd = k_raw.shape
    nc = (S - CMP_LEN) // CMP_STRIDE + 1
    idx = np.arange(nc)[:, None] * CMP_STRIDE + np.arange(CMP_LEN)[None, :]
    blk = k_raw[:, idx] + pos_emb[None, None, :, None, :]
    blk = blk.transpose(0, 1, 3, 2, 4).reshape(B, nc, G, CMP_LEN * hd)
    return jax.nn.gelu(blk @ w1) @ w2

def importance_map(nc, nsb):
    cs = np.arange(nc) * CMP_STRIDE
    ce = cs + CMP_LEN
    bs = np.arange(nsb) * SEL_BLOCK
    be = bs + SEL_BLOCK
    ov = np.clip(np.minimum(ce[:, None], be[None, :]) - np.maximum(cs[:, None], bs[None, :]), 0, None)
    return jnp.asarray(ov / CMP_LEN, jnp.float32)

def nsa_mixer(q, k_cmp_raw, v_cmp_raw, k_slc, v_slc, k_win, v_win, gates,
              cmp_pos_k, cmp_w1_k, cmp_w2_k, cmp_pos_v, cmp_w1_v, cmp_w2_v):
    B, S, _ = q.shape
    G, HPG, hd, QB = NSA_KV_GROUPS, NSA_HPG, HEAD_DIM, NSA_QBLOCK
    pos = jnp.arange(S, dtype=jnp.float32)
    q = rope(q.reshape(B, S, NSA_HEADS, hd), pos).reshape(B, S, G, HPG, hd) * (hd ** -0.5)
    nc = (S - CMP_LEN) // CMP_STRIDE + 1
    cmp_end_np = np.arange(nc) * CMP_STRIDE + CMP_LEN - 1
    kc = compress_blocks(k_cmp_raw.reshape(B, S, G, hd), cmp_pos_k, cmp_w1_k, cmp_w2_k)
    kc = rope(kc, jnp.asarray(cmp_end_np, jnp.float32))
    vc = compress_blocks(v_cmp_raw.reshape(B, S, G, hd), cmp_pos_v, cmp_w1_v, cmp_w2_v)
    cmp_end = jnp.asarray(cmp_end_np, jnp.int32)
    nsb = S // SEL_BLOCK
    topk = min(SEL_TOPK, nsb)
    ks = rope(k_slc.reshape(B, S, G, hd), pos)
    kb = ks.reshape(B, nsb, SEL_BLOCK, G, hd).transpose(0, 3, 1, 2, 4)
    vb = v_slc.reshape(B, nsb, SEL_BLOCK, G, hd).transpose(0, 3, 1, 2, 4)
    imp_map = importance_map(nc, nsb)
    blk_id = jnp.arange(nsb)
    bi = jnp.arange(B)[:, None, None, None]
    gi = jnp.arange(G)[None, :, None, None]
    kw = jnp.pad(rope(k_win.reshape(B, S, G, hd), pos), ((0, 0), (WINDOW, 0), (0, 0), (0, 0)))
    vw = jnp.pad(v_win.reshape(B, S, G, hd), ((0, 0), (WINDOW, 0), (0, 0), (0, 0)))
    gates = jax.nn.sigmoid(gates).reshape(B, S, G, HPG, 3)

    def query_block(i):
        s0 = i * QB
        t = s0 + jnp.arange(QB)
        qb = lax.dynamic_slice_in_dim(q, s0, QB, axis=1)
        gb = lax.dynamic_slice_in_dim(gates, s0, QB, axis=1)
        s = jnp.einsum('bqghd,bcgd->bghqc', qb, kc)
        p_cmp = masked_softmax(s, (cmp_end[None, :] <= t[:, None])[None, None, None])
        o_cmp = jnp.einsum('bghqc,bcgd->bqghd', p_cmp.astype(vc.dtype), vc)
        imp = jnp.einsum('bghqc,cn->bgqn', p_cmp, imp_map)
        tb = t // SEL_BLOCK
        valid = blk_id[None, :] * SEL_BLOCK <= t[:, None]
        forced = (blk_id[None, :] == 0) | (blk_id[None, :] == tb[:, None]) | (blk_id[None, :] == tb[:, None] - 1)
        score = jnp.where(valid, imp + jnp.where(forced, FORCE_BONUS, 0.0), -jnp.inf)
        _, idx = lax.top_k(score, topk)
        ksel = kb[bi, gi, idx].reshape(B, G, QB, topk * SEL_BLOCK, hd)
        vsel = vb[bi, gi, idx].reshape(B, G, QB, topk * SEL_BLOCK, hd)
        tok = (idx[..., None] * SEL_BLOCK + jnp.arange(SEL_BLOCK)).reshape(B, G, 1, QB, topk * SEL_BLOCK)
        s = jnp.einsum('bqghd,bgqmd->bghqm', qb, ksel)
        p = masked_softmax(s, tok <= t[None, None, None, :, None])
        o_slc = jnp.einsum('bghqm,bgqmd->bqghd', p.astype(vsel.dtype), vsel)
        kwb = lax.dynamic_slice_in_dim(kw, s0, WINDOW + QB, axis=1)
        vwb = lax.dynamic_slice_in_dim(vw, s0, WINDOW + QB, axis=1)
        kpos = s0 - WINDOW + jnp.arange(WINDOW + QB)
        wmask = (kpos[None, :] <= t[:, None]) & (kpos[None, :] > t[:, None] - WINDOW) & (kpos[None, :] >= 0)
        s = jnp.einsum('bqghd,bkgd->bghqk', qb, kwb)
        p = masked_softmax(s, wmask[None, None, None])
        o_win = jnp.einsum('bghqk,bkgd->bqghd', p.astype(vwb.dtype), vwb)
        return gb[..., 0:1] * o_cmp + gb[..., 1:2] * o_slc + gb[..., 2:3] * o_win

    out = lax.map(query_block, jnp.arange(S // QB))
    return out.transpose(1, 0, 2, 3, 4, 5).reshape(B, S, NSA_W)

def gla_mixer(q, k, v, a_lr, r, w_up, b_up, norm_g):
    B, S, _ = q.shape
    H, DK, DV, C = GLA_HEADS, GLA_DK, GLA_DV, GLA_CHUNK
    f32 = jnp.float32
    q = q.reshape(B, S, H, DK).astype(f32) * (DK ** -0.5)
    k = k.reshape(B, S, H, DK).astype(f32)
    v = v.reshape(B, S, H, DV).astype(f32)
    g = jax.nn.log_sigmoid((a_lr @ w_up + b_up).astype(f32)).reshape(B, S, H, DK) / GLA_TAU
    n = S // C

    def to_chunks(a):
        return a.reshape(B, n, C, H, a.shape[-1]).transpose(1, 0, 3, 2, 4)

    causal = jnp.tril(jnp.ones((C, C), dtype=bool))

    def step(state, inp):
        qc, kc, vc, gc = inp
        bcum = jnp.cumsum(gc, axis=2)
        o_inter = jnp.einsum('bhck,bhkv->bhcv', qc * jnp.exp(bcum), state)
        diff = bcum[:, :, :, None, :] - bcum[:, :, None, :, :]
        decay = jnp.exp(jnp.where(causal[None, None, :, :, None], diff, -jnp.inf))
        attn = jnp.einsum('bhik,bhjk,bhijk->bhij', qc, kc, decay)
        o_intra = jnp.einsum('bhij,bhjv->bhiv', attn, vc)
        blast = bcum[:, :, -1:, :]
        state = jnp.exp(blast[:, :, 0, :])[..., None] * state + jnp.einsum(
            'bhjk,bhjv->bhkv', kc * jnp.exp(blast - bcum), vc)
        return state, o_inter + o_intra

    state0 = jnp.zeros((B, H, DK, DV), f32)
    _, o = lax.scan(step, state0, (to_chunks(q), to_chunks(k), to_chunks(v), to_chunks(g)))
    o = o.transpose(1, 0, 3, 2, 4).reshape(B, S, H, DV)
    o = rmsnorm(o, norm_g) * jax.nn.silu(r.astype(f32)).reshape(B, S, H, DV)
    return o.reshape(B, S, GLA_W).astype(r.dtype)

def spatial_gating(uv, ln_g, ln_b, w_s, b_s):
    B, S, _ = uv.shape
    nch = S // SG_CHUNK
    u, v = jnp.split(jax.nn.gelu(uv), 2, axis=-1)
    v = layernorm(v, ln_g, ln_b).reshape(B, nch, SG_CHUNK, SG_GROUPS, SG_CH)
    w = jnp.tril(w_s)
    s = jnp.einsum('gij,bnjgc->bnigc', w, v) + b_s.T[None, None, :, :, None]
    out = u.reshape(B, nch, SG_CHUNK, SG_GROUPS, SG_CH) * s
    return out.reshape(B, S, SG_W)

def split_columns(z):
    offs = np.cumsum(IN_SIZES)[:-1]
    return jnp.split(z, [int(o) for o in offs], axis=-1)

def first_inputs(seed: int = 0) -> dict:
    key = jax.random.key(seed)
    ks = jax.random.split(key, 32)
    L = DEPTH
    res = (2.0 * DEPTH) ** -0.5

    def nrm(k, shape, scale):
        return jax.random.normal(k, shape, jnp.float32) * scale

    def gain(k, shape):
        return 1.0 + nrm(k, shape, 0.02)

    return {
        "x": nrm(ks[0], (BATCH, SEQ, D_MODEL), 1.0),
        "attn_norm": gain(ks[1], (L, D_MODEL)),
        "w_in": nrm(ks[2], (L, D_MODEL, D_IN), D_MODEL ** -0.5),
        "cmp_pos_k": nrm(ks[3], (L, CMP_LEN, HEAD_DIM), 0.1),
        "cmp_w1_k": nrm(ks[4], (L, CMP_LEN * HEAD_DIM, CMP_HIDDEN), (CMP_LEN * HEAD_DIM) ** -0.5),
        "cmp_w2_k": nrm(ks[5], (L, CMP_HIDDEN, HEAD_DIM), CMP_HIDDEN ** -0.5),
        "cmp_pos_v": nrm(ks[6], (L, CMP_LEN, HEAD_DIM), 0.1),
        "cmp_w1_v": nrm(ks[7], (L, CMP_LEN * HEAD_DIM, CMP_HIDDEN), (CMP_LEN * HEAD_DIM) ** -0.5),
        "cmp_w2_v": nrm(ks[8], (L, CMP_HIDDEN, HEAD_DIM), CMP_HIDDEN ** -0.5),
        "gla_w_up": nrm(ks[9], (L, GLA_RANK, GLA_HEADS * GLA_DK), GLA_RANK ** -0.5),
        "gla_b_up": nrm(ks[10], (L, GLA_HEADS * GLA_DK), 0.1),
        "gla_norm": gain(ks[11], (L, GLA_DV)),
        "sg_ln_g": gain(ks[12], (L, SG_W)),
        "sg_ln_b": nrm(ks[13], (L, SG_W), 0.02),
        "sg_w": nrm(ks[14], (L, SG_GROUPS, SG_CHUNK, SG_CHUNK), SG_CHUNK ** -0.5),
        "sg_b": 1.0 + nrm(ks[15], (L, SG_GROUPS, SG_CHUNK), 0.1),
        "w_out": nrm(ks[16], (L, D_MIX, D_MODEL), D_MIX ** -0.5 * res),
        "ffn_norm": gain(ks[17], (L, D_MODEL)),
        "w_gate": nrm(ks[18], (L, D_MODEL, D_FF), D_MODEL ** -0.5),
        "w_up": nrm(ks[19], (L, D_MODEL, D_FF), D_MODEL ** -0.5),
        "w_down": nrm(ks[20], (L, D_FF, D_MODEL), D_FF ** -0.5 * res),
        "final_norm": gain(ks[21], (D_MODEL,)),
    }

def first_block(x, attn_norm, w_in, cmp_pos_k, cmp_w1_k, cmp_w2_k, cmp_pos_v, cmp_w1_v, cmp_w2_v,
              gla_w_up, gla_b_up, gla_norm, sg_ln_g, sg_ln_b, sg_w, sg_b, w_out,
              ffn_norm, w_gate, w_up, w_down, final_norm):
    for l in range(DEPTH):
        h = rmsnorm(x, attn_norm[l])
        (q, kc, vc, ksl, vsl, kwn, vwn, gts, gq, gk, gv, ga, gr, uv) = split_columns(h @ w_in[l])
        o_nsa = nsa_mixer(q, kc, vc, ksl, vsl, kwn, vwn, gts,
                          cmp_pos_k[l], cmp_w1_k[l], cmp_w2_k[l], cmp_pos_v[l], cmp_w1_v[l], cmp_w2_v[l])
        o_gla = gla_mixer(gq, gk, gv, ga, gr, gla_w_up[l], gla_b_up[l], gla_norm[l])
        o_sg = spatial_gating(uv, sg_ln_g[l], sg_ln_b[l], sg_w[l], sg_b[l])
        x = x + jnp.concatenate([o_nsa, o_gla.astype(x.dtype), o_sg], axis=-1) @ w_out[l]
        h = rmsnorm(x, ffn_norm[l])
        x = x + (jax.nn.silu(h @ w_gate[l]) * (h @ w_up[l])) @ w_down[l]
    return rmsnorm(x, final_norm)


DEPTH_2 = 1

GRID_W = 64
CTX_LEN = 256
Q_BLOCK = 128
DIFF_HEADS = 4
DIFF_V_DIM = 2 * HEAD_DIM
DIFF_WIDTH = DIFF_HEADS * DIFF_V_DIM
GQA_Q_HEADS = 8
GQA_KV_HEADS = 2
GQA_GROUP = GQA_Q_HEADS // GQA_KV_HEADS
GQA_WIDTH = GQA_Q_HEADS * HEAD_DIM
MIX_WIDTH = DIFF_WIDTH + GQA_WIDTH
GQA_KV_WIDTH = GQA_KV_HEADS * HEAD_DIM
IN_COLS = 3 * DIFF_WIDTH + GQA_WIDTH + 2 * GQA_KV_WIDTH
_IN_SPLITS = (DIFF_WIDTH, 2 * DIFF_WIDTH, 3 * DIFF_WIDTH,
              3 * DIFF_WIDTH + GQA_WIDTH, 3 * DIFF_WIDTH + GQA_WIDTH + GQA_KV_WIDTH)
PEER_HEADS = 8
PEER_N_KEYS = 128
PEER_N_EXPERTS = PEER_N_KEYS * PEER_N_KEYS
PEER_QUERY_DIM = 256
PEER_HALF = PEER_QUERY_DIM // 2
PEER_TOPK = 16
PEER_CHUNK = 128


def rmsnorm_2(x, g):
    xf = x.astype(jnp.float32)
    y = xf * lax.rsqrt(jnp.mean(xf * xf, axis=-1, keepdims=True) + NORM_EPS)
    return (y * g.astype(jnp.float32)).astype(x.dtype)

def modulate(h, shift, scale):
    return h * (1 + scale) + shift

def _rope_axis(x, pos):
    d = x.shape[-1]
    half = d // 2
    freqs = ROPE_THETA ** (-jnp.arange(half, dtype=jnp.float32) / half)
    ang = pos.astype(jnp.float32)[:, None] * freqs[None, :]
    shape = (1, x.shape[1]) + (1,) * (x.ndim - 3) + (half,)
    cos = jnp.cos(ang).reshape(shape).astype(x.dtype)
    sin = jnp.sin(ang).reshape(shape).astype(x.dtype)
    x1, x2 = x[..., :half], x[..., half:]
    return jnp.concatenate([x1 * cos - x2 * sin, x1 * sin + x2 * cos], axis=-1)

def rope2d(x):
    n = x.shape[1]
    rows = n // GRID_W
    row_pos = jnp.broadcast_to(jnp.arange(rows, dtype=jnp.int32)[:, None], (rows, GRID_W)).reshape(-1)
    col_pos = jnp.broadcast_to(jnp.arange(GRID_W, dtype=jnp.int32)[None, :], (rows, GRID_W)).reshape(-1)
    d = x.shape[-1] // 2
    return jnp.concatenate([_rope_axis(x[..., :d], row_pos), _rope_axis(x[..., d:], col_pos)], axis=-1)

def attend(q, k, v):
    B, S, Hk, G, d = q.shape
    nb = S // Q_BLOCK
    qb = q.reshape(B, nb, Q_BLOCK, Hk, G, d).swapaxes(0, 1)
    scale = d ** -0.5

    def one(qblk):
        s = jnp.einsum('bqhgd,bkhd->bhgqk', qblk, k, preferred_element_type=jnp.float32) * scale
        p = jax.nn.softmax(s, axis=-1).astype(v.dtype)
        return jnp.einsum('bhgqk,bkhe->bqhge', p, v)

    o = lax.map(one, qb)
    return o.swapaxes(0, 1).reshape(B, S, Hk, G, v.shape[-1])

def _mixer_heads(p):
    B, S, _ = p.shape
    dq, dk, dv, gq, gk, gv = jnp.split(p, _IN_SPLITS, axis=-1)
    return (dq.reshape(B, S, DIFF_HEADS, 2, HEAD_DIM),
            dk.reshape(B, S, DIFF_HEADS, 2, HEAD_DIM),
            dv.reshape(B, S, DIFF_HEADS, DIFF_V_DIM),
            gq.reshape(B, S, GQA_Q_HEADS, HEAD_DIM),
            gk.reshape(B, S, GQA_KV_HEADS, HEAD_DIM),
            gv.reshape(B, S, GQA_KV_HEADS, HEAD_DIM))

def _mix_queries(dq, gq, dk, dv, gk, gv, lam, lambda_init, subln_g, w_out):
    B, S = dq.shape[:2]
    o1 = attend(dq[:, :, :, 0, None, :], dk[:, :, :, 0, :], dv)
    o2 = attend(dq[:, :, :, 1, None, :], dk[:, :, :, 1, :], dv)
    od = (o1 - lam.astype(o1.dtype) * o2)[:, :, :, 0, :]
    od = rmsnorm_2(od, subln_g) * (1.0 - lambda_init)
    og = attend(gq.reshape(B, S, GQA_KV_HEADS, GQA_GROUP, HEAD_DIM), gk, gv)
    o = jnp.concatenate([od.reshape(B, S, DIFF_WIDTH), og.reshape(B, S, GQA_WIDTH)], axis=-1)
    return o @ w_out

def peer(h, w_q, subkeys, u, v):
    B, S, D = h.shape
    xs = h.reshape(-1, PEER_CHUNK, D)

    def one(xc):
        C = xc.shape[0]
        q = (xc @ w_q).reshape(C, PEER_HEADS, 2, PEER_HALF)
        s = jnp.einsum('chpd,hpnd->chpn', q, subkeys, preferred_element_type=jnp.float32)
        sv, si = lax.top_k(s, PEER_TOPK)
        cand = sv[:, :, 0, :, None] + sv[:, :, 1, None, :]
        cand_id = si[:, :, 0, :, None] * PEER_N_KEYS + si[:, :, 1, None, :]
        best, pos = lax.top_k(cand.reshape(C, PEER_HEADS, PEER_TOPK * PEER_TOPK), PEER_TOPK)
        ids = jnp.take_along_axis(cand_id.reshape(C, PEER_HEADS, PEER_TOPK * PEER_TOPK), pos, axis=-1)
        g = jax.nn.softmax(best, axis=-1)
        ue = jnp.take(u, ids, axis=0)
        ve = jnp.take(v, ids, axis=0)
        a = jax.nn.gelu(jnp.einsum('cd,chkd->chk', xc, ue), approximate=False)
        return jnp.einsum('chk,chkd->cd', (g * a).astype(xc.dtype), ve)

    return lax.map(one, xs).reshape(B, S, D)

def second_inputs(seed: int = 0) -> dict:
    key = jax.random.key(seed)
    ks = jax.random.split(key, 24)
    D = D_MODEL
    nrm = lambda k, shape, s: jax.random.normal(k, shape, jnp.float32) * s
    return {
        "x": nrm(ks[0], (BATCH, SEQ, D), 1.0),
        "c": nrm(ks[1], (BATCH, D), 1.0),
        "ctx": nrm(ks[2], (BATCH, CTX_LEN, D), 1.0),
        "c_ctx": nrm(ks[3], (D,), 1.0),
        "w_mod": nrm(ks[4], (DEPTH_2, D, 6 * D), 0.5 * D ** -0.5),
        "b_mod": nrm(ks[5], (DEPTH_2, 6 * D), 0.01),
        "norm1_g": 1.0 + nrm(ks[6], (DEPTH_2, D), 0.02),
        "norm2_g": 1.0 + nrm(ks[7], (DEPTH_2, D), 0.02),
        "w_in": nrm(ks[8], (DEPTH_2, D, IN_COLS), D ** -0.5),
        "w_out": nrm(ks[9], (DEPTH_2, MIX_WIDTH, D), MIX_WIDTH ** -0.5),
        "diff_lq1": nrm(ks[10], (DEPTH_2, HEAD_DIM), 0.1),
        "diff_lk1": nrm(ks[11], (DEPTH_2, HEAD_DIM), 0.1),
        "diff_lq2": nrm(ks[12], (DEPTH_2, HEAD_DIM), 0.1),
        "diff_lk2": nrm(ks[13], (DEPTH_2, HEAD_DIM), 0.1),
        "diff_subln_g": 1.0 + nrm(ks[14], (DEPTH_2, DIFF_V_DIM), 0.02),
        "gqa_q_norm_g": 1.0 + nrm(ks[15], (DEPTH_2, HEAD_DIM), 0.02),
        "gqa_k_norm_g": 1.0 + nrm(ks[16], (DEPTH_2, HEAD_DIM), 0.02),
        "peer_wq": nrm(ks[17], (DEPTH_2, D, PEER_HEADS * PEER_QUERY_DIM), D ** -0.5),
        "peer_subkeys": nrm(ks[18], (DEPTH_2, PEER_HEADS, 2, PEER_N_KEYS, PEER_HALF), PEER_HALF ** -0.5),
        "peer_u": nrm(ks[19], (DEPTH_2, PEER_N_EXPERTS, D), D ** -0.5),
        "peer_v": nrm(ks[20], (DEPTH_2, PEER_N_EXPERTS, D), (PEER_HEADS * PEER_TOPK) ** -0.5),
        "final_norm_g": 1.0 + nrm(ks[21], (D,), 0.02),
    }

def second_block(x, c, ctx, c_ctx, w_mod, b_mod, norm1_g, norm2_g, w_in, w_out,
              diff_lq1, diff_lk1, diff_lq2, diff_lk2, diff_subln_g,
              gqa_q_norm_g, gqa_k_norm_g, peer_wq, peer_subkeys, peer_u, peer_v,
              final_norm_g):
    for i in range(DEPTH_2):
        last = i == DEPTH_2 - 1
        lambda_init = 0.8 - 0.6 * math.exp(-0.3 * i)
        mod_x = (jax.nn.silu(c) @ w_mod[i] + b_mod[i])[:, None, :]
        mod_c = jax.nn.silu(c_ctx) @ w_mod[i] + b_mod[i]
        sh1x, sc1x, g1x, sh2x, sc2x, g2x = jnp.split(mod_x, 6, axis=-1)
        sh1c, sc1c, g1c, sh2c, sc2c, g2c = jnp.split(mod_c, 6, axis=-1)

        hx = modulate(rmsnorm_2(x, norm1_g[i]), sh1x, sc1x)
        hc = modulate(rmsnorm_2(ctx, norm1_g[i]), sh1c, sc1c)
        c_dq, c_dk, c_dv, c_gq, c_gk, c_gv = _mixer_heads(hc @ w_in[i])
        x_dq, x_dk, x_dv, x_gq, x_gk, x_gv = _mixer_heads(hx @ w_in[i])
        c_gq = rmsnorm_2(c_gq, gqa_q_norm_g[i])
        c_gk = rmsnorm_2(c_gk, gqa_k_norm_g[i])
        x_gq = rope2d(rmsnorm_2(x_gq, gqa_q_norm_g[i]))
        x_gk = rope2d(rmsnorm_2(x_gk, gqa_k_norm_g[i]))
        x_dq = rope2d(x_dq)
        x_dk = rope2d(x_dk)
        lam = (jnp.exp(jnp.sum(diff_lq1[i].astype(jnp.float32) * diff_lk1[i].astype(jnp.float32)))
               - jnp.exp(jnp.sum(diff_lq2[i].astype(jnp.float32) * diff_lk2[i].astype(jnp.float32)))
               + lambda_init)
        out_x = _mix_queries(x_dq, x_gq,
                             jnp.concatenate([c_dk, x_dk], axis=1),
                             jnp.concatenate([c_dv, x_dv], axis=1),
                             jnp.concatenate([c_gk, x_gk], axis=1),
                             jnp.concatenate([c_gv, x_gv], axis=1),
                             lam, lambda_init, diff_subln_g[i], w_out[i])
        if not last:
            out_c = _mix_queries(c_dq, c_gq, c_dk, c_dv, c_gk, c_gv,
                                 lam, lambda_init, diff_subln_g[i], w_out[i])
            ctx = ctx + g1c * out_c
        x = x + g1x * out_x

        hx2 = modulate(rmsnorm_2(x, norm2_g[i]), sh2x, sc2x)
        x = x + g2x * peer(hx2, peer_wq[i], peer_subkeys[i], peer_u[i], peer_v[i])
        if not last:
            hc2 = modulate(rmsnorm_2(ctx, norm2_g[i]), sh2c, sc2c)
            ctx = ctx + g2c * peer(hc2, peer_wq[i], peer_subkeys[i], peer_u[i], peer_v[i])
    return rmsnorm_2(x, final_norm_g)


def setup_inputs(seed=0):
    out = dict(first_inputs(seed))
    for name, value in second_inputs(seed + 1).items():
        if name != "x":
            out[name + "_2"] = value
    return out


def reference(
    x, attn_norm, w_in, cmp_pos_k, cmp_w1_k, cmp_w2_k, cmp_pos_v, cmp_w1_v, cmp_w2_v, gla_w_up,
    gla_b_up, gla_norm, sg_ln_g, sg_ln_b, sg_w, sg_b, w_out, ffn_norm, w_gate, w_up, w_down,
    final_norm, c_2, ctx_2, c_ctx_2, w_mod_2, b_mod_2, norm1_g_2, norm2_g_2, w_in_2, w_out_2,
    diff_lq1_2, diff_lk1_2, diff_lq2_2, diff_lk2_2, diff_subln_g_2, gqa_q_norm_g_2,
    gqa_k_norm_g_2, peer_wq_2, peer_subkeys_2, peer_u_2, peer_v_2, final_norm_g_2,
):
    x = first_block(
        x, attn_norm, w_in, cmp_pos_k, cmp_w1_k, cmp_w2_k, cmp_pos_v, cmp_w1_v, cmp_w2_v,
        gla_w_up, gla_b_up, gla_norm, sg_ln_g, sg_ln_b, sg_w, sg_b, w_out, ffn_norm, w_gate,
        w_up, w_down, final_norm,
    )
    return second_block(
        x, c_2, ctx_2, c_ctx_2, w_mod_2, b_mod_2, norm1_g_2, norm2_g_2, w_in_2, w_out_2,
        diff_lq1_2, diff_lk1_2, diff_lq2_2, diff_lk2_2, diff_subln_g_2, gqa_q_norm_g_2,
        gqa_k_norm_g_2, peer_wq_2, peer_subkeys_2, peer_u_2, peer_v_2, final_norm_g_2,
    )


_drawn_inputs = setup_inputs


def setup_inputs(seed=0):
    import zlib

    import numpy as np

    out = dict(_drawn_inputs(seed))
    spreads = {}
    factors = {'attn_norm': 4.719,
     'cmp_pos_k': 8.0,
     'cmp_pos_v': 3.573,
     'gla_b_up': 5.949,
     'gla_norm': 8.0,
     'sg_ln_g': 8.0,
     'sg_ln_b': 8.0,
     'ffn_norm': 4.953,
     'final_norm': 2.759,
     'b_mod_2': 6.382,
     'norm1_g_2': 8.0,
     'norm2_g_2': 8.0,
     'diff_lq1_2': 8.0,
     'diff_lk1_2': 8.0,
     'diff_lq2_2': 5.757,
     'diff_lk2_2': 3.771,
     'diff_subln_g_2': 8.0,
     'gqa_q_norm_g_2': 8.0,
     'gqa_k_norm_g_2': 8.0,
     'peer_wq_2': 3.835,
     'peer_subkeys_2': 3.808,
     'peer_u_2': 4.279,
     'peer_v_2': 3.805,
     'final_norm_g_2': 2.838}
    for name, (base, spread) in spreads.items():
        noise = np.random.default_rng([zlib.crc32(name.encode()), seed]).standard_normal(out[name].shape)
        drawn = base * np.exp(spread * noise) if base else spread * noise
        out[name] = __import__('jax').numpy.asarray(drawn.astype(out[name].dtype))
    for name, factor in factors.items():
        out[name] = (out[name] * factor).astype(out[name].dtype)
    return out
```

```python
import itertools
from contextlib import ExitStack

import numpy as np
import concourse.bass as bass
from concourse import mybir

F32 = mybir.dt.float32
BF16 = mybir.dt.bfloat16
U32 = mybir.dt.uint32
ALU = mybir.AluOpType
ACT = mybir.ActivationFunctionType
AX_X = mybir.AxisListType.X

P = 128
D = 1024
KT = D // P
S = 512
ST = S // P
CTX = 256
HD = 64
DEPTH = 2
FF = 2816
FT = FF // P
NC_BLK = (S - 32) // 16 + 1
EPS = 1e-6
MASK = -1e30
MAX_FLOOR = -1e29
Z_Q, Z_KC, Z_VC, Z_KS, Z_KW, Z_GQ, Z_GK, Z_GR, Z_U = 0, 512, 640, 768, 896, 1024, 1152, 1280, 1536
Z_ROWS = 1792
T_VS, T_VW, T_GV, T_V = 0, 128, 256, 512
T_COLS = 768
Y_DQ, Y_GQ, Y_DK, Y_GK = 0, 512, 1024, 1536
Y_ROWS, YC_ROWS, Y2_COLS = 1664, 640, 640
GLA_LEVELS = [2, 4, 8, 16, 32, 64, 128, 256, 512]
TOPK = 16
PH = 8
NKEY = 128
PICKS = PH * TOPK


NAMES = itertools.count()


def sbuf(nc, shape, dt):
    return nc.sbuf_tensor(f"sbuf{next(NAMES)}", shape, dt)


def psum(nc, shape, dt):
    return nc.psum_tensor(f"psum{next(NAMES)}", shape, dt)


class Sems:

    def __init__(self, nc, ctx):
        self.nc, self.ctx = nc, ctx

    def one(self, name, credit=0):
        handle = self.ctx.enter_context(self.nc.semaphore(f"{name}_{next(NAMES)}"))
        self.ctx.callback(self.nc.gpsimd.sem_clear, handle)
        if credit:
            self.nc.gpsimd.sem_inc(handle, credit)
        return handle

    def two(self, name, credit=0):
        return [self.one(name + "0", credit), self.one(name + "1", credit)]


def wait_apart(eng, sem, value, passed):
    eng.wait_ge(sem, value)
    eng.sem_inc(passed, 1)


def paired(eng, n, body):
    if n // 2:
        with eng.Fori(0, n // 2) as p:
            body(p, 0)
            body(p, 1)
    if n % 2:
        body(n // 2, 0)


def load_all(nc, moves):
    with ExitStack() as ctx:
        landed = Sems(nc, ctx).one("copies_landed")
        block = ctx.enter_context(nc.Block())

        @block.sync
        def _(sp):
            for dst, src in moves:
                sp.dma_start(dst, src).then_inc(landed, 16)
            sp.wait_ge(landed, 16 * len(moves))


def rmsnorm(nc, C, src, gain, dst, n=S, shift=None, kt=KT, store=None):
    with ExitStack() as ctx:
        sem = Sems(nc, ctx)
        squares = ctx.enter_context(sbuf(nc, [P, kt, S], F32))
        root = ctx.enter_context(sbuf(nc, [P, S], F32))
        inv = ctx.enter_context(sbuf(nc, [P, S], F32))
        total = ctx.enter_context(psum(nc, [P, S], F32))
        squared, summed, rooted, inverted, scaled, done, stored = [
            sem.one(x) for x in ("squared", "summed", "rooted", "inverted", "scaled", "norm_done", "norm_stored")]
        block = ctx.enter_context(nc.Block())

        @block.scalar
        def _(act):
            for k in range(kt):
                nc.scalar.activation(squares[:, k, :n], src[:, k, :n], ACT.Square).then_inc(squared, 1)
            act.wait_ge(summed, 1)
            nc.scalar.activation(root[:, :n], total[:, :n], ACT.Sqrt, bias=C.eps[:, 0:1],
                                 scale=1.0 / (kt * P)).then_inc(rooted, 1)

        @block.tensor
        def _(pe):
            for k in range(kt):
                pe.wait_ge(squared, k + 1)
                mm = nc.tensor.matmul(total[:, :n], C.ones[:, :], squares[:, k, :n], start=(k == 0), stop=(k == kt - 1))
            mm.then_inc(summed, 1)

        @block.vector
        def _(dve):
            dve.wait_ge(rooted, 1)
            nc.vector.reciprocal(inv[:, :n], root[:, :n]).then_inc(inverted, 1)
            dve.wait_ge(inverted, 1)
            for k in range(kt):
                op = nc.vector.scalar_tensor_tensor(dst[:, k, :n], src[:, k, :n], gain[:, k:k + 1], inv[:, :n],
                                                    ALU.mult, ALU.mult)
                op.then_inc(scaled, 1)
                if shift is not None:
                    dve.wait_ge(scaled, k + 1)
                    nc.vector.tensor_scalar(dst[:, k, :n], dst[:, k, :n], shift[:, k:k + 1], None,
                                            ALU.add).then_inc(done, 1)

        @block.sync
        def _(sp):
            if store is not None:
                for k in range(kt):
                    sp.wait_ge(done if shift is not None else scaled, k + 1)
                    sp.dma_start(store[k * P:(k + 1) * P, :], dst[:, k, :n]).then_inc(stored, 16)
                sp.wait_ge(stored, 16 * kt)


def project(nc, C, weight, n, rhs, cols, dst):
    with ExitStack() as ctx:
        sem = Sems(nc, ctx)
        w = ctx.enter_context(sbuf(nc, [P, 2, KT * P], F32))
        out = ctx.enter_context(sbuf(nc, [P, 2, cols], F32))
        acc = ctx.enter_context(psum(nc, [P, 2, S], F32))
        w_landed = sem.two("w_landed")
        mm_done, evacuated, stored = sem.two("mm_done", 1), sem.two("evacuated", 1), sem.two("stored", 16)
        block = ctx.enter_context(nc.Block())

        @block.sync
        def _(sp):
            def body(p, s):
                sp.wait_ge(mm_done[s], p + 1)
                sp.dma_start(w[:, s, :], weight[2 * p + s]).then_inc(w_landed[s], 16)
            paired(sp, n, body)

        @block.tensor
        def _(pe):
            def body(p, s):
                pe.wait_ge(evacuated[s], p + 1)
                pe.wait_ge(w_landed[s], 16 * p + 16)
                for k in range(KT):
                    mm = nc.tensor.matmul(acc[:, s, :cols], w[:, s, k * P:(k + 1) * P], rhs(k),
                                          start=(k == 0), stop=(k == KT - 1))
                mm.then_inc(mm_done[s], 1)
            paired(pe, n, body)

        @block.scalar
        def _(act):
            def body(p, s):
                act.wait_ge(stored[s], 16 * p + 16)
                act.wait_ge(mm_done[s], p + 2)
                nc.scalar.activation(out[:, s, :], acc[:, s, :cols], ACT.Copy).then_inc(evacuated[s], 1)
                act.wait_ge(evacuated[s], p + 2)
                act.dma_start(dst[bass.ds((2 * p + s) * P, P), :], out[:, s, :]).then_inc(stored[s], 16)
            paired(act, n, body)
            for s in range(min(2, n)):
                act.wait_ge(stored[s], 16 * ((n + 1 - s) // 2) + 16)


def project_tokens(nc, C, weight, width, tiles, lhs, dst):
    with ExitStack() as ctx:
        sem = Sems(nc, ctx)
        w = ctx.enter_context(sbuf(nc, [P, KT, width], F32))
        out = ctx.enter_context(sbuf(nc, [P, tiles, width], F32))
        acc = ctx.enter_context(psum(nc, [P, 2, 2 * S], F32))
        w_landed, mm_done, evacuated, stored = [sem.one(x) for x in ("w_landed", "mm_done", "evacuated", "stored")]
        block = ctx.enter_context(nc.Block())
        half = width // 2

        @block.sync
        def _(sp):
            for k in range(KT):
                sp.dma_start(w[:, k, :], weight[k * P:(k + 1) * P, :]).then_inc(w_landed, 16)
            for t in range(tiles):
                sp.wait_ge(evacuated, 2 * t + 2)
                sp.dma_start(dst[t * P:(t + 1) * P, :], out[:, t, :]).then_inc(stored, 16)
            sp.wait_ge(stored, 16 * tiles)

        @block.tensor
        def _(pe):
            pe.wait_ge(w_landed, 16 * KT)
            for t in range(tiles):
                if t >= 2:
                    pe.wait_ge(evacuated, 2 * (t - 1))
                for c in range(2):
                    for k in range(KT):
                        mm = nc.tensor.matmul(acc[:, t % 2, c * S:c * S + half], lhs(k, t),
                                              w[:, k, c * half:(c + 1) * half], start=(k == 0), stop=(k == KT - 1))
                    mm.then_inc(mm_done, 1)

        @block.scalar
        def _(act):
            for t in range(tiles):
                for c in range(2):
                    act.wait_ge(mm_done, 2 * t + c + 1)
                    nc.scalar.activation(out[:, t, c * half:(c + 1) * half], acc[:, t % 2, c * S:c * S + half],
                                         ACT.Copy).then_inc(evacuated, 1)


def project_add(nc, C, weight, kt, rhs, x, gate=None):
    with ExitStack() as ctx:
        sem = Sems(nc, ctx)
        w = ctx.enter_context(sbuf(nc, [P, 2, kt * P], F32))
        acc = ctx.enter_context(psum(nc, [P, 2, S], F32))
        w_landed, mm_done, added = sem.two("w_landed"), sem.two("mm_done", 1), sem.two("added", 1)
        block = ctx.enter_context(nc.Block())

        @block.sync
        def _(sp):
            def body(p, s):
                sp.wait_ge(mm_done[s], p + 1)
                sp.dma_start(w[:, s, :], weight[2 * p + s]).then_inc(w_landed[s], 16)
            paired(sp, KT, body)

        @block.tensor
        def _(pe):
            def body(p, s):
                pe.wait_ge(added[s], p + 1)
                pe.wait_ge(w_landed[s], 16 * p + 16)
                for k in range(kt):
                    mm = nc.tensor.matmul(acc[:, s, :], w[:, s, k * P:(k + 1) * P], rhs(k),
                                          start=(k == 0), stop=(k == kt - 1))
                mm.then_inc(mm_done[s], 1)
            paired(pe, KT, body)

        @block.vector
        def _(dve):
            def body(p, s):
                dve.wait_ge(mm_done[s], p + 2)
                xt = x[:, 2 * p + s, :]
                g = 1.0 if gate is None else gate[:, bass.ds(2 * p + s, 1)]
                nc.vector.scalar_tensor_tensor(xt, acc[:, s, :], g, xt, ALU.mult, ALU.add).then_inc(added[s], 1)
            paired(dve, KT, body)


def ffn_up(nc, C, weight, h, a):
    with ExitStack() as ctx:
        sem = Sems(nc, ctx)
        w = ctx.enter_context(sbuf(nc, [P, 4, KT * P], F32))
        sig = ctx.enter_context(sbuf(nc, [P, 2, S], F32))
        acc = ctx.enter_context(psum(nc, [P, 4, S], F32))
        w_landed, gated = sem.two("w_landed"), sem.two("gated")
        mm_done, product = sem.two("mm_done", 1), sem.two("product", 1)
        block = ctx.enter_context(nc.Block())

        @block.sync
        def _(sp):
            def body(p, s):
                sp.wait_ge(mm_done[s], 2 * p + 1)
                for j in range(2):
                    sp.dma_start(w[:, 2 * s + j, :], weight[j, 2 * p + s]).then_inc(w_landed[s], 16)
            paired(sp, FT, body)

        @block.tensor
        def _(pe):
            def body(p, s):
                pe.wait_ge(product[s], p + 1)
                pe.wait_ge(w_landed[s], 32 * p + 32)
                for j in range(2):
                    for k in range(KT):
                        mm = nc.tensor.matmul(acc[:, 2 * s + j, :], w[:, 2 * s + j, k * P:(k + 1) * P], h[:, k, :],
                                              start=(k == 0), stop=(k == KT - 1))
                    mm.then_inc(mm_done[s], 1)
            paired(pe, FT, body)

        @block.scalar
        def _(act):
            def body(p, s):
                act.wait_ge(product[s], p + 1)
                act.wait_ge(mm_done[s], 2 * p + 2)
                nc.scalar.activation(sig[:, s, :], acc[:, 2 * s, :], ACT.Silu).then_inc(gated[s], 1)
            paired(act, FT, body)

        @block.vector
        def _(dve):
            def body(p, s):
                dve.wait_ge(gated[s], p + 1)
                dve.wait_ge(mm_done[s], 2 * p + 3)
                nc.vector.tensor_tensor(a[:, 2 * p + s, :], sig[:, s, :], acc[:, 2 * s + 1, :],
                                        ALU.mult).then_inc(product[s], 1)
            paired(dve, FT, body)


def rope(nc, C, src, dst, n, cos, sin, rot, cols=S, col0=0, head_gain=None):
    with ExitStack() as ctx:
        sem = Sems(nc, ctx)
        z, zn, sq, a, b, out = [ctx.enter_context(sbuf(nc, [P, 2, cols], F32)) for _ in range(6)]
        turned = ctx.enter_context(psum(nc, [P, 2, S], F32))
        total = ctx.enter_context(psum(nc, [P, 2, S], F32))
        landed, squared, summed, rooted, turn_done, cos_done = [
            sem.two(x) for x in ("z_landed", "squared", "sq_summed", "rooted", "turned", "cos_done")]
        inverted, normed, sin_done, summed2 = [sem.two(x, 1) for x in ("inverted", "normed", "sin_done", "roped")]
        stored = sem.two("stored", 16)
        block = ctx.enter_context(nc.Block())
        x = zn if head_gain is not None else z
        ready, unit, first = (normed, 1, 2) if head_gain is not None else (landed, 16, 16)
        last = summed2 if cos is not None else normed
        fin = out if cos is not None else zn

        @block.sync
        def _(sp):
            def body(p, s):
                sp.wait_ge(last[s], p + 1)
                sp.dma_start(z[:, s, :], src[bass.ds((2 * p + s) * P, P), :]).then_inc(landed[s], 16)
            paired(sp, n, body)

        @block.tensor
        def _(pe):
            def body(p, s):
                if head_gain is not None:
                    pe.wait_ge(inverted[s], p + 1)
                    pe.wait_ge(squared[s], p + 1)
                    nc.tensor.matmul(total[:, s, :cols], C.ones64[:, :], sq[:, s, :],
                                     start=True, stop=True).then_inc(summed[s], 1)
                if cos is not None:
                    pe.wait_ge(sin_done[s], p + 1)
                    pe.wait_ge(ready[s], unit * p + first)
                    nc.tensor.matmul(turned[:, s, :cols], rot[:, :], x[:, s, :],
                                     start=True, stop=True).then_inc(turn_done[s], 1)
            paired(pe, n, body)

        @block.scalar
        def _(act):
            def body(p, s):
                if head_gain is not None:
                    act.wait_ge(landed[s], 16 * (p + 1))
                    nc.scalar.activation(sq[:, s, :], z[:, s, :], ACT.Square).then_inc(squared[s], 1)
                    act.wait_ge(summed[s], p + 1)
                    nc.scalar.activation(a[:, s, :], total[:, s, :cols], ACT.Sqrt, bias=C.eps[:, 0:1],
                                         scale=1.0 / HD).then_inc(rooted[s], 1)
                act.wait_ge(last[s], p + 2)
                act.dma_start(dst[bass.ds((2 * p + s) * P, P), col0:col0 + cols], fin[:, s, :]).then_inc(stored[s], 16)
            paired(act, n, body)
            for s in range(min(2, n)):
                act.wait_ge(stored[s], 16 * ((n + 1 - s) // 2) + 16)

        @block.vector
        def _(dve):
            def body(p, s):
                if head_gain is not None:
                    dve.wait_ge(rooted[s], p + 1)
                    nc.vector.reciprocal(b[:, s, :], a[:, s, :]).then_inc(inverted[s], 1)
                    dve.wait_ge(inverted[s], p + 2)
                    if cos is None:
                        dve.wait_ge(stored[s], 16 * p + 16)
                    nc.vector.scalar_tensor_tensor(zn[:, s, :], z[:, s, :], head_gain, b[:, s, :], ALU.mult,
                                                   ALU.mult).then_inc(normed[s], 1)
                    dve.wait_ge(normed[s], p + 2)
                else:
                    dve.wait_ge(landed[s], 16 * (p + 1))
                if cos is not None:
                    nc.vector.tensor_tensor(a[:, s, :], x[:, s, :], cos[:, :], ALU.mult).then_inc(cos_done[s], 1)
                    dve.wait_ge(turn_done[s], p + 1)
                    nc.vector.tensor_tensor(b[:, s, :], turned[:, s, :cols], sin[:, :], ALU.mult).then_inc(sin_done[s], 1)
                    dve.wait_ge(cos_done[s], p + 1)
                    dve.wait_ge(sin_done[s], p + 2)
                    dve.wait_ge(stored[s], 16 * p + 16)
                    nc.vector.tensor_tensor(out[:, s, :], a[:, s, :], b[:, s, :], ALU.add).then_inc(summed2[s], 1)
            paired(dve, n, body)


def attention(nc, C, outer, inner, q_src, k_src, v_src, keys, causal, dv, dst, gate=None, acc=None,
              first=False, own_mask=None):
    kt = (keys + P - 1) // P
    kw = [min(P, keys - j * P) for j in range(kt)]
    q0 = [j * P if causal else 0 for j in range(kt)]
    with ExitStack() as ctx:
        sem = Sems(nc, ctx)
        sb = lambda shape: ctx.enter_context(sbuf(nc, shape, F32))
        q = sb([HD + 1, 2, S])
        k = sb([HD + 1, 2, kt * P])
        v = sb([P, 2, kt, P])
        prob = sb([P, 2, kt, S])
        rowmax = sb([P, 2, ST])
        diag = sb([P, 2, ST, P])
        den, inv, part, part2, gates = [sb([P, 2, S]) for _ in range(5)]
        scores = ctx.enter_context(psum(nc, [P, 2, 2 * S], F32))
        shifted = ctx.enter_context(psum(nc, [P, 2, S], F32))
        summed = ctx.enter_context(psum(nc, [P, S], F32))
        aux = ctx.enter_context(psum(nc, [P, S], F32))
        landed = sem.two("qkv_landed")
        diag_made, row_made, row_placed, pv_done, out_made, max_read, exp_read = [sem.two(x, 1) for x in (
            "diag_made", "row_made", "row_placed", "pv_done", "out_made", "max_read", "exp_read")]
        stored, out_free = sem.two("out_stored"), sem.two("out_free", 1)
        scores_made, shifted_made, ones_set = sem.one("scores_made"), sem.one("shifted_made"), sem.one("ones_set")
        den_copied, inverted, gated, read_out = [sem.one(x, c) for x, c in (
            ("den_floored", 0), ("inverted", 0), ("gated", 0), ("read_out", 1))]
        loads = 3 + (gate is not None)
        wide = dv == P
        block = ctx.enter_context(nc.Block())

        def pairs(eng, body):
            with eng.Fori(0, outer) as o:
                with eng.Fori(0, inner) as i:
                    body(o, i, o * inner + i)

        @block.sync
        def _(sp):
            def body(o, i, pair):
                for s in range(2):
                    sp.wait_ge(out_made[s], pair + 1)
                    sp.dma_start(q[0:HD, s, :], q_src(o, i, s)).then_inc(landed[s], 16)
                    sp.dma_start(k[0:HD, s, 0:keys], k_src(o, i, s)).then_inc(landed[s], 16)
                    if keys % P:
                        sp.dma_start(v[0:keys, s, 0, 0:dv], v_src(o, i, s)).then_inc(landed[s], 16)
                    else:
                        sp.dma_start(v[:, s, :, 0:dv], v_src(o, i, s)).then_inc(landed[s], 16)
                    if gate is not None:
                        sp.dma_start(gates[0:HD, s, :], gate(o, i, s)).then_inc(landed[s], 16)
            pairs(sp, body)

        @block.tensor
        def _(pe):
            def raw_scores(pair, s):
                pe.wait_ge(landed[s], 16 * loads * (pair + 1))
                for t in range(ST):
                    n = (t + 1) * P if causal else keys
                    pe.wait_ge(max_read[t % 2], 2 * (2 * pair + s) + t // 2 + 1)
                    for c in range(0, n, S):
                        w = min(S, n - c)
                        mm = nc.tensor.matmul(scores[:, t % 2, c:c + w], q[0:HD, s, t * P:(t + 1) * P],
                                              k[0:HD, s, c:c + w], start=True, stop=True)
                    if causal:
                        mm = nc.tensor.matmul(scores[:, t % 2, n - P:n], C.ident_b[:, :], C.mask_q[:, :],
                                              start=False, stop=True, skip_group_check=True)
                    if own_mask is not None:
                        mm = nc.tensor.matmul(scores[:, t % 2, 0:keys], C.ident_b[:, :], own_mask[0][:, t, 0:keys],
                                              start=False, stop=True, skip_group_check=True)
                    mm.then_inc(scores_made, 1)

            def max_row(pair, s):
                pe.wait_ge(diag_made[s], pair + 2)
                pe.wait_ge(read_out, 2 * pair + s + 1)
                if s == 1:
                    pe.wait_ge(row_placed[0], pair + 2)
                else:
                    pe.wait_ge(row_placed[1], pair + 1)
                nc.tensor.matmul(aux[0:1, :], C.ones[:, 0:1], diag[:, s, :, :],
                                 start=True, stop=True).then_inc(row_made[s], 1)

            def shifted_scores(pair, s):
                pe.wait_ge(row_placed[s], pair + 2)
                if s == 0:
                    pe.wait_ge(ones_set, 1 if wide else 2)
                for j in range(kt):
                    pe.wait_ge(exp_read[j % 2], (2 * pair + s) * ((kt + 1 - j % 2) // 2) + j // 2 + 1)
                    mm = nc.tensor.matmul(shifted[0:kw[j], j % 2, q0[j]:S], k[:, s, j * P:j * P + kw[j]],
                                          q[:, s, q0[j]:S], start=True, stop=True)
                    if causal:
                        mm = nc.tensor.matmul(shifted[:, j % 2, q0[j]:q0[j] + P], C.ident_b[:, :], C.mask_k[:, :],
                                              start=False, stop=True, skip_group_check=True)
                    if own_mask is not None:
                        mm = nc.tensor.matmul(shifted[0:keys, 0, :], C.ident_b[0:keys, 0:keys], own_mask[1][0:keys, :],
                                              start=False, stop=True, skip_group_check=True)
                    mm.then_inc(shifted_made, 1)

            def values(pair, s):
                pe.wait_ge(read_out, 2 * pair + s + 1)
                for j in range(kt):
                    pe.wait_ge(exp_read[j % 2], (2 * pair + s) * ((kt + 1 - j % 2) // 2) + j // 2 + 2)
                    mm = nc.tensor.matmul(summed[:, q0[j]:S], v[0:kw[j], s, j, :], prob[0:kw[j], s, j, q0[j]:S],
                                          start=(j == 0), stop=(j == kt - 1))
                if wide:
                    for j in range(kt):
                        mm = nc.tensor.matmul(aux[:, :], C.ones[:, :], prob[:, s, j, :],
                                              start=(j == 0), stop=(j == kt - 1))
                mm.then_inc(pv_done[s], 1)

            def body(o, i, pair):
                raw_scores(pair, 0)
                raw_scores(pair, 1)
                max_row(pair, 0)
                shifted_scores(pair, 0)
                values(pair, 0)
                max_row(pair, 1)
                shifted_scores(pair, 1)
                values(pair, 1)
            pairs(pe, body)

        @block.vector
        def _(dve):
            nc.vector.memset(k[HD:HD + 1, :, :], 1.0).then_inc(ones_set, 1)
            if not wide:
                nc.vector.memset(v[:, :, :, HD:P], 1.0).then_inc(ones_set, 1)

            def maxima(pair, s):
                head = 2 * pair + s
                for t in range(ST):
                    dve.wait_ge(scores_made, 4 * head + t + 1)
                    if t == 0:
                        dve.wait_ge(diag_made[s], pair + 1)
                    n = (t + 1) * P if causal else keys
                    nc.vector.tensor_reduce(rowmax[:, s, t:t + 1], scores[:, t % 2, 0:n], AX_X,
                                            ALU.max).then_inc(max_read[t % 2], 1)
                dve.wait_ge(max_read[0], 2 * head + 3)
                dve.wait_ge(max_read[1], 2 * head + 3)
                dve.wait_ge(row_made[s], pair + 1)
                nc.vector.scalar_tensor_tensor(
                    diag[:, s, :, :], rowmax[:, s, :].unsqueeze(2).to_broadcast([P, ST, P]), MAX_FLOOR,
                    C.neg_ident[:, :].unsqueeze(1).to_broadcast([P, ST, P]), ALU.max,
                    ALU.mult).then_inc(diag_made[s], 1)

            def finish(pair, s):
                head = 2 * pair + s
                dve.wait_ge(pv_done[s], pair + 2)
                dve.wait_ge(out_made[s], pair + 1)
                if wide:
                    nc.vector.reciprocal(inv[:, s, :], aux[:, :]).then_inc(inverted, 1)
                else:
                    nc.vector.tensor_scalar(den[0:HD, s, :], summed[HD:P, :], 1e-30, None,
                                            ALU.max).then_inc(den_copied, 1)
                    dve.wait_ge(den_copied, head + 1)
                    nc.vector.reciprocal(inv[0:HD, s, :], den[0:HD, s, :]).then_inc(inverted, 1)
                dve.wait_ge(inverted, head + 1)
                if gate is None:
                    dve.wait_ge(out_free[s], pair + 1)
                    nc.vector.tensor_tensor(part[0:dv, s, :], summed[0:dv, :], inv[0:dv, s, :],
                                            ALU.mult).then_inc(read_out, 1)
                    dve.wait_ge(read_out, head + 2)
                    nc.vector.tensor_copy(part2[0:dv, s, :], part[0:dv, s, :]).then_inc(out_made[s], 1)
                else:
                    nc.vector.tensor_tensor(part[0:dv, s, :], summed[0:dv, :], inv[0:dv, s, :],
                                            ALU.mult).then_inc(read_out, 1)
                    dve.wait_ge(read_out, head + 2)
                    place = acc[:, bass.ds(head, 1), :]
                    if first:
                        nc.vector.tensor_tensor(place, part[0:HD, s:s + 1, :], gates[0:HD, s:s + 1, :],
                                                ALU.mult).then_inc(out_made[s], 1)
                    else:
                        nc.vector.tensor_tensor(part2[0:HD, s, :], part[0:HD, s, :], gates[0:HD, s, :],
                                                ALU.mult).then_inc(gated, 1)
                        dve.wait_ge(gated, head + 1)
                        nc.vector.tensor_tensor(place, part2[0:HD, s:s + 1, :], place, ALU.add).then_inc(out_made[s], 1)

            def body(o, i, pair):
                maxima(pair, 0)
                maxima(pair, 1)
                finish(pair, 0)
                finish(pair, 1)
            pairs(dve, body)

        @block.scalar
        def _(act):
            def place_row(pair, s):
                act.wait_ge(row_made[s], pair + 2)
                nc.scalar.activation(q[HD:HD + 1, s, :], aux[0:1, :], ACT.Copy).then_inc(row_placed[s], 1)

            def exponentials(pair, s):
                act.wait_ge(pv_done[s], pair + 1)
                for j in range(kt):
                    act.wait_ge(shifted_made, kt * (2 * pair + s) + j + 1)
                    nc.scalar.activation(prob[0:kw[j], s, j, q0[j]:S], shifted[0:kw[j], j % 2, q0[j]:S],
                                         ACT.Exp, scale=HD ** -0.5).then_inc(exp_read[j % 2], 1)

            def body(o, i, pair):
                for s in range(2):
                    place_row(pair, s)
                    exponentials(pair, s)
            pairs(act, body)

        @block.gpsimd
        def _(pool):
            if gate is None:
                def body(o, i, pair):
                    for s in range(2):
                        pool.wait_ge(out_made[s], pair + 2)
                        pool.dma_start(dst(o, i, s), part2[0:dv, s, :]).then_inc(stored[s], 16)
                    for s in range(2):
                        pool.wait_ge(stored[s], 16 * pair + 16)
                        pool.sem_inc(out_free[s], 1)
                pairs(pool, body)


def cast_masks(nc, src_q, src_k, cmp_q, cmp_k):
    with ExitStack() as ctx:
        sem = Sems(nc, ctx)
        q, k = ctx.enter_context(sbuf(nc, [P, ST, 32], F32)), ctx.enter_context(sbuf(nc, [32, S], F32))
        landed, cast = sem.one("landed"), sem.one("cast")
        block = ctx.enter_context(nc.Block())

        @block.sync
        def _(sp):
            sp.dma_start(q[:, :, :], src_q).then_inc(landed, 16)
            sp.dma_start(k[:, :], src_k).then_inc(landed, 16)

        @block.vector
        def _(dve):
            dve.wait_ge(landed, 32)
            nc.vector.tensor_copy(cmp_q[:, :, :], q[:, :, :]).then_inc(cast, 1)
            nc.vector.tensor_copy(cmp_k[:, :], k[:, :]).then_inc(cast, 1)


def gates_and_rank(nc, C, weight, h, gates_d, rank_d):
    with ExitStack() as ctx:
        sem = Sems(nc, ctx)
        w = ctx.enter_context(sbuf(nc, [P, KT, 40], F32))
        g, r = [ctx.enter_context(sbuf(nc, [40, S], F32)) for _ in range(2)]
        acc = ctx.enter_context(psum(nc, [P, S], F32))
        landed, mm_done, made, stored = [sem.one(x) for x in ("w_landed", "mm_done", "made", "stored")]
        block = ctx.enter_context(nc.Block())

        @block.sync
        def _(sp):
            sp.dma_start(w[:, :, :], weight).then_inc(landed, 16)
            sp.wait_ge(made, 2)
            sp.dma_start(gates_d, g[0:24, :]).then_inc(stored, 16)
            sp.dma_start(rank_d, r[24:40, :]).then_inc(stored, 16)
            sp.wait_ge(stored, 32)

        @block.tensor
        def _(pe):
            pe.wait_ge(landed, 16)
            for k in range(KT):
                mm = nc.tensor.matmul(acc[0:40, :], w[:, k, :], h[:, k, :], start=(k == 0), stop=(k == KT - 1))
            mm.then_inc(mm_done, 1)

        @block.scalar
        def _(act):
            act.wait_ge(mm_done, 1)
            nc.scalar.activation(g[:, :], acc[0:40, :], ACT.Sigmoid).then_inc(made, 1)
            nc.scalar.activation(r[:, :], acc[0:40, :], ACT.Copy).then_inc(made, 1)


def compress(nc, C, zT, w1, w2, pos, kc_d, vc_d):
    nb = NC_BLK
    with ExitStack() as ctx:
        sem = Sems(nc, ctx)
        sb = lambda shape: ctx.enter_context(sbuf(nc, shape, F32))
        raw, w1s, w2s, poss = sb([P, 4, S]), sb([P, 2, 16, 256]), sb([P, 2, 2, HD]), sb([P, 2, 16])
        bias, hid = sb([P, 4]), sb([P, 4, 2 * nb])
        kc, kcos, ksin, kout, vc = sb([HD, 2 * nb]), sb([HD, 2 * nb]), sb([HD, 2 * nb]), sb([HD, 2 * nb]), sb([nb, 2, HD])
        acc = ctx.enter_context(psum(nc, [P, 4, S], F32))
        accb = ctx.enter_context(psum(nc, [P, S], F32))
        acck = ctx.enter_context(psum(nc, [P, 2, S], F32))
        landed, hid_mm, bias_made, hid_made, kc_mm, kc_copied, turned, vc_mm, dve_done, roped, vc_made, stored = [
            sem.one(x) for x in ("landed", "hid_mm", "bias_made", "hid_made", "kc_mm", "kc_copied", "turned",
                                 "vc_mm", "parts_made", "roped", "vc_made", "stored")]
        block = ctx.enter_context(nc.Block())

        @block.sync
        def _(sp):
            n = 0
            for j in range(2):
                base = (Z_KC, Z_VC)[j]
                for g in range(2):
                    rows = zT[base + g * HD:base + (g + 1) * HD, :]
                    sp.dma_start(raw[0:HD, 2 * j + g, :], rows).then_inc(landed, 16)
                    sp.dma_start(raw[HD:P, 2 * j + g, 0:S - 1], rows[:, 1:S]).then_inc(landed, 16)
                sp.dma_start(w1s[:, j, :, :], w1[j]).then_inc(landed, 16)
                sp.dma_start(w2s[:, j, :, :], w2[j]).then_inc(landed, 16)
                sp.dma_start(poss[:, j, :], pos[j]).then_inc(landed, 16)
            sp.wait_ge(roped, 1)
            for g in range(2):
                sp.dma_start(kc_d[g], kout[:, g * nb:(g + 1) * nb]).then_inc(stored, 16)
            sp.wait_ge(vc_made, 1)
            for g in range(2):
                sp.dma_start(vc_d[g], vc[:, g, :]).then_inc(stored, 16)
            sp.wait_ge(stored, 64)

        @block.tensor
        def _(pe):
            pe.wait_ge(landed, 16 * 14)
            for j in range(2):
                for m in range(2):
                    for c in range(16):
                        mm = nc.tensor.matmul(accb[:, 2 * j + m:2 * j + m + 1], w1s[:, j, c, m * P:(m + 1) * P],
                                              poss[:, j, c:c + 1], start=(c == 0), stop=(c == 15))
                    for c in range(16):
                        mm = nc.tensor.matmul(acc[:, 2 * j + m, 0:2 * nb], w1s[:, j, c, m * P:(m + 1) * P],
                                              raw[:, 2 * j:2 * j + 2, 2 * c:2 * c + 16 * (nb - 1) + 1:16],
                                              start=(c == 0), stop=(c == 15))
                    mm.then_inc(hid_mm, 1)
            pe.wait_ge(hid_made, 4)
            for m in range(2):
                mm = nc.tensor.matmul(acck[0:HD, 0, 0:2 * nb], w2s[:, 0, m, :], hid[:, m, :], start=(m == 0), stop=(m == 1))
            mm.then_inc(kc_mm, 1)
            for g in range(2):
                for m in range(2):
                    mm = nc.tensor.matmul(acck[0:nb, 1, g * HD:(g + 1) * HD], hid[:, 2 + m, g * nb:(g + 1) * nb],
                                          w2s[:, 1, m, :], start=(m == 0), stop=(m == 1))
            mm.then_inc(vc_mm, 1)
            pe.wait_ge(kc_copied, 1)
            nc.tensor.matmul(acck[0:HD, 0, 128:128 + 2 * nb], C.rot[0:HD, 0:HD], kc[:, :], start=True,
                             stop=True).then_inc(turned, 1)

        @block.scalar
        def _(act):
            act.wait_ge(hid_mm, 4)
            nc.scalar.activation(bias[:, :], accb[:, 0:4], ACT.Copy).then_inc(bias_made, 1)
            act.wait_ge(bias_made, 1)
            for i in range(4):
                nc.scalar.activation(hid[:, i, :], acc[:, i, 0:2 * nb], ACT.Gelu_apprx_tanh,
                                     bias=bias[:, i:i + 1]).then_inc(hid_made, 1)
            act.wait_ge(kc_mm, 1)
            nc.scalar.activation(kc[:, :], acck[0:HD, 0, 0:2 * nb], ACT.Copy).then_inc(kc_copied, 1)
            act.wait_ge(vc_mm, 1)
            nc.scalar.activation(vc[:, :, :], acck[0:nb, 1, 0:2 * HD].rearrange("p (g d) -> p g d", g=2),
                                 ACT.Copy).then_inc(vc_made, 1)

        @block.vector
        def _(dve):
            dve.wait_ge(kc_copied, 1)
            nc.vector.tensor_tensor(kcos[:, :], kc[:, :], C.kc_cos[:, :], ALU.mult).then_inc(dve_done, 1)
            dve.wait_ge(turned, 1)
            nc.vector.tensor_tensor(ksin[:, :], acck[0:HD, 0, 128:128 + 2 * nb], C.kc_sin[:, :],
                                    ALU.mult).then_inc(dve_done, 1)
            dve.wait_ge(dve_done, 2)
            nc.vector.tensor_tensor(kout[:, :], kcos[:, :], ksin[:, :], ALU.add).then_inc(roped, 1)


def spatial_gate(nc, C, zT, ztok, w_d, b_d, lng_d, lnb_d, mix):
    G = 4
    with ExitStack() as ctx:
        sem = Sems(nc, ctx)
        sb = lambda shape: ctx.enter_context(sbuf(nc, shape, F32))
        u, v, w, wm, b = sb([HD, G, S]), sb([P, ST, 256]), sb([P, G, P]), sb([P, G, P]), sb([1, G * P])
        lng, lnb, sq, out = sb([P, 256]), sb([P, 256]), sb([P, ST, 256]), sb([HD, G, S])
        vg, ug = sb([P, ST, 256]), sb([HD, G, S])
        mean, var, root, inv = sb([P, ST]), sb([P, ST]), sb([P, ST]), sb([P, ST])
        acc = ctx.enter_context(psum(nc, [HD, G, S], F32))
        landed, act_done, dve_done, mm_done, made, stored = [
            sem.one(x) for x in ("landed", "act_done", "dve_done", "mm_done", "out_made", "stored")]
        block = ctx.enter_context(nc.Block())
        over = lambda t: t[:, :].unsqueeze(2).to_broadcast([P, ST, 256])
        along = lambda t: t[:, :].unsqueeze(1).to_broadcast([P, ST, 256])

        @block.sync
        def _(sp):
            for dst, src in ((v[:, :, :], ztok[:, T_V:T_V + 256].rearrange("(t p) c -> p t c", p=P)),
                             (u[:, :, :], zT[Z_U:Z_U + 256, :].rearrange("(g p) s -> p g s", p=HD)),
                             (w[:, :, :], w_d), (b[:, :], b_d), (lng[:, :], lng_d.to_broadcast([P, 256])),
                             (lnb[:, :], lnb_d.to_broadcast([P, 256]))):
                sp.dma_start(dst, src).then_inc(landed, 16)
            sp.wait_ge(made, 1)
            sp.dma_start(mix[768:1024, :].rearrange("(g p) s -> p g s", p=HD), out[:, :, :]).then_inc(stored, 16)
            sp.wait_ge(stored, 16)

        @block.scalar
        def _(act):
            act.wait_ge(landed, 96)
            nc.scalar.activation(vg[:, :, :], v[:, :, :], ACT.Gelu_apprx_tanh).then_inc(act_done, 1)
            nc.scalar.activation(ug[:, :, :], u[:, :, :], ACT.Gelu_apprx_tanh).then_inc(act_done, 1)
            act.wait_ge(dve_done, 3)
            nc.scalar.activation(sq[:, :, :], v[:, :, :], ACT.Square).then_inc(act_done, 1)
            act.wait_ge(dve_done, 4)
            nc.scalar.activation(root[:, :], var[:, :], ACT.Sqrt, bias=C.eps[:, 0:1], scale=1 / 256).then_inc(act_done, 1)

        @block.vector
        def _(dve):
            dve.wait_ge(act_done, 1)
            nc.vector.tensor_reduce(mean[:, :], vg[:, :, :], AX_X, ALU.add).then_inc(dve_done, 1)
            dve.wait_ge(dve_done, 1)
            nc.vector.tensor_scalar(mean[:, :], mean[:, :], 1 / 256, None, ALU.mult).then_inc(dve_done, 1)
            dve.wait_ge(dve_done, 2)
            nc.vector.tensor_tensor(v[:, :, :], vg[:, :, :], over(mean), ALU.subtract).then_inc(dve_done, 1)
            dve.wait_ge(act_done, 3)
            nc.vector.tensor_reduce(var[:, :], sq[:, :, :], AX_X, ALU.add).then_inc(dve_done, 1)
            dve.wait_ge(act_done, 4)
            nc.vector.reciprocal(inv[:, :], root[:, :]).then_inc(dve_done, 1)
            dve.wait_ge(dve_done, 5)
            nc.vector.tensor_tensor(vg[:, :, :], v[:, :, :], over(inv), ALU.mult).then_inc(dve_done, 1)
            dve.wait_ge(dve_done, 6)
            nc.vector.tensor_tensor(v[:, :, :], vg[:, :, :], along(lng), ALU.mult).then_inc(dve_done, 1)
            dve.wait_ge(dve_done, 7)
            nc.vector.tensor_tensor(vg[:, :, :], v[:, :, :], along(lnb), ALU.add).then_inc(dve_done, 1)
            nc.vector.tensor_tensor(wm[:, :, :], w[:, :, :], C.causal[:, :].unsqueeze(1).to_broadcast([P, G, P]),
                                    ALU.mult).then_inc(dve_done, 1)
            dve.wait_ge(mm_done, 1)
            dve.wait_ge(act_done, 2)
            nc.vector.tensor_tensor(out[:, :, :], acc[:, :, :], ug[:, :, :], ALU.mult).then_inc(made, 1)

        @block.tensor
        def _(pe):
            pe.wait_ge(dve_done, 9)
            for g in range(G):
                for t in range(ST):
                    place = acc[:, g, t * P:(t + 1) * P]
                    nc.tensor.matmul(place, vg[:, t, g * HD:(g + 1) * HD], wm[:, g, :], start=True, stop=False)
                    mm = nc.tensor.matmul(place, C.ones[0:1, 0:HD], b[0:1, g * P:(g + 1) * P], start=False, stop=True)
            mm.then_inc(mm_done, 1)


def gla(nc, C, zT, ztok, rank_d, wup_d, bup_d, norm_d, mix):
    H, DK = 4, 32
    with ExitStack() as ctx:
        sem = Sems(nc, ctx)
        sb = lambda shape: ctx.enter_context(sbuf(nc, shape, F32))
        q, k, b, diff, decay, tmp, tmp2 = [sb([P, S]) for _ in range(7)]
        qd, kd = sb([P, 2, S]), sb([P, 2, S])
        rank, wup, bup, norm = sb([16, S]), sb([16, P]), sb([P, 1]), sb([HD, 1])
        v, r = sb([P, ST, 256]), sb([HD, H, S])
        att = sb([P, H, ST, S])
        masked = sb([P, S])
        o, osq, oroot, oinv, rs = sb([HD, H, S]), sb([HD, H, S]), sb([HD, H, S]), sb([HD, H, S]), sb([HD, H, S])
        acc = ctx.enter_context(psum(nc, [P, H, S], F32))
        acc2 = ctx.enter_context(psum(nc, [P, H, S], F32))
        landed, dve_done, act_done, z_mm, level_mm, level_read, o_mm, rms_mm, made, stored = [sem.one(x) for x in (
            "landed", "dve_done", "act_done", "z_mm", "level_mm", "level_read", "o_mm", "rms_mm", "out_made", "stored")]
        factors, decayed, diffed = sem.one("factors_made"), sem.one("decayed"), sem.one("diffed")
        block = ctx.enter_context(nc.Block())
        levels = [1] + GLA_LEVELS

        @block.sync
        def _(sp):
            for dst, src in ((q[:, :], zT[Z_GQ:Z_GQ + P, :]), (k[:, :], zT[Z_GK:Z_GK + P, :]),
                             (rank[:, :], rank_d), (wup[:, :], wup_d), (bup[:, :], bup_d), (norm[:, :], norm_d),
                             (v[:, :, :], ztok[:, T_GV:T_GV + 256].rearrange("(t p) c -> p t c", p=P)),
                             (r[:, :, :], zT[Z_GR:Z_GR + 256, :].rearrange("(h p) s -> p h s", p=HD))):
                sp.dma_start(dst, src).then_inc(landed, 16)
            sp.wait_ge(made, 1)
            sp.dma_start(mix[512:768, :].rearrange("(h p) s -> p h s", p=HD), o[:, :, :]).then_inc(stored, 16)
            sp.wait_ge(stored, 16)

        @block.tensor
        def _(pe):
            pe.wait_ge(landed, 128)
            nc.tensor.matmul(acc[:, 0, :], wup[:, :], rank[:, :], start=True, stop=True).then_inc(z_mm, 1)
            for n, s in enumerate(levels):
                pe.wait_ge(factors, 2 * n + 2)
                bank = (acc, acc2)[n % 2]
                if n >= 2:
                    pe.wait_ge(level_read, n - 1)
                if n == 0:
                    pe.wait_ge(dve_done, 1)
                if s <= P:
                    pairs = [(t, t, t) for t in range(ST)]
                elif s == 256:
                    pairs = [(0, 0, 1), (1, 2, 3)]
                else:
                    pairs = [(0, 0, 2), (1, 0, 3), (2, 1, 2), (3, 1, 3)]
                for place, jt, it in pairs:
                    for h in range(H):
                        rows = slice(h * DK, (h + 1) * DK)
                        mm = nc.tensor.matmul(bank[:, h, place * P:(place + 1) * P],
                                              kd[rows, n % 2, jt * P:(jt + 1) * P],
                                              qd[rows, n % 2, it * P:(it + 1) * P], start=True, stop=True)
                mm.then_inc(level_mm, 1)
            pe.wait_ge(level_read, len(levels))
            for h in range(H):
                for j in range(ST):
                    mm = nc.tensor.matmul(acc[0:HD, h, j * P:S], v[:, j, h * HD:(h + 1) * HD], att[:, h, j, j * P:S],
                                          start=(j == 0), stop=(j == ST - 1))
            mm.then_inc(o_mm, 1)
            pe.wait_ge(act_done, 5)
            for h in range(H):
                mm = nc.tensor.matmul(acc2[0:HD, h, :], C.ones[0:HD, 0:HD], osq[:, h, :], start=True, stop=True)
            mm.then_inc(rms_mm, 1)

        @block.scalar
        def _(act):
            act.wait_ge(dve_done, 3)
            nc.scalar.activation(tmp[:, :], diff[:, :], ACT.Exp).then_inc(act_done, 1)
            act.wait_ge(act_done, 1)
            nc.scalar.activation(decay[:, :], tmp[:, :], ACT.Ln, bias=1.0).then_inc(act_done, 1)
            for n in range(1, len(levels)):
                act.wait_ge(diffed, 2 * n)
                act.wait_ge(factors, 2 * n)
                nc.scalar.activation(decay[:, :], diff[:, :], ACT.Exp, scale=1 / 16).then_inc(decayed, 1)
            nc.scalar.activation(rs[:, :, :], r[:, :, :], ACT.Silu).then_inc(act_done, 1)
            act.wait_ge(o_mm, 1)
            nc.scalar.activation(o[:, :, :], acc[0:HD, :, :], ACT.Copy).then_inc(act_done, 1)
            nc.scalar.activation(osq[:, :, :], acc[0:HD, :, :], ACT.Square).then_inc(act_done, 1)
            act.wait_ge(rms_mm, 1)
            nc.scalar.activation(oroot[:, :, :], acc2[0:HD, :, :], ACT.Sqrt, bias=C.eps[0:HD, 0:1],
                                 scale=1 / HD).then_inc(act_done, 1)

        @block.vector
        def _(dve):
            dve.wait_ge(z_mm, 1)
            nc.vector.tensor_scalar(b[:, :], acc[:, 0, :], bup[:, 0:1], None, ALU.add).then_inc(dve_done, 1)
            dve.wait_ge(dve_done, 1)
            nc.vector.tensor_scalar(tmp[:, :], b[:, :], -1.0, None, ALU.mult).then_inc(dve_done, 1)
            dve.wait_ge(dve_done, 2)
            nc.vector.tensor_tensor(diff[:, :], b[:, :], tmp[:, :], ALU.min).then_inc(dve_done, 1)
            dve.wait_ge(act_done, 2)
            nc.vector.scalar_tensor_tensor(tmp2[:, :], b[:, :], 0.0, decay[:, :], ALU.min,
                                           ALU.subtract).then_inc(dve_done, 1)
            nc.vector.memset(tmp[:, :], 1.0).then_inc(dve_done, 1)
            nc.vector.memset(att[:, :, :, :], 0.0).then_inc(dve_done, 1)
            dve.wait_ge(dve_done, 6)
            nc.vector.tensor_tensor_scan(b[:, :], tmp[:, :], tmp2[:, :], 0.0, ALU.mult, ALU.add).then_inc(dve_done, 1)
            dve.wait_ge(landed, 128)
            nc.vector.tensor_scalar(q[:, :], q[:, :], DK ** -0.5, None, ALU.mult).then_inc(dve_done, 1)
            dve.wait_ge(dve_done, 8)

            def make_factors(n, s):
                if n >= 2:
                    dve.wait_ge(level_mm, n - 1)
                if s == 1:
                    nc.vector.tensor_copy(qd[:, 0, :], q[:, :]).then_inc(factors, 1)
                    nc.vector.tensor_copy(kd[:, 0, :], k[:, :]).then_inc(factors, 1)
                    return
                if n >= 2:
                    dve.wait_ge(decayed, n - 1)
                half = s // 2
                bv = b[:, :].rearrange("p (n s) -> p n s", s=s)
                dv = diff[:, :].rearrange("p (n s) -> p n s", s=s)
                ref = bv[:, :, half - 1:half].to_broadcast([P, S // s, half])
                nc.vector.tensor_tensor(dv[:, :, half:s], bv[:, :, half:s], ref, ALU.subtract).then_inc(diffed, 1)
                nc.vector.tensor_tensor(dv[:, :, 0:half], ref, bv[:, :, 0:half], ALU.subtract).then_inc(diffed, 1)
                dve.wait_ge(decayed, n)
                nc.vector.tensor_tensor(qd[:, n % 2, :], q[:, :], decay[:, :], ALU.mult).then_inc(factors, 1)
                nc.vector.tensor_tensor(kd[:, n % 2, :], k[:, :], decay[:, :], ALU.mult).then_inc(factors, 1)

            steps = [8]

            def take_level(n, s):
                dve.wait_ge(level_mm, n + 1)
                bank = (acc, acc2)[n % 2]
                if s <= P:
                    for h in range(H):
                        nc.vector.tensor_tensor(masked[:, :].rearrange("p (t i) -> p t i", t=ST),
                                                bank[:, h, :].rearrange("p (t i) -> p t i", t=ST),
                                                C.level_mask[:, n, :].unsqueeze(1).to_broadcast([P, ST, P]),
                                                ALU.mult).then_inc(dve_done, 1)
                        steps[0] += 1
                        dve.wait_ge(dve_done, steps[0])
                        for t in range(ST):
                            place = att[:, h, t, t * P:(t + 1) * P]
                            op = nc.vector.tensor_tensor(place, place, masked[:, t * P:(t + 1) * P], ALU.add)
                            if h == H - 1 and t == ST - 1:
                                op.then_inc(level_read, 1)
                                dve.wait_ge(level_read, n + 1)
                            else:
                                op.then_inc(dve_done, 1)
                                steps[0] += 1
                        dve.wait_ge(dve_done, steps[0])
                elif s == 256:
                    nc.vector.tensor_copy(att[:, :, 0, P:2 * P], bank[:, :, 0:P]).then_inc(dve_done, 1)
                    nc.vector.tensor_copy(att[:, :, 2, 3 * P:S], bank[:, :, P:2 * P]).then_inc(level_read, 1)
                    steps[0] += 1
                else:
                    nc.vector.tensor_copy(att[:, :, 0, 2 * P:S], bank[:, :, 0:2 * P]).then_inc(dve_done, 1)
                    nc.vector.tensor_copy(att[:, :, 1, 2 * P:S], bank[:, :, 2 * P:S]).then_inc(level_read, 1)
                    steps[0] += 1

            make_factors(0, levels[0])
            for n in range(1, len(levels)):
                make_factors(n, levels[n])
                take_level(n - 1, levels[n - 1])
            take_level(len(levels) - 1, levels[-1])
            dve.wait_ge(act_done, 6)
            nc.vector.reciprocal(oinv[:, :, :], oroot[:, :, :]).then_inc(dve_done, 1)
            dve.wait_ge(dve_done, steps[0] + 1)
            nc.vector.scalar_tensor_tensor(osq[:, :, :], o[:, :, :], norm[:, 0:1], oinv[:, :, :], ALU.mult,
                                           ALU.mult).then_inc(dve_done, 1)
            dve.wait_ge(dve_done, steps[0] + 2)
            nc.vector.tensor_tensor(o[:, :, :], osq[:, :, :], rs[:, :, :], ALU.mult).then_inc(made, 1)


def modulation(nc, C, cvec, weight, bias, mod):
    n = 6 * KT
    with ExitStack() as ctx:
        sem = Sems(nc, ctx)
        w = ctx.enter_context(sbuf(nc, [P, 2, 2 * KT * P], F32))
        c, sc = [ctx.enter_context(sbuf(nc, [P, KT, 2], F32)) for _ in range(2)]
        b = ctx.enter_context(sbuf(nc, [P, n], F32))
        acc = ctx.enter_context(psum(nc, [P, 2, S], F32))
        c_landed, c_made = sem.one("c_landed"), sem.one("silu_made")
        w_landed, mm_done, evacuated = sem.two("w_landed"), sem.two("mm_done", 1), sem.two("evacuated", 1)
        block = ctx.enter_context(nc.Block())

        @block.sync
        def _(sp):
            sp.dma_start(c[:, :, :], cvec).then_inc(c_landed, 16)
            sp.dma_start(b[:, :], bias).then_inc(c_landed, 16)

            def body(p, s):
                sp.wait_ge(mm_done[s], p + 1)
                sp.dma_start(w[:, s, :].rearrange("p (t c) -> p t c", t=2),
                             weight[bass.ds((2 * p + s) * 2, 2)].rearrange("t p c -> p t c")).then_inc(w_landed[s], 16)
            paired(sp, n // 2, body)

        @block.scalar
        def _(act):
            act.wait_ge(c_landed, 32)
            nc.scalar.activation(sc[:, :, :], c[:, :, :], ACT.Silu).then_inc(c_made, 1)

        @block.tensor
        def _(pe):
            pe.wait_ge(c_made, 1)

            def body(p, s):
                pe.wait_ge(evacuated[s], p + 1)
                pe.wait_ge(w_landed[s], 16 * p + 16)
                for t in range(2):
                    for k in range(KT):
                        at = (t * KT + k) * P
                        mm = nc.tensor.matmul(acc[:, s, 2 * t:2 * t + 2], w[:, s, at:at + P], sc[:, k, :],
                                              start=(k == 0), stop=(k == KT - 1))
                mm.then_inc(mm_done[s], 1)
            paired(pe, n // 2, body)

        @block.vector
        def _(dve):
            dve.wait_ge(c_landed, 32)

            def body(p, s):
                dve.wait_ge(mm_done[s], p + 2)
                at = bass.ds((2 * p + s) * 2, 2)
                nc.vector.tensor_tensor(mod[:, at, :], acc[:, s, 0:4].rearrange("p (t v) -> p t v", t=2),
                                        b[:, at].unsqueeze(2).to_broadcast([P, 2, 2]), ALU.add).then_inc(evacuated[s], 1)
            paired(dve, n // 2, body)


def block2_scalars(nc, C, mod, n1, n2, lqk, g1x, g1c, g2x, lam):
    with ExitStack() as ctx:
        sem = Sems(nc, ctx)
        sb = lambda shape: ctx.enter_context(sbuf(nc, shape, F32))
        n1s, n2s, l, prod, tot, e = sb([P, KT]), sb([P, KT]), sb([P, 4, HD]), sb([P, 2, HD]), sb([P, 2]), sb([P, 2])
        landed, done, exped = sem.one("landed"), sem.one("dve_done"), sem.one("exp_done")
        block = ctx.enter_context(nc.Block())

        @block.sync
        def _(sp):
            sp.dma_start(n1s[:, :], n1).then_inc(landed, 16)
            sp.dma_start(n2s[:, :], n2).then_inc(landed, 16)
            for i in range(4):
                sp.dma_start(l[:, i, :], lqk[i].to_broadcast([P, HD])).then_inc(landed, 16)

        @block.vector
        def _(dve):
            dve.wait_ge(landed, 96)
            for g, n, at, v in ((g1x, n1s, KT, 0), (g1c, n1s, KT, 1), (g2x, n2s, 4 * KT, 0)):
                nc.vector.scalar_tensor_tensor(g[:, :], mod[:, at:at + KT, v], 1.0, n[:, :], ALU.add,
                                               ALU.mult).then_inc(done, 1)
            nc.vector.tensor_tensor(prod[:, :, :], l[:, 0:2, :], l[:, 2:4, :], ALU.mult).then_inc(done, 1)
            dve.wait_ge(done, 4)
            nc.vector.tensor_reduce(tot[:, :], prod[:, :, :], AX_X, ALU.add).then_inc(done, 1)
            dve.wait_ge(exped, 1)
            nc.vector.tensor_tensor(lam[:, :], e[:, 1:2], e[:, 0:1], ALU.subtract).then_inc(done, 1)
            dve.wait_ge(done, 6)
            nc.vector.tensor_scalar(lam[:, :], lam[:, :], 0.2, None, ALU.subtract).then_inc(done, 1)

        @block.scalar
        def _(act):
            act.wait_ge(done, 5)
            nc.scalar.activation(e[:, :], tot[:, :], ACT.Exp).then_inc(exped, 1)


def diff_combine(nc, C, od, lam, subln, mix):
    n = 4
    with ExitStack() as ctx:
        sem = Sems(nc, ctx)
        sb = lambda shape: ctx.enter_context(sbuf(nc, shape, F32))
        o, d, sq, root, inv, out, g = sb([P, 2 * n, S]), sb([P, n, S]), sb([P, n, S]), sb([P, n, S]), sb([P, n, S]), sb([P, n, S]), sb([P, 1])
        acc = ctx.enter_context(psum(nc, [P, n, S], F32))
        landed, differ, squared, summed, rooted, inverted, made, g_made, stored = [sem.one(x) for x in (
            "landed", "differ", "squared", "summed", "rooted", "inverted", "made", "gain_made", "stored")]
        block = ctx.enter_context(nc.Block())

        @block.sync
        def _(sp):
            sp.dma_start(g[:, :], subln).then_inc(landed, 16)
            sp.dma_start(o[:, :, :], od.rearrange("(n p) s -> p n s", p=P)).then_inc(landed, 16)
            sp.wait_ge(made, n)
            sp.dma_start(mix.rearrange("(n p) s -> p n s", p=P), out[:, :, :]).then_inc(stored, 16)
            sp.wait_ge(stored, 16)

        @block.vector
        def _(dve):
            dve.wait_ge(landed, 32)
            nc.vector.tensor_scalar(g[:, :], g[:, :], 0.8, None, ALU.mult).then_inc(g_made, 1)
            for h in range(n):
                nc.vector.scalar_tensor_tensor(d[:, h, :], o[:, 2 * h + 1, :], lam[:, 0:1], o[:, 2 * h, :], ALU.mult,
                                               ALU.add).then_inc(differ, 1)
            dve.wait_ge(g_made, 1)
            dve.wait_ge(differ, n)
            for h in range(n):
                dve.wait_ge(rooted, h + 1)
                nc.vector.reciprocal(inv[:, h, :], root[:, h, :]).then_inc(inverted, 1)
                dve.wait_ge(inverted, h + 1)
                nc.vector.scalar_tensor_tensor(out[:, h, :], d[:, h, :], g[:, 0:1], inv[:, h, :], ALU.mult,
                                               ALU.mult).then_inc(made, 1)

        @block.scalar
        def _(act):
            for h in range(n):
                act.wait_ge(differ, h + 1)
                nc.scalar.activation(sq[:, h, :], d[:, h, :], ACT.Square).then_inc(squared, 1)
            for h in range(n):
                act.wait_ge(summed, h + 1)
                nc.scalar.activation(root[:, h, :], acc[:, h, :], ACT.Sqrt, bias=C.eps[:, 0:1],
                                     scale=1 / P).then_inc(rooted, 1)

        @block.tensor
        def _(pe):
            for h in range(n):
                pe.wait_ge(squared, h + 1)
                nc.tensor.matmul(acc[:, h, :], C.ones[:, :], sq[:, h, :], start=True, stop=True).then_inc(summed, 1)


def turn(nc, C, count, src, take):
    with ExitStack() as ctx:
        sem = Sems(nc, ctx)
        ps = ctx.enter_context(psum(nc, [P, 4, S], F32))
        turned, taken = sem.one("turned"), sem.one("taken")
        block = ctx.enter_context(nc.Block())

        @block.tensor
        def _(pe):
            for i in range(count):
                if i >= 4:
                    pe.wait_ge(taken, i - 3)
                nc.tensor.transpose(ps[:, i % 4, 0:P], src(i), C.ident[:, :]).then_inc(turned, 1)

        @block.vector
        def _(dve):
            for i in range(count):
                dve.wait_ge(turned, i + 1)
                take(dve, i, ps[:, i % 4, 0:P]).then_inc(taken, 1)


def peer_pick(nc, C, qT, keys, stream, weights):
    T = TOPK
    with ExitStack() as ctx:
        sem = Sems(nc, ctx)
        sb = lambda shape, dt=F32: ctx.enter_context(sbuf(nc, shape, dt))
        q, kk = sb([P, 2, S]), sb([P, 2, NKEY])
        sc, sc2 = sb([P, 2, ST, NKEY]), sb([P, 2, ST, NKEY])
        val, idx, idf = sb([P, 2, ST, T]), sb([P, 2, ST, T], U32), sb([P, 2, ST, T])
        cand, cand2 = sb([P, ST, T * T]), sb([P, ST, T * T])
        best, pos, half, halff = sb([P, ST, T]), sb([P, ST, T], U32), sb([P, 2, ST, T], U32), sb([P, 2, ST, T])
        hot = sb([P, ST * T, T])
        hot2 = sb([P, ST * T, T])
        found, exps, tot, inv, shifted = sb([P, 2, ST * T]), sb([P, ST, T]), sb([P, ST]), sb([P, ST]), sb([P, ST, T])
        ps = ctx.enter_context(psum(nc, [P, 2, S], F32))
        landed, exp_done, dve_done, passed = [sem.one(x) for x in ("landed", "exp_done", "dve_done", "waits_passed")]
        mm_done, copied, topped = [sem.one(x, 1) for x in ("mm_done", "copied", "topped")]
        block = ctx.enter_context(nc.Block())
        SHIFT_AT = 2 * ST * 5 + 1 + ST * 5 + 1
        STEPS = SHIFT_AT + 2 + 1 + 6 + 2 + 3

        @block.sync
        def _(sp):
            with sp.Fori(0, PH) as h:
                sp.wait_ge(mm_done, h + 1)
                for p in range(2):
                    sp.dma_start(q[:, p, :], qT[bass.ds((2 * h + p) * P, P), :]).then_inc(landed, 16)
                    sp.dma_start(kk[:, p, :], keys[2 * h + p]).then_inc(landed, 16)

        @block.tensor
        def _(pe):
            with pe.Fori(0, PH) as h:
                pe.wait_ge(landed, 64 * h + 64)
                pe.wait_ge(copied, 2 * h + 1)
                for p in range(2):
                    for t in range(ST):
                        mm = nc.tensor.matmul(ps[:, p, t * P:(t + 1) * P], q[:, p, t * P:(t + 1) * P], kk[:, p, :],
                                              start=True, stop=True)
                mm.then_inc(mm_done, 1)

        @block.scalar
        def _(act):
            with act.Fori(0, PH) as h:
                act.wait_ge(mm_done, h + 2)
                act.wait_ge(topped, h + 1)
                for p in range(2):
                    nc.scalar.activation(sc[:, p, :, :], ps[:, p, :].rearrange("p (t n) -> p t n", t=ST),
                                         ACT.Copy).then_inc(copied, 1)
                act.wait_ge(dve_done, STEPS * h + SHIFT_AT)
                nc.scalar.activation(exps[:, :, :], shifted[:, :, :], ACT.Exp).then_inc(exp_done, 1)

        @block.vector
        def _(dve):
            nc.vector.memset(stream[:, 2 * ST * PICKS:], 0)
            with dve.Fori(0, PH) as h:
                step = [0]

                def did(op):
                    step[0] += 1
                    op.then_inc(dve_done, 1)

                def after():
                    wait_apart(dve, dve_done, STEPS * h + step[0], passed)

                def top16(x, x2, v, i):
                    did(nc.vector.max(v[:, 0:8], x))
                    after()
                    did(nc.vector.max_index(i[:, 0:8], v[:, 0:8], x))
                    did(nc.vector.match_replace(x2, v[:, 0:8], x, -3e38))
                    after()
                    did(nc.vector.max(v[:, 8:16], x2))
                    after()
                    did(nc.vector.max_index(i[:, 8:16], v[:, 8:16], x2))

                wait_apart(dve, copied, 2 * h + 3, passed)
                for p in range(2):
                    for t in range(ST):
                        top16(sc[:, p, t, :], sc2[:, p, t, :], val[:, p, t, :], idx[:, p, t, :])
                after()
                did(nc.vector.tensor_copy(idf[:, :, :, :], idx[:, :, :, :]))
                after()
                nc.vector.tensor_tensor(cand[:, :, :].rearrange("p t (a b) -> p t a b", a=T),
                                        val[:, 0, :, :].unsqueeze(3).to_broadcast([P, ST, T, T]),
                                        val[:, 1, :, :].unsqueeze(2).to_broadcast([P, ST, T, T]),
                                        ALU.add).then_inc(topped, 1)
                wait_apart(dve, topped, h + 2, passed)
                for t in range(ST):
                    top16(cand[:, t, :], cand2[:, t, :], best[:, t, :], pos[:, t, :])
                after()
                did(nc.vector.tensor_tensor(shifted[:, :, :], best[:, :, :], best[:, :, 0:1].to_broadcast([P, ST, T]),
                                            ALU.subtract))
                did(nc.vector.tensor_scalar(half[:, 0, :, :], pos[:, :, :], 4, None, ALU.logical_shift_right))
                did(nc.vector.tensor_scalar(half[:, 1, :, :], pos[:, :, :], T - 1, None, ALU.bitwise_and))
                after()
                did(nc.vector.tensor_copy(halff[:, :, :, :], half[:, :, :, :]))
                for p in range(2):
                    after()
                    did(nc.vector.tensor_tensor(hot[:, :, :],
                                                halff[:, p, :, :].rearrange("p t k -> p (t k)").unsqueeze(2)
                                                .to_broadcast([P, ST * T, T]),
                                                C.iota[:, :].unsqueeze(1).to_broadcast([P, ST * T, T]), ALU.is_equal))
                    after()
                    did(nc.vector.tensor_tensor(hot2[:, :, :].rearrange("p (t k) a -> p t k a", t=ST),
                                                hot[:, :, :].rearrange("p (t k) a -> p t k a", t=ST),
                                                idf[:, p, :, :].unsqueeze(2).to_broadcast([P, ST, T, T]), ALU.mult))
                    after()
                    did(nc.vector.tensor_reduce(found[:, p, :], hot2[:, :, :], AX_X, ALU.add))
                after()
                cols = bass.ds(h * T, T)
                for f in range(2):
                    did(nc.vector.scalar_tensor_tensor(
                        stream[:, 0:2 * ST * PICKS].rearrange("p (t f k) -> p t f k", f=2, k=PICKS)[:, :, f, cols],
                        found[:, 0, :].rearrange("p (t k) -> p t k", t=ST), float(NKEY),
                        found[:, 1, :].rearrange("p (t k) -> p t k", t=ST), ALU.mult, ALU.add))
                dve.wait_ge(exp_done, h + 1)
                did(nc.vector.tensor_reduce(tot[:, :], exps[:, :, :], AX_X, ALU.add))
                after()
                did(nc.vector.reciprocal(inv[:, :], tot[:, :]))
                after()
                did(nc.vector.tensor_tensor(weights[:, :, cols], exps[:, :, :],
                                            inv[:, :].unsqueeze(2).to_broadcast([P, ST, T]), ALU.mult))
                after()
                assert step[0] == STEPS, (step[0], STEPS)


RING = 8
GROUPS = PICKS // RING


def peer_experts(nc, C, h_tok, stream, weights, u, v, y):
    with ExitStack() as ctx:
        sem = Sems(nc, ctx)
        sb = lambda shape, dt=F32: ctx.enter_context(sbuf(nc, shape, dt))
        rows = sb([P, RING, D])
        h_cur, acc = sb([P, D]), sb([P, D])
        pick = sb([P, 2, RING], U32)
        dots, wcur = sb([P, 2, RING]), sb([P, 2, RING])
        a, ga, wa = sb([P, PICKS]), sb([P, PICKS]), sb([P, PICKS])
        gathered = [sem.one(f"gathered{r}") for r in range(RING)]
        used = [sem.one(f"used{r}", 1) for r in range(RING)]
        picked, tile_set, dots_kept, gelu_done, w_made, w_set = [sem.one(x) for x in (
            "picked", "tile_set", "dots_kept", "gelu_done", "w_made", "w_set")]
        y_kept = sem.one("y_kept", 1)
        passed, passed_pool = sem.one("vector_waits_passed"), sem.one("pool_waits_passed")
        block = ctx.enter_context(nc.Block())

        def steps(eng, t, f, body):
            with eng.Fori(0, GROUPS // 2) as g:
                for b in range(2):
                    body((t * 2 + f) * GROUPS + 2 * g + b, 2 * g + b, b)

        @block.gpsimd
        def _(pool):
            with pool.Fori(0, ST) as t:
                for f, table in ((0, u), (1, v)):
                    def body(n, g, b):
                        for r in range(RING):
                            if r == 0:
                                pool.wait_ge(picked, n + 1)
                            wait_apart(pool, used[r], n + 1, passed_pool)
                            pool.indirect_dma_start(
                                rows[:, r, :], None, table,
                                bass.IndirectOffsetOnAxis(ap=pick[:, b, r:r + 1], axis=0)).then_inc(gathered[r], 16)
                    steps(pool, t, f, body)

        @block.scalar
        def _(act):
            with act.Fori(0, ST) as t:
                act.wait_ge(dots_kept, GROUPS * (t + 1))
                nc.scalar.activation(ga[:, :], a[:, :], ACT.Gelu).then_inc(gelu_done, 1)

        @block.vector
        def _(dve):
            def pick_rows(n, b):
                nc.vector.tensor_copy(pick[:, b, :], stream[:, bass.ds(n * RING, RING)]).then_inc(picked, 1)

            pick_rows(0, 0)
            pick_rows(1, 1)
            with dve.Fori(0, ST) as t:
                nc.vector.tensor_copy(h_cur[:, :], h_tok[:, t, :]).then_inc(tile_set, 1)
                dve.wait_ge(y_kept, t + 1)
                nc.vector.memset(acc[:, :], 0.0).then_inc(tile_set, 1)
                wait_apart(dve, tile_set, 2 * t + 2, passed)

                def dot(n, g, b):
                    for r in range(RING):
                        dve.wait_ge(gathered[r], 16 * n + 16)
                        nc.vector.tensor_tensor_reduce(out=rows[:, r, :], in0=rows[:, r, :], in1=h_cur[:, :], scale=1.0,
                                                       scalar=0.0, op0=ALU.mult, op1=ALU.add,
                                                       accum_out=dots[:, b, r:r + 1]).then_inc(used[r], 1)
                    pick_rows(n + 2, b)
                    for r in range(RING):
                        dve.wait_ge(used[r], n + 2)
                    nc.vector.tensor_copy(a[:, bass.ds(g * RING, RING)], dots[:, b, :]).then_inc(dots_kept, 1)

                steps(dve, t, 0, dot)
                dve.wait_ge(gelu_done, t + 1)
                nc.vector.tensor_tensor(wa[:, :], ga[:, :], weights[:, t, :], ALU.mult).then_inc(w_made, 1)
                wait_apart(dve, w_made, t + 1, passed)

                def add(n, g, b):
                    nc.vector.tensor_copy(wcur[:, b, :], wa[:, bass.ds(g * RING, RING)]).then_inc(w_set, 1)
                    dve.wait_ge(w_set, GROUPS * t + g + 1)
                    for r in range(RING):
                        dve.wait_ge(gathered[r], 16 * n + 16)
                        if r:
                            dve.wait_ge(used[r - 1], n + 2)
                        else:
                            dve.wait_ge(used[RING - 1], n + 1)
                        nc.vector.scalar_tensor_tensor(acc[:, :], rows[:, r, :], wcur[:, b, r:r + 1], acc[:, :],
                                                       ALU.mult, ALU.add).then_inc(used[r], 1)
                    pick_rows(n + 2, b)

                steps(dve, t, 1, add)
                dve.wait_ge(used[RING - 1], 2 * GROUPS * (t + 1) + 1)
                nc.vector.tensor_copy(y[:, t, :], acc[:, :]).then_inc(y_kept, 1)


INPUTS = dict(
    xT=(D, S), gains1=(DEPTH, P, KT), gains2=(DEPTH, P, KT), gain_end=(P, KT),
    w_fm=(DEPTH, Z_ROWS // P, P, D), w_tm=(DEPTH, D, T_COLS), w_small=(DEPTH, P, KT, 40),
    cw1=(DEPTH, 2, P, 16, 256), cw2=(DEPTH, 2, P, 2, HD), cpos=(DEPTH, 2, P, 16),
    gla_up=(DEPTH, 16, P), gla_b=(DEPTH, P, 1), gla_g=(DEPTH, HD, 1),
    sg_w=(DEPTH, P, 4, P), sg_b=(DEPTH, 1, 4 * P), sg_lng=(DEPTH, 1, 256), sg_lnb=(DEPTH, 1, 256),
    w_out=(DEPTH, KT, P, D), w_ffn=(DEPTH, 2, FT, P, D), w_down=(DEPTH, KT, P, FT * P),
    cvec=(P, KT, 2), ctxT=(D, CTX), w_mod=(6 * KT, P, D), b_mod=(P, 6 * KT), n1=(P, KT), n2=(P, KT), n3=(P, KT),
    w2_fm=(Y_ROWS // P, P, D), w2_tm=(D, Y2_COLS), w2_out=(KT, P, D), lqk=(4, 1, HD), subln=(P, 1),
    gq_g=(P, 1), gk_g=(P, 1), wq=(2 * PH, P, D), keys=(2 * PH, P, NKEY),
    peer_u=(NKEY * NKEY, D), peer_v=(NKEY * NKEY, D),
    c_ident=(P, P), c_ones64=(P, P), c_rot=(P, P), c_rot2=(P, P), c_cos=(P, S), c_sin=(P, S), c_cos2=(P, S),
    c_sin2=(P, S), c_kcos=(HD, 2 * NC_BLK), c_ksin=(HD, 2 * NC_BLK), c_causal=(P, P), c_levels=(P, 8, P),
    c_iota=(P, TOPK), c_mask_q=(P, P), c_mask_k=(P, P), c_cmp_q=(P, ST, 32), c_cmp_k=(32, S),
)


def build(nc, A, out, stop=None):
    with ExitStack() as ctx:
        sb = lambda shape, dt=F32: ctx.enter_context(sbuf(nc, shape, dt))
        dram = lambda name, shape: nc.dram_tensor(name, shape, F32).ap()

        class C:
            pass
        C.ones, C.ident, C.neg_ident, C.ones64 = sb([P, P]), sb([P, P]), sb([P, P]), sb([P, P])
        C.ident_b, C.mask_q, C.mask_k = sb([P, P], BF16), sb([P, P], BF16), sb([P, P], BF16)
        C.eps = sb([P, 1])
        with ExitStack() as c2:
            sem = Sems(nc, c2)
            landed, made = sem.one("consts_landed"), sem.one("consts_made")
            mask_q, mask_k = [c2.enter_context(sbuf(nc, [P, P], F32)) for _ in range(2)]
            block = c2.enter_context(nc.Block())

            @block.sync
            def _(sp):
                for dst, name in ((C.ident, "c_ident"), (C.ones64, "c_ones64"), (mask_q, "c_mask_q"),
                                  (mask_k, "c_mask_k")):
                    sp.dma_start(dst[:, :], A[name]).then_inc(landed, 16)

            @block.vector
            def _(dve):
                nc.vector.memset(C.ones[:, :], 1.0).then_inc(made, 1)
                nc.vector.memset(C.eps[:, :], EPS).then_inc(made, 1)
                dve.wait_ge(landed, 64)
                nc.vector.tensor_copy(C.ident_b[:, :], C.ident[:, :]).then_inc(made, 1)
                nc.vector.tensor_copy(C.mask_q[:, :], mask_q[:, :]).then_inc(made, 1)
                nc.vector.tensor_copy(C.mask_k[:, :], mask_k[:, :]).then_inc(made, 1)
                nc.vector.tensor_scalar(C.neg_ident[:, :], C.ident[:, :], -1.0, None, ALU.mult).then_inc(made, 1)

        xT, hT = sb([P, KT, S]), sb([P, KT, S])
        block1(nc, A, C, xT, hT, stop)
        if stop in (None, "b2"):
            block2(nc, A, C, xT, hT)
        store_x(nc, xT, hT, out, stop)


def store_x(nc, xT, hT, out, stop):
    moves = [(out[k * P:(k + 1) * P, :], (xT if stop == "b1" else hT)[:, k, :]) for k in range(KT)]
    load_all(nc, moves)


def block1(nc, A, C, xT, hT, stop):
    dram = lambda name, shape: nc.dram_tensor(name, shape, F32).ap()
    zT, ztok, mix = dram("zT", (Z_ROWS, S)), dram("ztok", (S, T_COLS)), dram("mix", (D, S))
    roped = dram("roped", (768, S))
    gates_d, rank_d = dram("gates", (24, S)), dram("rank", (16, S))
    kc_d, vc_d = dram("kc", (2, HD, NC_BLK)), dram("vc", (2, NC_BLK, HD))
    load_all(nc, [(xT[:, k, :], A["xT"][k * P:(k + 1) * P, :]) for k in range(KT)])
    with nc.Fori(0, DEPTH) as l:
        with ExitStack() as ctx:
            gain = ctx.enter_context(sbuf(nc, [P, KT], F32))
            load_all(nc, [(gain[:, :], A["gains1"][l])])
            rmsnorm(nc, C, xT, gain, hT)
        project(nc, C, A["w_fm"][l], Z_ROWS // P, lambda k: hT[:, k, :], S, zT)
        project_tokens(nc, C, A["w_tm"][l], T_COLS, ST, lambda k, t: hT[:, k, t * P:(t + 1) * P], ztok)
        gates_and_rank(nc, C, A["w_small"][l], hT, gates_d, rank_d)
        with ExitStack() as ctx:
            sb = lambda shape, dt=F32: ctx.enter_context(sbuf(nc, shape, dt))
            cos, sin, C.rot, C.kc_cos, C.kc_sin = sb([P, S]), sb([P, S]), sb([P, P]), sb([HD, 2 * NC_BLK]), sb([HD, 2 * NC_BLK])
            load_all(nc, [(cos[:, :], A["c_cos"]), (sin[:, :], A["c_sin"]), (C.rot[:, :], A["c_rot"]),
                          (C.kc_cos[:, :], A["c_kcos"]), (C.kc_sin[:, :], A["c_ksin"])])
            rope(nc, C, zT[Z_Q:Z_Q + 512, :], roped[0:512, :], 4, cos, sin, C.rot)
            rope(nc, C, zT[Z_KS:Z_KW + P, :], roped[512:768, :], 2, cos, sin, C.rot)
            compress(nc, C, zT, A["cw1"][l], A["cw2"][l], A["cpos"][l], kc_d, vc_d)
        with ExitStack() as ctx:
            sb = lambda shape, dt=F32: ctx.enter_context(sbuf(nc, shape, dt))
            heads, cmp_q, cmp_k = sb([HD, 8, S]), sb([P, ST, 32], BF16), sb([32, S], BF16)
            cast_masks(nc, A["c_cmp_q"], A["c_cmp_k"], cmp_q, cmp_k)
            q_src = lambda g, i, s: roped[bass.ds((g * 4 + i * 2 + s) * HD, HD), :]
            gate = lambda j: (lambda g, i, s: gates_d[bass.ds((g * 4 + i * 2 + s) * 3 + j, 1), :].to_broadcast([HD, S]))
            tokens = lambda c: (lambda g, i, s: ztok[:, bass.ds(g * HD + c, HD)].rearrange("(t p) d -> p t d", p=P))
            attention(nc, C, 2, 2, q_src, lambda g, i, s: kc_d[g], lambda g, i, s: vc_d[g], NC_BLK, False, HD, None,
                      gate=gate(0), acc=heads, first=True, own_mask=(cmp_q, cmp_k))
            for j, krow, vcol in ((1, 512, T_VS), (2, 640, T_VW)):
                attention(nc, C, 2, 2, q_src, lambda g, i, s, krow=krow: roped[bass.ds(g * HD + krow, HD), :],
                          tokens(vcol), S, True, HD, None, gate=gate(j), acc=heads)
            load_all(nc, [(mix[0:512, :].rearrange("(h p) s -> p h s", p=HD), heads[:, :, :])])
        with ExitStack() as ctx:
            C.level_mask = ctx.enter_context(sbuf(nc, [P, 8, P], F32))
            load_all(nc, [(C.level_mask[:, :, :], A["c_levels"])])
            gla(nc, C, zT, ztok, rank_d, A["gla_up"][l], A["gla_b"][l], A["gla_g"][l], mix)
        with ExitStack() as ctx:
            C.causal = ctx.enter_context(sbuf(nc, [P, P], F32))
            load_all(nc, [(C.causal[:, :], A["c_causal"])])
            spatial_gate(nc, C, zT, ztok, A["sg_w"][l], A["sg_b"][l], A["sg_lng"][l], A["sg_lnb"][l], mix)
        load_all(nc, [(hT[:, k, :], mix[k * P:(k + 1) * P, :]) for k in range(KT)])
        project_add(nc, C, A["w_out"][l], KT, lambda k: hT[:, k, :], xT)
        with ExitStack() as ctx:
            gain = ctx.enter_context(sbuf(nc, [P, KT], F32))
            load_all(nc, [(gain[:, :], A["gains2"][l])])
            rmsnorm(nc, C, xT, gain, hT)
        with ExitStack() as ctx:
            a = ctx.enter_context(sbuf(nc, [P, FT, S], F32))
            ffn_up(nc, C, A["w_ffn"][l], hT, a)
            project_add(nc, C, A["w_down"][l], FT, lambda k: a[:, k, :], xT)
    with ExitStack() as ctx:
        gain = ctx.enter_context(sbuf(nc, [P, KT], F32))
        load_all(nc, [(gain[:, :], A["gain_end"])])
        rmsnorm(nc, C, xT, gain, hT)
    load_all(nc, [(xT[:, :, :], hT[:, :, :])])


def block2(nc, A, C, xT, hT):
    dram = lambda name, shape: nc.dram_tensor(name, shape, F32).ap()
    N2 = CTX + S
    y, yc = dram("y", (Y_ROWS, S)), dram("yc", (YC_ROWS, CTX))
    ytok = dram("ytok", (N2, Y2_COLS))
    qr, kr = dram("qr", (1024, S)), dram("kr", (YC_ROWS, N2))
    od, mix2, qp = dram("od", (1024, S)), dram("mix2", (1024, S)), dram("qp", (2048, S))
    with ExitStack() as ctx:
        sb = lambda shape, dt=F32: ctx.enter_context(sbuf(nc, shape, dt))
        mod = sb([P, 6 * KT, 2])
        g1x, g1c, g2x, lam = sb([P, KT]), sb([P, KT]), sb([P, KT]), sb([P, 1])
        modulation(nc, C, A["cvec"], A["w_mod"], A["b_mod"], mod)
        block2_scalars(nc, C, mod, A["n1"], A["n2"], A["lqk"], g1x, g1c, g2x, lam)
        part = lambda j, v: mod[:, j * KT:(j + 1) * KT, v]
        rmsnorm(nc, C, xT, g1x, hT, shift=part(0, 0))
        project(nc, C, A["w2_fm"], Y_ROWS // P, lambda k: hT[:, k, :], S, y)
        project_tokens(nc, C, A["w2_tm"], Y2_COLS, ST, lambda k, t: hT[:, k, t * P:(t + 1) * P], ytok[CTX:N2, :])
        with ExitStack() as c2:
            ctxT = c2.enter_context(sbuf(nc, [P, KT, CTX], F32))
            load_all(nc, [(ctxT[:, k, :], A["ctxT"][k * P:(k + 1) * P, :]) for k in range(KT)])
            rmsnorm(nc, C, ctxT, g1c, hT, n=CTX, shift=part(0, 1))
        project(nc, C, A["w2_fm"][8:13], YC_ROWS // P, lambda k: hT[:, k, 0:CTX], CTX, yc)
        project_tokens(nc, C, A["w2_tm"], Y2_COLS, CTX // P, lambda k, t: hT[:, k, t * P:(t + 1) * P], ytok[0:CTX, :])
        with ExitStack() as c2:
            sb2 = lambda shape, dt=F32: c2.enter_context(sbuf(nc, shape, dt))
            cos, sin, rot, gqg, gkg = sb2([P, S]), sb2([P, S]), sb2([P, P]), sb2([P, 1]), sb2([P, 1])
            load_all(nc, [(cos[:, :], A["c_cos2"]), (sin[:, :], A["c_sin2"]), (rot[:, :], A["c_rot2"]),
                          (gqg[:, :], A["gq_g"]), (gkg[:, :], A["gk_g"])])
            rope(nc, C, y[0:512, :], qr[0:512, :], 4, cos, sin, rot)
            rope(nc, C, y[512:1024, :], qr[512:1024, :], 4, cos, sin, rot, head_gain=gqg[:, 0:1])
            rope(nc, C, y[1024:1536, :], kr[0:512, :], 4, cos, sin, rot, col0=CTX)
            rope(nc, C, y[1536:1664, :], kr[512:640, :], 1, cos, sin, rot, col0=CTX, head_gain=gkg[:, 0:1])
            rope(nc, C, yc[512:640, :], kr[512:640, :], 1, None, None, None, cols=CTX, head_gain=gkg[:, 0:1])
        load_all(nc, [(kr[0:512, 0:CTX], yc[0:512, :])])
        attention(nc, C, 4, 1, lambda o, i, s: qr[bass.ds(o * P + s * HD, HD), :],
                  lambda o, i, s: kr[bass.ds(o * P + s * HD, HD), :],
                  lambda o, i, s: ytok[:, bass.ds(o * P, P)].rearrange("(t p) d -> p t d", p=P), N2, False, P,
                  lambda o, i, s: od[bass.ds((o * 2 + s) * P, P), :])
        attention(nc, C, 2, 2, lambda g, i, s: qr[bass.ds((g * 4 + i * 2 + s) * HD + 512, HD), :],
                  lambda g, i, s: kr[bass.ds(g * HD + 512, HD), :],
                  lambda g, i, s: ytok[:, bass.ds(g * HD + 512, HD)].rearrange("(t p) d -> p t d", p=P), N2, False, HD,
                  lambda g, i, s: mix2[bass.ds((g * 4 + i * 2 + s) * HD + 512, HD), :])
        diff_combine(nc, C, od, lam, A["subln"], mix2[0:512, :])
        load_all(nc, [(hT[:, k, :], mix2[k * P:(k + 1) * P, :]) for k in range(KT)])
        project_add(nc, C, A["w2_out"], KT, lambda k: hT[:, k, :], xT, gate=part(2, 0))
        rmsnorm(nc, C, xT, g2x, hT, shift=part(3, 0))
        project(nc, C, A["wq"], 2 * PH, lambda k: hT[:, k, :], S, qp)
        with ExitStack() as c2:
            sb2 = lambda shape, dt=F32: c2.enter_context(sbuf(nc, shape, dt))
            stream = sb2([P, 2 * ST * PICKS + 2 * RING], U32)
            weights = sb2([P, ST, PICKS])
            with ExitStack() as c3:
                C.iota = c3.enter_context(sbuf(nc, [P, TOPK], F32))
                load_all(nc, [(C.iota[:, :], A["c_iota"])])
                peer_pick(nc, C, qp, A["keys"], stream, weights)
            h_tok, yt = sb2([P, ST, D]), sb2([P, ST, D])
            at = lambda i: (i // KT, slice(i % KT * P, (i % KT + 1) * P), i % KT, slice(i // KT * P, (i // KT + 1) * P))

            def to_tokens(dve, i, tile):
                t, cols, k, toks = at(i)
                return nc.vector.tensor_copy(h_tok[:, t, cols], tile)
            turn(nc, C, ST * KT, lambda i: hT[:, at(i)[2], at(i)[3]], to_tokens)
            peer_experts(nc, C, h_tok, stream, weights, A["peer_u"], A["peer_v"], yt)

            def add_back(dve, i, tile):
                t, cols, k, toks = at(i)
                return nc.vector.scalar_tensor_tensor(xT[:, k, toks], tile, mod[:, 5 * KT + k, 0:1], xT[:, k, toks],
                                                      ALU.mult, ALU.add)
            turn(nc, C, ST * KT, lambda i: yt[:, at(i)[0], at(i)[1]], add_back)
        with ExitStack() as c2:
            gain = c2.enter_context(sbuf(nc, [P, KT], F32))
            load_all(nc, [(gain[:, :], A["n3"])])
            rmsnorm(nc, C, xT, gain, hT)


def constants():
    f = np.float32
    i = np.arange(P)
    c = {}
    c["c_ident"] = np.eye(P, dtype=f)
    c["c_ones64"] = (i[:, None] // HD == i[None, :] // HD).astype(f)

    def turned(half):
        r = np.zeros((P, P), f)
        for m in range(P):
            if m % (2 * half) < half:
                r[m + half, m] = -1
            else:
                r[m - half, m] = 1
        return r
    c["c_rot"], c["c_rot2"] = turned(32), turned(16)

    def table(pos, half):
        inv = (1.0 / (f(10000.0) ** (np.arange(half, dtype=f) / f(half)))).astype(f)
        ang = (pos.astype(f)[None, :] * inv[:, None]).astype(f)
        return np.concatenate([np.cos(ang)] * 2).astype(f), np.concatenate([np.sin(ang)] * 2).astype(f)
    pos = np.arange(S)
    cos, sin = table(pos, 32)
    c["c_cos"], c["c_sin"] = np.tile(cos, (2, 1)), np.tile(sin, (2, 1))
    cos, sin = table(np.arange(NC_BLK) * 16 + 31, 32)
    c["c_kcos"], c["c_ksin"] = np.tile(cos, (1, 2)), np.tile(sin, (1, 2))
    rc, rs = table(pos // 64, 16)
    cc, cs = table(pos % 64, 16)
    c["c_cos2"], c["c_sin2"] = np.concatenate([rc, cc, rc, cc]), np.concatenate([rs, cs, rs, cs])
    c["c_causal"] = (i[None, :] >= i[:, None]).astype(f)
    lv = np.zeros((P, 8, P), f)
    lv[:, 0] = np.eye(P)
    for n, s in enumerate(GLA_LEVELS[:7]):
        same = i[:, None] // s == i[None, :] // s
        lv[:, n + 1] = same & (i[:, None] % s < s // 2) & (i[None, :] % s >= s // 2)
    c["c_levels"] = lv
    c["c_iota"] = np.tile(np.arange(TOPK, dtype=f), (P, 1))
    c["c_mask_q"] = np.where(i[None, :] > i[:, None], MASK, 0).astype(f)
    c["c_mask_k"] = np.where(i[:, None] > i[None, :], MASK, 0).astype(f)
    end = np.arange(32) * 16 + 31
    t = np.arange(S)
    ck = np.where(end[:, None] > t[None, :], MASK, 0)
    c["c_cmp_k"] = ck.astype(f)
    c["c_cmp_q"] = np.ascontiguousarray(ck.T.reshape(ST, P, 32).transpose(1, 0, 2)).astype(f)
    return c


def tiles(w):
    K, N = w.shape
    return np.ascontiguousarray(w.reshape(K // P, P, N // P, P).transpose(2, 1, 0, 3).reshape(N // P, P, K))


def columns(v):
    return np.ascontiguousarray(v.reshape(-1, P).T)


def laid_out(I):
    L = range(DEPTH)
    a = {}
    a["xT"] = I["x"][0].T
    a["gains1"] = np.stack([columns(I["attn_norm"][l]) for l in L])
    a["gains2"] = np.stack([columns(I["ffn_norm"][l]) for l in L])
    a["gain_end"] = columns(I["final_norm"])
    w = I["w_in"]
    cat = lambda *parts: np.concatenate([w[:, :, s:s + n] for s, n in parts], axis=2)
    fm = cat((0, 512), (512, 128), (640, 128), (768, 128), (1024, 128), (1304, 128), (1432, 128), (1832, 256), (2088, 256))
    a["w_fm"] = np.stack([tiles(fm[l]) for l in L])
    a["w_tm"] = cat((896, 128), (1152, 128), (1560, 256), (2344, 256))
    small = cat((1280, 24), (1816, 16))
    a["w_small"] = small.reshape(DEPTH, KT, P, 40).transpose(0, 2, 1, 3)
    a["cw1"] = np.stack([I["cmp_w1_k"], I["cmp_w1_v"]], 1).reshape(DEPTH, 2, 16, P, 256).transpose(0, 1, 3, 2, 4)
    a["cw2"] = np.stack([I["cmp_w2_k"], I["cmp_w2_v"]], 1).reshape(DEPTH, 2, 2, P, HD).transpose(0, 1, 3, 2, 4)
    a["cpos"] = np.stack([I["cmp_pos_k"], I["cmp_pos_v"]], 1).reshape(DEPTH, 2, 16, P).transpose(0, 1, 3, 2)
    a["gla_up"] = I["gla_w_up"]
    a["gla_b"] = I["gla_b_up"][:, :, None]
    a["gla_g"] = I["gla_norm"][:, :, None]
    a["sg_w"] = I["sg_w"].transpose(0, 3, 1, 2)
    a["sg_b"] = I["sg_b"].reshape(DEPTH, 1, 4 * P)
    a["sg_lng"], a["sg_lnb"] = I["sg_ln_g"][:, None, :], I["sg_ln_b"][:, None, :]
    a["w_out"] = np.stack([tiles(I["w_out"][l]) for l in L])
    a["w_ffn"] = np.stack([np.stack([tiles(I["w_gate"][l]), tiles(I["w_up"][l])]) for l in L])
    a["w_down"] = np.stack([tiles(I["w_down"][l]) for l in L])
    a["cvec"] = np.stack([columns(I["c_2"][0]), columns(I["c_ctx_2"])], 2)
    a["ctxT"] = I["ctx_2"][0].T
    a["w_mod"] = tiles(I["w_mod_2"][0])
    a["b_mod"] = columns(I["b_mod_2"][0])
    a["n1"], a["n2"], a["n3"] = columns(I["norm1_g_2"][0]), columns(I["norm2_g_2"][0]), columns(I["final_norm_g_2"])
    w = I["w_in_2"]
    a["w2_fm"] = tiles(cat((0, 512), (1536, 512), (512, 512), (2048, 128))[0])
    a["w2_tm"] = cat((1024, 512), (2176, 128))[0]
    a["w2_out"] = tiles(I["w_out_2"][0])
    a["lqk"] = np.stack([I["diff_lq1_2"], I["diff_lq2_2"], I["diff_lk1_2"], I["diff_lk2_2"]])
    a["subln"] = I["diff_subln_g_2"][0][:, None]
    a["gq_g"], a["gk_g"] = [np.tile(I[n][0], 2)[:, None] for n in ("gqa_q_norm_g_2", "gqa_k_norm_g_2")]
    a["wq"] = tiles(I["peer_wq_2"][0])
    a["keys"] = I["peer_subkeys_2"][0].reshape(2 * PH, NKEY, P).transpose(0, 2, 1)
    a["peer_u"], a["peer_v"] = I["peer_u_2"][0], I["peer_v_2"][0]
    a.update(constants())
    return {n: np.ascontiguousarray(a[n]) for n in INPUTS}


def kernel(**inputs):
    import concourse.bacc as bacc
    from concourse.bass_utils import run_bass_kernel_spmd
    nc = bacc.Bacc("TRN2", target_bir_lowering=False, num_devices=1)
    arrays = laid_out({n: np.asarray(v) for n, v in inputs.items()})
    args = {}
    for n, shape in INPUTS.items():
        assert arrays[n].shape == tuple(shape), (n, arrays[n].shape, shape)
        args[n] = nc.dram_tensor(n, shape, F32, kind="ExternalInput").ap()
    out = nc.dram_tensor("out_x", (D, S), F32, kind="ExternalOutput").ap()
    build(nc, args, out)
    got = run_bass_kernel_spmd(nc, [arrays], core_ids=[0]).results[0]["out_x"]
    return np.ascontiguousarray(got.T)[None]
```

```python
import itertools
from contextlib import ExitStack

import numpy as np
import concourse.bass as bass
from concourse import mybir

F32 = mybir.dt.float32
F32R = mybir.dt.float32r
BF16 = mybir.dt.bfloat16
U32 = mybir.dt.uint32
ALU = mybir.AluOpType
ACT = mybir.ActivationFunctionType
AX_X = mybir.AxisListType.X

P = 128
D = 1024
KT = D // P
S = 512
ST = S // P
CTX = 256
HD = 64
DEPTH = 2
FF = 2816
FT = FF // P
NC_BLK = (S - 32) // 16 + 1
EPS = 1e-6
MASK = -1e30
MAX_FLOOR = -1e29
Z_Q, Z_KC, Z_VC, Z_KS, Z_KW, Z_GQ, Z_GK, Z_GR, Z_U = 0, 512, 640, 768, 896, 1024, 1152, 1280, 1536
Z_ROWS = 1792
T_VS, T_VW, T_GV, T_V = 0, 128, 256, 512
T_COLS = 768
Y_DQ, Y_GQ, Y_DK, Y_GK = 0, 512, 1024, 1536
Y_ROWS, YC_ROWS, Y2_COLS = 1664, 640, 640
GLA_LEVELS = [2, 4, 8, 16, 32, 64, 128, 256, 512]
TOPK = 16
PH = 8
NKEY = 128
PICKS = PH * TOPK


NAMES = itertools.count()


def sbuf(nc, shape, dt):
    return nc.sbuf_tensor(f"sbuf{next(NAMES)}", shape, dt)


def psum(nc, shape, dt):
    return nc.psum_tensor(f"psum{next(NAMES)}", shape, dt)


class Sems:

    def __init__(self, nc, ctx):
        self.nc, self.ctx = nc, ctx

    def one(self, name, credit=0):
        handle = self.ctx.enter_context(self.nc.semaphore(f"{name}_{next(NAMES)}"))
        self.ctx.callback(self.nc.gpsimd.sem_clear, handle)
        if credit:
            self.nc.gpsimd.sem_inc(handle, credit)
        return handle

    def two(self, name, credit=0):
        return [self.one(name + "0", credit), self.one(name + "1", credit)]


def wait_apart(eng, sem, value, passed):
    eng.wait_ge(sem, value)
    eng.sem_inc(passed, 1)


def paired(eng, n, body):
    if n // 2:
        with eng.Fori(0, n // 2) as p:
            body(p, 0)
            body(p, 1)
    if n % 2:
        body(n // 2, 0)


def split_products(nc, acc, kt, w_high, w_low, x_high, x_low):
    for k in range(kt):
        nc.tensor.matmul(acc, w_high(k), x_high(k), start=(k == 0), stop=False)
        nc.tensor.matmul(acc, w_high(k), x_low(k), start=False, stop=False)
        mm = nc.tensor.matmul(acc, w_low(k), x_high(k), start=False, stop=(k == kt - 1))
    return mm


def ahead(eng, pairs, prepare, finish):
    prepare(0, 0)
    prepare(0, 1)
    with eng.Fori(0, pairs - 1) as p:
        for s in range(2):
            finish(p, s)
            prepare(p + 1, s)
    finish(pairs - 1, 0)
    finish(pairs - 1, 1)


def load_all(nc, moves):
    with ExitStack() as ctx:
        landed = Sems(nc, ctx).one("copies_landed")
        block = ctx.enter_context(nc.Block())

        @block.sync
        def _(sp):
            for dst, src in moves:
                sp.dma_start(dst, src).then_inc(landed, 16)
            sp.wait_ge(landed, 16 * len(moves))


def rmsnorm(nc, C, src, gain, dst, n=S, shift=None, kt=KT, store=None):
    with ExitStack() as ctx:
        sem = Sems(nc, ctx)
        squares = ctx.enter_context(sbuf(nc, [P, kt, S], F32))
        root = ctx.enter_context(sbuf(nc, [P, S], F32))
        inv = ctx.enter_context(sbuf(nc, [P, S], F32))
        total = ctx.enter_context(psum(nc, [P, S], F32))
        squared, summed, rooted, inverted, scaled, done, stored = [
            sem.one(x) for x in ("squared", "summed", "rooted", "inverted", "scaled", "norm_done", "norm_stored")]
        block = ctx.enter_context(nc.Block())

        @block.scalar
        def _(act):
            for k in range(kt):
                nc.scalar.activation(squares[:, k, :n], src[:, k, :n], ACT.Square).then_inc(squared, 1)
            act.wait_ge(summed, 1)
            nc.scalar.activation(root[:, :n], total[:, :n], ACT.Sqrt, bias=C.eps[:, 0:1],
                                 scale=1.0 / (kt * P)).then_inc(rooted, 1)

        @block.tensor
        def _(pe):
            for k in range(kt):
                pe.wait_ge(squared, k + 1)
                mm = nc.tensor.matmul(total[:, :n], C.ones[:, :], squares[:, k, :n], start=(k == 0), stop=(k == kt - 1))
            mm.then_inc(summed, 1)

        @block.vector
        def _(dve):
            dve.wait_ge(rooted, 1)
            nc.vector.reciprocal(inv[:, :n], root[:, :n]).then_inc(inverted, 1)
            dve.wait_ge(inverted, 1)
            for k in range(kt):
                op = nc.vector.scalar_tensor_tensor(dst[:, k, :n], src[:, k, :n], gain[:, k:k + 1], inv[:, :n],
                                                    ALU.mult, ALU.mult)
                op.then_inc(scaled, 1)
                if shift is not None:
                    dve.wait_ge(scaled, k + 1)
                    nc.vector.tensor_scalar(dst[:, k, :n], dst[:, k, :n], shift[:, k:k + 1], None,
                                            ALU.add).then_inc(done, 1)

        @block.sync
        def _(sp):
            if store is not None:
                for k in range(kt):
                    sp.wait_ge(done if shift is not None else scaled, k + 1)
                    sp.dma_start(store[k * P:(k + 1) * P, :], dst[:, k, :n]).then_inc(stored, 16)
                sp.wait_ge(stored, 16 * kt)


def project(nc, C, weight, n, rhs, cols, dst):
    with ExitStack() as ctx:
        sem = Sems(nc, ctx)
        w = ctx.enter_context(sbuf(nc, [P, 2, KT * P], F32))
        out = ctx.enter_context(sbuf(nc, [P, 2, cols], F32))
        acc = ctx.enter_context(psum(nc, [P, 2, S], F32))
        w_landed = sem.two("w_landed")
        mm_done, evacuated, stored = sem.two("mm_done", 1), sem.two("evacuated", 1), sem.two("stored", 16)
        block = ctx.enter_context(nc.Block())

        @block.sync
        def _(sp):
            def body(p, s):
                sp.wait_ge(mm_done[s], p + 1)
                sp.dma_start(w[:, s, :], weight[2 * p + s]).then_inc(w_landed[s], 16)
            paired(sp, n, body)

        @block.tensor
        def _(pe):
            def body(p, s):
                pe.wait_ge(evacuated[s], p + 1)
                pe.wait_ge(w_landed[s], 16 * p + 16)
                for k in range(KT):
                    mm = nc.tensor.matmul(acc[:, s, :cols], w[:, s, k * P:(k + 1) * P], rhs(k),
                                          start=(k == 0), stop=(k == KT - 1))
                mm.then_inc(mm_done[s], 1)
            paired(pe, n, body)

        @block.scalar
        def _(act):
            def body(p, s):
                act.wait_ge(stored[s], 16 * p + 16)
                act.wait_ge(mm_done[s], p + 2)
                nc.scalar.activation(out[:, s, :], acc[:, s, :cols], ACT.Copy).then_inc(evacuated[s], 1)
                act.wait_ge(evacuated[s], p + 2)
                act.dma_start(dst[bass.ds((2 * p + s) * P, P), :], out[:, s, :]).then_inc(stored[s], 16)
            paired(act, n, body)
            for s in range(min(2, n)):
                act.wait_ge(stored[s], 16 * ((n + 1 - s) // 2) + 16)


def project_tokens(nc, C, weight, width, tiles, lhs, dst):
    with ExitStack() as ctx:
        sem = Sems(nc, ctx)
        w = ctx.enter_context(sbuf(nc, [P, KT, width], F32))
        out = ctx.enter_context(sbuf(nc, [P, tiles, width], F32))
        acc = ctx.enter_context(psum(nc, [P, 2, 2 * S], F32))
        w_landed, mm_done, evacuated, stored = [sem.one(x) for x in ("w_landed", "mm_done", "evacuated", "stored")]
        block = ctx.enter_context(nc.Block())
        half = width // 2

        @block.sync
        def _(sp):
            for k in range(KT):
                sp.dma_start(w[:, k, :], weight[k * P:(k + 1) * P, :]).then_inc(w_landed, 16)
            for t in range(tiles):
                sp.wait_ge(evacuated, 2 * t + 2)
                sp.dma_start(dst[t * P:(t + 1) * P, :], out[:, t, :]).then_inc(stored, 16)
            sp.wait_ge(stored, 16 * tiles)

        @block.tensor
        def _(pe):
            pe.wait_ge(w_landed, 16 * KT)
            for t in range(tiles):
                if t >= 2:
                    pe.wait_ge(evacuated, 2 * (t - 1))
                for c in range(2):
                    for k in range(KT):
                        mm = nc.tensor.matmul(acc[:, t % 2, c * S:c * S + half], lhs(k, t),
                                              w[:, k, c * half:(c + 1) * half], start=(k == 0), stop=(k == KT - 1))
                    mm.then_inc(mm_done, 1)

        @block.scalar
        def _(act):
            for t in range(tiles):
                for c in range(2):
                    act.wait_ge(mm_done, 2 * t + c + 1)
                    nc.scalar.activation(out[:, t, c * half:(c + 1) * half], acc[:, t % 2, c * S:c * S + half],
                                         ACT.Copy).then_inc(evacuated, 1)


def project_add(nc, C, weight, kt, rhs, x, gate=None):
    with ExitStack() as ctx:
        sem = Sems(nc, ctx)
        w = ctx.enter_context(sbuf(nc, [P, 2, kt * P], F32))
        acc = ctx.enter_context(psum(nc, [P, 2, S], F32))
        w_landed, mm_done, added = sem.two("w_landed"), sem.two("mm_done", 1), sem.two("added", 1)
        block = ctx.enter_context(nc.Block())

        @block.sync
        def _(sp):
            def body(p, s):
                sp.wait_ge(mm_done[s], p + 1)
                sp.dma_start(w[:, s, :], weight[2 * p + s]).then_inc(w_landed[s], 16)
            paired(sp, KT, body)

        @block.tensor
        def _(pe):
            def body(p, s):
                pe.wait_ge(added[s], p + 1)
                pe.wait_ge(w_landed[s], 16 * p + 16)
                for k in range(kt):
                    mm = nc.tensor.matmul(acc[:, s, :], w[:, s, k * P:(k + 1) * P], rhs(k),
                                          start=(k == 0), stop=(k == kt - 1))
                mm.then_inc(mm_done[s], 1)
            paired(pe, KT, body)

        @block.vector
        def _(dve):
            def body(p, s):
                dve.wait_ge(mm_done[s], p + 2)
                xt = x[:, 2 * p + s, :]
                g = 1.0 if gate is None else gate[:, bass.ds(2 * p + s, 1)]
                nc.vector.scalar_tensor_tensor(xt, acc[:, s, :], g, xt, ALU.mult, ALU.add).then_inc(added[s], 1)
            paired(dve, KT, body)


def project_add_split(nc, C, weight, kt, x_high, x_low, x):
    with ExitStack() as ctx:
        sem = Sems(nc, ctx)
        w = ctx.enter_context(sbuf(nc, [P, kt * P], F32))
        w_high, w_low = [ctx.enter_context(sbuf(nc, [P, 2, kt * P], F32R)) for _ in range(2)]
        acc = ctx.enter_context(psum(nc, [P, 2, S], F32))
        w_landed, high_done, low_done = sem.one("w_landed"), sem.one("high_done"), sem.one("low_done", 1)
        mm_done, added = sem.two("mm_done", 1), sem.two("added", 1)
        block = ctx.enter_context(nc.Block())

        @block.sync
        def _(sp):
            def body(p, s):
                sp.wait_ge(low_done, 2 * p + s + 1)
                sp.dma_start(w[:, :], weight[2 * p + s]).then_inc(w_landed, 16)
            paired(sp, KT, body)

        @block.tensor
        def _(pe):
            def body(p, s):
                pe.wait_ge(added[s], p + 1)
                pe.wait_ge(low_done, 2 * p + s + 2)
                split_products(nc, acc[:, s, :], kt, lambda k: w_high[:, s, k * P:(k + 1) * P],
                               lambda k: w_low[:, s, k * P:(k + 1) * P],
                               x_high, x_low).then_inc(mm_done[s], 1)
            paired(pe, KT, body)

        @block.scalar
        def _(act):
            def body(p, s):
                act.wait_ge(w_landed, 16 * (2 * p + s) + 16)
                act.wait_ge(mm_done[s], p + 1)
                nc.scalar.activation(w_high[:, s, :], w[:, :], ACT.Copy).then_inc(high_done, 1)
            paired(act, KT, body)

        @block.vector
        def _(dve):
            def split(p, s):
                dve.wait_ge(high_done, 2 * p + s + 1)
                nc.vector.tensor_tensor(w_low[:, s, :], w[:, :], w_high[:, s, :].bitcast(F32),
                                        ALU.subtract).then_inc(low_done, 1)

            def add(p, s):
                dve.wait_ge(mm_done[s], p + 2)
                xt = x[:, 2 * p + s, :]
                nc.vector.tensor_tensor(xt, acc[:, s, :], xt, ALU.add).then_inc(added[s], 1)

            ahead(dve, KT // 2, split, add)


def ffn_up(nc, C, weight, h, a_high, a_low):
    assert FT % 2 == 0
    with ExitStack() as ctx:
        sem = Sems(nc, ctx)
        w = ctx.enter_context(sbuf(nc, [P, 2, KT * P], F32))
        w_high, w_low = [ctx.enter_context(sbuf(nc, [P, 2, KT * P], F32R)) for _ in range(2)]
        h_high, h_low = [ctx.enter_context(sbuf(nc, [P, KT, S], F32R)) for _ in range(2)]
        sig = ctx.enter_context(sbuf(nc, [P, 2, S], F32))
        prod = ctx.enter_context(sbuf(nc, [P, 2, S], F32))
        acc = ctx.enter_context(psum(nc, [P, 4, S], F32))
        w_landed, high_done, gated = sem.two("w_landed"), sem.two("high_done"), sem.two("gated")
        h_highs, h_lows, rounded = [sem.one(x) for x in ("h_highs", "h_lows", "rounded")]
        low_done, mm_done = sem.two("low_done", 1), sem.two("mm_done", 1)
        product, kept = sem.two("product", 1), sem.two("kept", 1)
        block = ctx.enter_context(nc.Block())

        def ahead(eng, split, finish):
            for j in range(2):
                split(0, j)
            with eng.Fori(0, FT // 2 - 1) as p:
                for s in range(2):
                    finish(p, s, lambda j: split(2 * p + s + 1, j))
            finish(FT // 2 - 1, 0, lambda j: split(FT - 1, j))
            finish(FT // 2 - 1, 1, lambda j: None)

        @block.sync
        def _(sp):
            def body(p, s):
                for j in range(2):
                    sp.wait_ge(low_done[j], 2 * p + s + 1)
                    sp.dma_start(w[:, j, :], weight[j, 2 * p + s]).then_inc(w_landed[j], 16)
            paired(sp, FT, body)

        @block.tensor
        def _(pe):
            pe.wait_ge(h_lows, KT)

            def body(p, s):
                pe.wait_ge(product[s], p + 1)
                for j in range(2):
                    pe.wait_ge(low_done[j], 2 * p + s + 2)
                    split_products(nc, acc[:, 2 * s + j, :], KT, lambda k: w_high[:, j, k * P:(k + 1) * P],
                                   lambda k: w_low[:, j, k * P:(k + 1) * P], lambda k: h_high[:, k, :],
                                   lambda k: h_low[:, k, :]).then_inc(mm_done[j], 1)
            paired(pe, FT, body)

        @block.scalar
        def _(act):
            for k in range(KT):
                nc.scalar.activation(h_high[:, k, :], h[:, k, :], ACT.Copy).then_inc(h_highs, 1)

            def split(i, j):
                act.wait_ge(w_landed[j], 16 * i + 16)
                act.wait_ge(mm_done[j], i + 1)
                nc.scalar.activation(w_high[:, j, :], w[:, j, :], ACT.Copy).then_inc(high_done[j], 1)

            def gate(p, s, split_next):
                split_next(0)
                act.wait_ge(product[s], p + 1)
                act.wait_ge(mm_done[0], 2 * p + s + 2)
                nc.scalar.activation(sig[:, s, :], acc[:, 2 * s, :], ACT.Silu).then_inc(gated[s], 1)
                split_next(1)

            ahead(act, split, gate)

        @block.vector
        def _(dve):
            for k in range(KT):
                dve.wait_ge(h_highs, k + 1)
                nc.vector.tensor_tensor(h_low[:, k, :], h[:, k, :], h_high[:, k, :].bitcast(F32),
                                        ALU.subtract).then_inc(h_lows, 1)

            def split(i, j):
                dve.wait_ge(high_done[j], i + 1)
                nc.vector.tensor_tensor(w_low[:, j, :], w[:, j, :], w_high[:, j, :].bitcast(F32),
                                        ALU.subtract).then_inc(low_done[j], 1)

            def multiply(p, s, split_next):
                split_next(0)
                split_next(1)
                dve.wait_ge(gated[s], p + 1)
                dve.wait_ge(mm_done[1], 2 * p + s + 2)
                dve.wait_ge(kept[s], p + 1)
                nc.vector.tensor_tensor(prod[:, s, :], sig[:, s, :], acc[:, 2 * s + 1, :],
                                        ALU.mult).then_inc(product[s], 1)
                dve.wait_ge(product[s], p + 2)
                nc.vector.tensor_copy(a_high[:, 2 * p + s, :], prod[:, s, :]).then_inc(rounded, 1)
                dve.wait_ge(rounded, 2 * p + s + 1)
                nc.vector.tensor_tensor(a_low[:, 2 * p + s, :], prod[:, s, :], a_high[:, 2 * p + s, :].bitcast(F32),
                                        ALU.subtract).then_inc(kept[s], 1)

            ahead(dve, split, multiply)


def rope(nc, C, src, dst, n, cos, sin, rot, cols=S, col0=0, head_gain=None):
    with ExitStack() as ctx:
        sem = Sems(nc, ctx)
        z, zn, sq, a, b, out = [ctx.enter_context(sbuf(nc, [P, 2, cols], F32)) for _ in range(6)]
        turned = ctx.enter_context(psum(nc, [P, 2, S], F32))
        total = ctx.enter_context(psum(nc, [P, 2, S], F32))
        landed, squared, summed, rooted, turn_done, cos_done = [
            sem.two(x) for x in ("z_landed", "squared", "sq_summed", "rooted", "turned", "cos_done")]
        inverted, normed, sin_done, summed2 = [sem.two(x, 1) for x in ("inverted", "normed", "sin_done", "roped")]
        stored = sem.two("stored", 16)
        block = ctx.enter_context(nc.Block())
        x = zn if head_gain is not None else z
        ready, unit, first = (normed, 1, 2) if head_gain is not None else (landed, 16, 16)
        last = summed2 if cos is not None else normed
        fin = out if cos is not None else zn

        @block.sync
        def _(sp):
            def body(p, s):
                sp.wait_ge(last[s], p + 1)
                sp.dma_start(z[:, s, :], src[bass.ds((2 * p + s) * P, P), :]).then_inc(landed[s], 16)
            paired(sp, n, body)

        @block.tensor
        def _(pe):
            def body(p, s):
                if head_gain is not None:
                    pe.wait_ge(inverted[s], p + 1)
                    pe.wait_ge(squared[s], p + 1)
                    nc.tensor.matmul(total[:, s, :cols], C.ones64[:, :], sq[:, s, :],
                                     start=True, stop=True).then_inc(summed[s], 1)
                if cos is not None:
                    pe.wait_ge(sin_done[s], p + 1)
                    pe.wait_ge(ready[s], unit * p + first)
                    nc.tensor.matmul(turned[:, s, :cols], rot[:, :], x[:, s, :],
                                     start=True, stop=True).then_inc(turn_done[s], 1)
            paired(pe, n, body)

        @block.scalar
        def _(act):
            def body(p, s):
                if head_gain is not None:
                    act.wait_ge(landed[s], 16 * (p + 1))
                    nc.scalar.activation(sq[:, s, :], z[:, s, :], ACT.Square).then_inc(squared[s], 1)
                    act.wait_ge(summed[s], p + 1)
                    nc.scalar.activation(a[:, s, :], total[:, s, :cols], ACT.Sqrt, bias=C.eps[:, 0:1],
                                         scale=1.0 / HD).then_inc(rooted[s], 1)
                act.wait_ge(last[s], p + 2)
                act.dma_start(dst[bass.ds((2 * p + s) * P, P), col0:col0 + cols], fin[:, s, :]).then_inc(stored[s], 16)
            paired(act, n, body)
            for s in range(min(2, n)):
                act.wait_ge(stored[s], 16 * ((n + 1 - s) // 2) + 16)

        @block.vector
        def _(dve):
            def body(p, s):
                if head_gain is not None:
                    dve.wait_ge(rooted[s], p + 1)
                    nc.vector.reciprocal(b[:, s, :], a[:, s, :]).then_inc(inverted[s], 1)
                    dve.wait_ge(inverted[s], p + 2)
                    if cos is None:
                        dve.wait_ge(stored[s], 16 * p + 16)
                    nc.vector.scalar_tensor_tensor(zn[:, s, :], z[:, s, :], head_gain, b[:, s, :], ALU.mult,
                                                   ALU.mult).then_inc(normed[s], 1)
                    dve.wait_ge(normed[s], p + 2)
                else:
                    dve.wait_ge(landed[s], 16 * (p + 1))
                if cos is not None:
                    nc.vector.tensor_tensor(a[:, s, :], x[:, s, :], cos[:, :], ALU.mult).then_inc(cos_done[s], 1)
                    dve.wait_ge(turn_done[s], p + 1)
                    nc.vector.tensor_tensor(b[:, s, :], turned[:, s, :cols], sin[:, :], ALU.mult).then_inc(sin_done[s], 1)
                    dve.wait_ge(cos_done[s], p + 1)
                    dve.wait_ge(sin_done[s], p + 2)
                    dve.wait_ge(stored[s], 16 * p + 16)
                    nc.vector.tensor_tensor(out[:, s, :], a[:, s, :], b[:, s, :], ALU.add).then_inc(summed2[s], 1)
            paired(dve, n, body)


def attention(nc, C, steps, q_src, k_src, v_src, keys, causal, dv, dst, gate=None, acc=None,
              first=False, own_mask=None):
    kt = (keys + P - 1) // P
    kw = [min(P, keys - j * P) for j in range(kt)]
    q0 = [j * P if causal else 0 for j in range(kt)]
    with ExitStack() as ctx:
        sem = Sems(nc, ctx)
        sb = lambda shape: ctx.enter_context(sbuf(nc, shape, F32))
        q = sb([HD + 1, 4, S])
        k = sb([HD + 1, 4, kt * P])
        v = sb([P, 4, kt, P])
        gates = sb([P, 4, S])
        prob = sb([P, 2, kt, S])
        rowmax = sb([P, 2, ST])
        diag = sb([P, 2, ST, P])
        den, inv, part, part2 = [sb([P, 2, S]) for _ in range(4)]
        stride = S if keys <= S else 2 * S
        outs = 2 if stride == S else 1
        scores = ctx.enter_context(psum(nc, [P, 2 * stride], F32))
        shifted = ctx.enter_context(psum(nc, [P, 2, S], F32))
        summed = ctx.enter_context(psum(nc, [P, outs, S], F32))
        aux = ctx.enter_context(psum(nc, [P, S], F32))
        landed = [sem.one(f"qkv_landed{s}") for s in range(4)]
        diag_made, row_made, row_placed, pv_done, max_read, exp_read = [sem.two(x, 1) for x in (
            "diag_made", "row_made", "row_placed", "pv_done", "max_read", "exp_read")]
        out_made = sem.two("out_made", 2)
        stored, out_free = sem.two("out_stored"), sem.two("out_free", 1)
        scores_made, shifted_made, ones_set = sem.one("scores_made"), sem.one("shifted_made"), sem.one("ones_set")
        den_floored, inverted, gated = [sem.one(x, c) for x, c in (
            ("den_floored", 0), ("inverted", 1), ("gated", 0))]
        read_out = sem.two("read_out", 1)
        loads = 3 + (gate is not None)
        wide = dv == P
        block = ctx.enter_context(nc.Block())

        def ahead(eng, by, early, late):
            def at(p, s):
                p, s = (p, s) if s < 4 else (p + 1, s - 4)
                return p, s, s % 2, 2 * p + s // 2
            for s in range(by):
                early(*at(0, s))
            with eng.Fori(0, steps - 1) as p:
                for s in range(4):
                    early(*at(p, s + by))
                    late(*at(p, s))
            for s in range(4):
                if s + by < 4:
                    early(*at(steps - 1, s + by))
                late(*at(steps - 1, s))

        def in_turn(eng, body):
            with eng.Fori(0, steps) as p:
                for s in range(4):
                    body(p, s, s % 2, 2 * p + s // 2)

        @block.sync
        def _(sp):
            def body(p, s, w, m):
                sp.wait_ge(out_made[w], m + 1)
                sp.dma_start(q[0:HD, s, :], q_src(p, s)).then_inc(landed[s], 16)
                sp.dma_start(k[0:HD, s, 0:keys], k_src(p, s)).then_inc(landed[s], 16)
                if keys % P:
                    sp.dma_start(v[0:keys, s, 0, 0:dv], v_src(p, s)).then_inc(landed[s], 16)
                else:
                    sp.dma_start(v[:, s, :, 0:dv], v_src(p, s)).then_inc(landed[s], 16)
                if gate is not None:
                    sp.dma_start(gates[0:HD, s, :], gate(p, s)).then_inc(landed[s], 16)
            in_turn(sp, body)

        @block.tensor
        def _(pe):
            def raw_scores(p, s, w, m):
                pe.wait_ge(landed[s], 16 * loads * p + 16 * loads)
                for t in range(ST):
                    n = (t + 1) * P if causal else keys
                    pe.wait_ge(max_read[t % 2], 2 * (4 * p + s) + t // 2 + 1)
                    base = t % 2 * stride
                    for c in range(0, n, S):
                        e = min(c + S, n)
                        mm = nc.tensor.matmul(scores[:, base + c:base + e], q[0:HD, s, t * P:(t + 1) * P],
                                              k[0:HD, s, c:e], start=True, stop=True)
                    if causal:
                        mm = nc.tensor.matmul(scores[:, base + n - P:base + n], C.ident_b[:, :], C.mask_q[:, :],
                                              start=False, stop=True, skip_group_check=True)
                    if own_mask is not None:
                        mm = nc.tensor.matmul(scores[:, base:base + keys], C.ident_b[:, :], own_mask[0][:, t, 0:keys],
                                              start=False, stop=True, skip_group_check=True)
                    mm.then_inc(scores_made, 1)

            def finish(p, s, w, m):
                head = 4 * p + s
                pe.wait_ge(diag_made[w], m + 2)
                pe.wait_ge(row_placed[1 - w], m + 1 + w)
                if wide:
                    pe.wait_ge(inverted, head + 1)
                nc.tensor.matmul(aux[0:1, :], C.ones[:, 0:1], diag[:, w, :, :],
                                 start=True, stop=True).then_inc(row_made[w], 1)
                pe.wait_ge(row_placed[w], m + 2)
                pe.wait_ge(ones_set, 1 if wide else 2)
                for j in range(kt):
                    pe.wait_ge(exp_read[j % 2], head * ((kt + 1 - j % 2) // 2) + j // 2 + 1)
                    mm = nc.tensor.matmul(shifted[0:kw[j], j % 2, q0[j]:S], k[:, s, j * P:j * P + kw[j]],
                                          q[:, s, q0[j]:S], start=True, stop=True)
                    if causal:
                        mm = nc.tensor.matmul(shifted[:, j % 2, q0[j]:q0[j] + P], C.ident_b[:, :], C.mask_k[:, :],
                                              start=False, stop=True, skip_group_check=True)
                    if own_mask is not None:
                        mm = nc.tensor.matmul(shifted[0:keys, 0, :], C.ident_b[0:keys, 0:keys], own_mask[1][0:keys, :],
                                              start=False, stop=True, skip_group_check=True)
                    mm.then_inc(shifted_made, 1)
                    if j > 0:
                        values(head, s, w, m, j - 1)
                mm = values(head, s, w, m, kt - 1)
                if wide:
                    for j in range(kt):
                        mm = nc.tensor.matmul(aux[:, :], C.ones[:, :], prob[:, w, j, :],
                                              start=(j == 0), stop=(j == kt - 1))
                mm.then_inc(pv_done[w], 1)

            def values(head, s, w, m, j):
                pe.wait_ge(exp_read[j % 2], head * ((kt + 1 - j % 2) // 2) + j // 2 + 2)
                if j == 0 and outs == 2:
                    pe.wait_ge(read_out[w], m + 1)
                elif j == 0:
                    pe.wait_ge(read_out[1 - w], m + 1 + w)
                return nc.tensor.matmul(summed[:, w % outs, q0[j]:S], v[0:kw[j], s, j, :], prob[0:kw[j], w, j, q0[j]:S],
                                        start=(j == 0), stop=(j == kt - 1))
            ahead(pe, 1, raw_scores, finish)

        @block.vector
        def _(dve):
            nc.vector.memset(k[HD:HD + 1, :, :], 1.0).then_inc(ones_set, 1)
            if not wide:
                nc.vector.memset(v[:, :, :, HD:P], 1.0).then_inc(ones_set, 1)

            def maxima(p, s, w, m):
                head = 4 * p + s
                for t in range(ST):
                    if t == 0:
                        dve.wait_ge(diag_made[w], m + 1)
                    dve.wait_ge(scores_made, 4 * head + t + 1)
                    n = (t + 1) * P if causal else keys
                    nc.vector.tensor_reduce(rowmax[:, w, t:t + 1], scores[:, t % 2 * stride:t % 2 * stride + n], AX_X,
                                            ALU.max).then_inc(max_read[t % 2], 1)
                dve.wait_ge(max_read[0], 2 * head + 3)
                dve.wait_ge(max_read[1], 2 * head + 3)
                dve.wait_ge(row_made[w], m + 1)
                nc.vector.scalar_tensor_tensor(
                    diag[:, w, :, :], rowmax[:, w, :].unsqueeze(2).to_broadcast([P, ST, P]), MAX_FLOOR,
                    C.neg_ident[:, :].unsqueeze(1).to_broadcast([P, ST, P]), ALU.max,
                    ALU.mult).then_inc(diag_made[w], 1)

            def finish(p, s, w, m):
                head = 4 * p + s
                dve.wait_ge(pv_done[w], m + 2)
                dve.wait_ge(out_made[w], m + 2)
                if wide:
                    nc.vector.reciprocal(inv[:, w, :], aux[:, :]).then_inc(inverted, 1)
                elif own_mask is not None:
                    nc.vector.tensor_scalar(den[0:HD, w, :], summed[HD:P, w % outs, :], 1e-30, None,
                                            ALU.max).then_inc(den_floored, 1)
                    dve.wait_ge(den_floored, head + 1)
                    nc.vector.reciprocal(inv[0:HD, w, :], den[0:HD, w, :]).then_inc(inverted, 1)
                else:
                    nc.vector.reciprocal(inv[0:HD, w, :], summed[HD:P, w % outs, :]).then_inc(inverted, 1)
                dve.wait_ge(inverted, head + 2)
                if gate is None:
                    dve.wait_ge(out_free[w], m + 1)
                nc.vector.tensor_tensor(part[0:dv, w, :], summed[0:dv, w % outs, :], inv[0:dv, w, :],
                                        ALU.mult).then_inc(read_out[w], 1)
                dve.wait_ge(read_out[w], m + 2)
                if gate is None:
                    nc.vector.tensor_copy(part2[0:dv, w, :], part[0:dv, w, :]).then_inc(out_made[w], 1)
                elif first:
                    nc.vector.tensor_tensor(acc[:, bass.ds(head, 1), :], part[0:HD, w:w + 1, :],
                                            gates[0:HD, s:s + 1, :], ALU.mult).then_inc(out_made[w], 1)
                else:
                    place = acc[:, bass.ds(head, 1), :]
                    nc.vector.tensor_tensor(part2[0:HD, w, :], part[0:HD, w, :], gates[0:HD, s, :],
                                            ALU.mult).then_inc(gated, 1)
                    dve.wait_ge(gated, head + 1)
                    nc.vector.tensor_tensor(place, part2[0:HD, w:w + 1, :], place, ALU.add).then_inc(out_made[w], 1)
            ahead(dve, 2, maxima, finish)

        @block.scalar
        def _(act):
            def body(p, s, w, m):
                act.wait_ge(row_made[w], m + 2)
                nc.scalar.activation(q[HD:HD + 1, s, :], aux[0:1, :], ACT.Copy).then_inc(row_placed[w], 1)
                act.wait_ge(pv_done[w], m + 1)
                for j in range(kt):
                    act.wait_ge(shifted_made, kt * (4 * p + s) + j + 1)
                    nc.scalar.activation(prob[0:kw[j], w, j, q0[j]:S], shifted[0:kw[j], j % 2, q0[j]:S],
                                         ACT.Exp, scale=HD ** -0.5).then_inc(exp_read[j % 2], 1)
            in_turn(act, body)

        @block.gpsimd
        def _(pool):
            if gate is None:
                def body(p, s, w, m):
                    pool.wait_ge(out_made[w], m + 3)
                    pool.dma_start(dst(p, s), part2[0:dv, w, :]).then_inc(stored[w], 16)
                    pool.wait_ge(stored[w], 16 * m + 16)
                    pool.sem_inc(out_free[w], 1)
                in_turn(pool, body)


def cast_masks(nc, src_q, src_k, cmp_q, cmp_k):
    with ExitStack() as ctx:
        sem = Sems(nc, ctx)
        q, k = ctx.enter_context(sbuf(nc, [P, ST, 32], F32)), ctx.enter_context(sbuf(nc, [32, S], F32))
        landed, cast = sem.one("landed"), sem.one("cast")
        block = ctx.enter_context(nc.Block())

        @block.sync
        def _(sp):
            sp.dma_start(q[:, :, :], src_q).then_inc(landed, 16)
            sp.dma_start(k[:, :], src_k).then_inc(landed, 16)

        @block.vector
        def _(dve):
            dve.wait_ge(landed, 32)
            nc.vector.tensor_copy(cmp_q[:, :, :], q[:, :, :]).then_inc(cast, 1)
            nc.vector.tensor_copy(cmp_k[:, :], k[:, :]).then_inc(cast, 1)


def gates_and_rank(nc, C, weight, h, gates_d, rank_d):
    with ExitStack() as ctx:
        sem = Sems(nc, ctx)
        w = ctx.enter_context(sbuf(nc, [P, KT, 40], F32))
        g, r = [ctx.enter_context(sbuf(nc, [40, S], F32)) for _ in range(2)]
        acc = ctx.enter_context(psum(nc, [P, S], F32))
        landed, mm_done, made, stored = [sem.one(x) for x in ("w_landed", "mm_done", "made", "stored")]
        block = ctx.enter_context(nc.Block())

        @block.sync
        def _(sp):
            sp.dma_start(w[:, :, :], weight).then_inc(landed, 16)
            sp.wait_ge(made, 2)
            sp.dma_start(gates_d, g[0:24, :]).then_inc(stored, 16)
            sp.dma_start(rank_d, r[24:40, :]).then_inc(stored, 16)
            sp.wait_ge(stored, 32)

        @block.tensor
        def _(pe):
            pe.wait_ge(landed, 16)
            for k in range(KT):
                mm = nc.tensor.matmul(acc[0:40, :], w[:, k, :], h[:, k, :], start=(k == 0), stop=(k == KT - 1))
            mm.then_inc(mm_done, 1)

        @block.scalar
        def _(act):
            act.wait_ge(mm_done, 1)
            nc.scalar.activation(g[:, :], acc[0:40, :], ACT.Sigmoid).then_inc(made, 1)
            nc.scalar.activation(r[:, :], acc[0:40, :], ACT.Copy).then_inc(made, 1)


def compress(nc, C, zT, w1s, w1_landed, w2, pos, kc_d, vc_d):
    nb = NC_BLK
    with ExitStack() as ctx:
        sem = Sems(nc, ctx)
        sb = lambda shape: ctx.enter_context(sbuf(nc, shape, F32))
        raw, w2s, poss = sb([P, 4, S]), sb([P, 2, 2, HD]), sb([P, 2, 16])
        blocks, hidt = sb([P, 2, 16, 2 * nb]), sb([2 * nb, 2, 256])
        hid = sb([P, 4, 2 * nb])
        kc, kcos, ksin, kout, vc = sb([HD, 2 * nb]), sb([HD, 2 * nb]), sb([HD, 2 * nb]), sb([HD, 2 * nb]), sb([nb, 2, HD])
        acc = ctx.enter_context(psum(nc, [P, 2, S], F32))
        acct = ctx.enter_context(psum(nc, [P, S], F32))
        acck = ctx.enter_context(psum(nc, [P, 2, S], F32))
        landed, hid_mm, blocks_made, hidt_made, hid_turned, hid_made, kc_mm, kc_copied, turned, vc_mm, dve_done, roped, vc_made, stored = [
            sem.one(x) for x in ("landed", "hid_mm", "blocks_made", "hidt_made", "hid_turned", "hid_made", "kc_mm", "kc_copied", "turned",
                                 "vc_mm", "parts_made", "roped", "vc_made", "stored")]
        block = ctx.enter_context(nc.Block())

        @block.sync
        def _(sp):
            n = 0
            for j in range(2):
                base = (Z_KC, Z_VC)[j]
                for g in range(2):
                    rows = zT[base + g * HD:base + (g + 1) * HD, :]
                    sp.dma_start(raw[0:HD, 2 * j + g, :], rows).then_inc(landed, 16)
                    sp.dma_start(raw[HD:P, 2 * j + g, 0:S - 1], rows[:, 1:S]).then_inc(landed, 16)
                sp.dma_start(w2s[:, j, :, :], w2[j]).then_inc(landed, 16)
                sp.dma_start(poss[:, j, :], pos[j]).then_inc(landed, 16)
            sp.wait_ge(roped, 1)
            for g in range(2):
                sp.dma_start(kc_d[g], kout[:, g * nb:(g + 1) * nb]).then_inc(stored, 16)
            sp.wait_ge(vc_made, 1)
            for g in range(2):
                sp.dma_start(vc_d[g], vc[:, g, :]).then_inc(stored, 16)
            sp.wait_ge(stored, 64)

        @block.tensor
        def _(pe):
            pe.wait_ge(w1_landed, 32)
            for j in range(2):
                pe.wait_ge(blocks_made, 16 * (j + 1))
                for ch in range(16):
                    mm = nc.tensor.matmul(acc[0:2 * nb, j, 0:256], blocks[:, j, ch, :], w1s[:, j, ch, :],
                                          start=(ch == 0), stop=(ch == 15))
                mm.then_inc(hid_mm, 1)
            for j in range(2):
                pe.wait_ge(hidt_made, j + 1)
                for m in range(2):
                    at = (2 * j + m) * 2 * nb
                    mm = nc.tensor.transpose(acct[:, at:at + 2 * nb], hidt[:, j, m * P:(m + 1) * P],
                                             C.ident[0:2 * nb, 0:2 * nb])
            mm.then_inc(hid_turned, 1)
            pe.wait_ge(hid_made, 1)
            for m in range(2):
                mm = nc.tensor.matmul(acck[0:HD, 0, 0:2 * nb], w2s[:, 0, m, :], hid[:, m, :], start=(m == 0), stop=(m == 1))
            mm.then_inc(kc_mm, 1)
            for g in range(2):
                for m in range(2):
                    mm = nc.tensor.matmul(acck[0:nb, 1, g * HD:(g + 1) * HD], hid[:, 2 + m, g * nb:(g + 1) * nb],
                                          w2s[:, 1, m, :], start=(m == 0), stop=(m == 1))
            mm.then_inc(vc_mm, 1)
            pe.wait_ge(kc_copied, 1)
            nc.tensor.matmul(acck[0:HD, 0, 128:128 + 2 * nb], C.rot[0:HD, 0:HD], kc[:, :], start=True,
                             stop=True).then_inc(turned, 1)

        @block.scalar
        def _(act):
            for j in range(2):
                act.wait_ge(hid_mm, j + 1)
                nc.scalar.activation(hidt[:, j, :], acc[0:2 * nb, j, 0:256], ACT.Gelu_apprx_tanh).then_inc(hidt_made, 1)
            act.wait_ge(hid_turned, 1)
            nc.scalar.activation(hid[:, :, :], acct[:, 0:8 * nb].rearrange("p (i n) -> p i n", i=4),
                                 ACT.Copy).then_inc(hid_made, 1)
            act.wait_ge(kc_mm, 1)
            nc.scalar.activation(kc[:, :], acck[0:HD, 0, 0:2 * nb], ACT.Copy).then_inc(kc_copied, 1)
            act.wait_ge(vc_mm, 1)
            nc.scalar.activation(vc[:, :, :], acck[0:nb, 1, 0:2 * HD].rearrange("p (g d) -> p g d", g=2),
                                 ACT.Copy).then_inc(vc_made, 1)

        @block.vector
        def _(dve):
            dve.wait_ge(landed, 16 * 12)
            for j in range(2):
                for ch in range(16):
                    nc.vector.tensor_scalar(blocks[:, j, ch, :].rearrange("p (g n) -> p g n", g=2),
                                            raw[:, 2 * j:2 * j + 2, 2 * ch:2 * ch + 16 * (nb - 1) + 1:16],
                                            poss[:, j, ch:ch + 1], None, ALU.add).then_inc(blocks_made, 1)
            dve.wait_ge(kc_copied, 1)
            nc.vector.tensor_tensor(kcos[:, :], kc[:, :], C.kc_cos[:, :], ALU.mult).then_inc(dve_done, 1)
            dve.wait_ge(turned, 1)
            nc.vector.tensor_tensor(ksin[:, :], acck[0:HD, 0, 128:128 + 2 * nb], C.kc_sin[:, :],
                                    ALU.mult).then_inc(dve_done, 1)
            dve.wait_ge(dve_done, 2)
            nc.vector.tensor_tensor(kout[:, :], kcos[:, :], ksin[:, :], ALU.add).then_inc(roped, 1)


def spatial_gate(nc, C, zT, ztok, w_d, b_d, lng_d, lnb_d, mix):
    G = 4
    with ExitStack() as ctx:
        sem = Sems(nc, ctx)
        sb = lambda shape: ctx.enter_context(sbuf(nc, shape, F32))
        u, v, w, wm, b = sb([HD, G, S]), sb([P, ST, 256]), sb([P, G, P]), sb([P, G, P]), sb([1, G * P])
        lng, lnb, sq, out = sb([P, 256]), sb([P, 256]), sb([P, ST, 256]), sb([HD, G, S])
        vg, ug = sb([P, ST, 256]), sb([HD, G, S])
        mean, var, root, inv = sb([P, ST]), sb([P, ST]), sb([P, ST]), sb([P, ST])
        acc = ctx.enter_context(psum(nc, [HD, G, S], F32))
        landed, act_done, dve_done, mm_done, made, stored = [
            sem.one(x) for x in ("landed", "act_done", "dve_done", "mm_done", "out_made", "stored")]
        block = ctx.enter_context(nc.Block())
        over = lambda t: t[:, :].unsqueeze(2).to_broadcast([P, ST, 256])
        along = lambda t: t[:, :].unsqueeze(1).to_broadcast([P, ST, 256])

        @block.sync
        def _(sp):
            for dst, src in ((v[:, :, :], ztok[:, T_V:T_V + 256].rearrange("(t p) c -> p t c", p=P)),
                             (u[:, :, :], zT[Z_U:Z_U + 256, :].rearrange("(g p) s -> p g s", p=HD)),
                             (w[:, :, :], w_d), (b[:, :], b_d), (lng[:, :], lng_d.to_broadcast([P, 256])),
                             (lnb[:, :], lnb_d.to_broadcast([P, 256]))):
                sp.dma_start(dst, src).then_inc(landed, 16)
            sp.wait_ge(made, 1)
            sp.dma_start(mix[768:1024, :].rearrange("(g p) s -> p g s", p=HD), out[:, :, :]).then_inc(stored, 16)
            sp.wait_ge(stored, 16)

        @block.scalar
        def _(act):
            act.wait_ge(landed, 96)
            nc.scalar.activation(vg[:, :, :], v[:, :, :], ACT.Gelu_apprx_tanh).then_inc(act_done, 1)
            nc.scalar.activation(ug[:, :, :], u[:, :, :], ACT.Gelu_apprx_tanh).then_inc(act_done, 1)
            act.wait_ge(dve_done, 3)
            nc.scalar.activation(sq[:, :, :], v[:, :, :], ACT.Square).then_inc(act_done, 1)
            act.wait_ge(dve_done, 4)
            nc.scalar.activation(root[:, :], var[:, :], ACT.Sqrt, bias=C.eps[:, 0:1], scale=1 / 256).then_inc(act_done, 1)

        @block.vector
        def _(dve):
            dve.wait_ge(act_done, 1)
            nc.vector.tensor_reduce(mean[:, :], vg[:, :, :], AX_X, ALU.add).then_inc(dve_done, 1)
            dve.wait_ge(dve_done, 1)
            nc.vector.tensor_scalar(mean[:, :], mean[:, :], 1 / 256, None, ALU.mult).then_inc(dve_done, 1)
            dve.wait_ge(dve_done, 2)
            nc.vector.tensor_tensor(v[:, :, :], vg[:, :, :], over(mean), ALU.subtract).then_inc(dve_done, 1)
            dve.wait_ge(act_done, 3)
            nc.vector.tensor_reduce(var[:, :], sq[:, :, :], AX_X, ALU.add).then_inc(dve_done, 1)
            dve.wait_ge(act_done, 4)
            nc.vector.reciprocal(inv[:, :], root[:, :]).then_inc(dve_done, 1)
            dve.wait_ge(dve_done, 5)
            nc.vector.tensor_tensor(vg[:, :, :], v[:, :, :], over(inv), ALU.mult).then_inc(dve_done, 1)
            dve.wait_ge(dve_done, 6)
            nc.vector.tensor_tensor(v[:, :, :], vg[:, :, :], along(lng), ALU.mult).then_inc(dve_done, 1)
            dve.wait_ge(dve_done, 7)
            nc.vector.tensor_tensor(vg[:, :, :], v[:, :, :], along(lnb), ALU.add).then_inc(dve_done, 1)
            nc.vector.tensor_tensor(wm[:, :, :], w[:, :, :], C.causal[:, :].unsqueeze(1).to_broadcast([P, G, P]),
                                    ALU.mult).then_inc(dve_done, 1)
            dve.wait_ge(mm_done, 1)
            dve.wait_ge(act_done, 2)
            nc.vector.tensor_tensor(out[:, :, :], acc[:, :, :], ug[:, :, :], ALU.mult).then_inc(made, 1)

        @block.tensor
        def _(pe):
            pe.wait_ge(dve_done, 9)
            for g in range(G):
                for t in range(ST):
                    place = acc[:, g, t * P:(t + 1) * P]
                    nc.tensor.matmul(place, vg[:, t, g * HD:(g + 1) * HD], wm[:, g, :], start=True, stop=False)
                    mm = nc.tensor.matmul(place, C.ones[0:1, 0:HD], b[0:1, g * P:(g + 1) * P], start=False, stop=True)
            mm.then_inc(mm_done, 1)


def gla(nc, C, zT, ztok, rank_d, wup_d, bup_d, norm_d, mix):
    H, DK = 4, 32
    with ExitStack() as ctx:
        sem = Sems(nc, ctx)
        sb = lambda shape: ctx.enter_context(sbuf(nc, shape, F32))
        q, k, b, diff, decay, tmp, tmp2 = [sb([P, S]) for _ in range(7)]
        qd, kd = sb([P, 2, S]), sb([P, 2, S])
        rank, wup, bup, norm = sb([16, S]), sb([16, P]), sb([P, 1]), sb([HD, 1])
        v, r = sb([P, ST, 256]), sb([HD, H, S])
        att = sb([P, H, 2, S])
        att23 = sb([P, H, P])
        near = sb([P, H, ST, P])
        masked = sb([P, H, ST, P])
        o, osq, oroot, oinv, rs = sb([HD, H, S]), sb([HD, H, S]), sb([HD, H, S]), sb([HD, H, S]), sb([HD, H, S])
        acc = ctx.enter_context(psum(nc, [P, H, S], F32))
        acc2 = ctx.enter_context(psum(nc, [P, H, S], F32))
        landed, dve_done, act_done, z_mm, level_mm, level_read, o_mm, rms_mm, made, stored = [sem.one(x) for x in (
            "landed", "dve_done", "act_done", "z_mm", "level_mm", "level_read", "o_mm", "rms_mm", "out_made", "stored")]
        factors, decayed, diffed = sem.one("factors_made"), sem.one("decayed"), sem.one("diffed")
        block = ctx.enter_context(nc.Block())
        levels = [1] + GLA_LEVELS

        @block.sync
        def _(sp):
            for dst, src in ((q[:, :], zT[Z_GQ:Z_GQ + P, :]), (k[:, :], zT[Z_GK:Z_GK + P, :]),
                             (rank[:, :], rank_d), (wup[:, :], wup_d), (bup[:, :], bup_d), (norm[:, :], norm_d),
                             (v[:, :, :], ztok[:, T_GV:T_GV + 256].rearrange("(t p) c -> p t c", p=P)),
                             (r[:, :, :], zT[Z_GR:Z_GR + 256, :].rearrange("(h p) s -> p h s", p=HD))):
                sp.dma_start(dst, src).then_inc(landed, 16)
            sp.wait_ge(made, 1)
            sp.dma_start(mix[512:768, :].rearrange("(h p) s -> p h s", p=HD), o[:, :, :]).then_inc(stored, 16)
            sp.wait_ge(stored, 16)

        @block.tensor
        def _(pe):
            pe.wait_ge(landed, 128)
            nc.tensor.matmul(acc[:, 0, :], wup[:, :], rank[:, :], start=True, stop=True).then_inc(z_mm, 1)
            for n, s in enumerate(levels):
                pe.wait_ge(factors, 2 * n + 2)
                bank = (acc, acc2)[n % 2]
                if n >= 2:
                    pe.wait_ge(level_read, n - 1)
                if n == 0:
                    pe.wait_ge(dve_done, 1)
                if s <= P:
                    pairs = [(t, t, t) for t in range(ST)]
                elif s == 256:
                    pairs = [(0, 0, 1), (1, 2, 3)]
                else:
                    pairs = [(0, 0, 2), (1, 0, 3), (2, 1, 2), (3, 1, 3)]
                for place, jt, it in pairs:
                    for h in range(H):
                        rows = slice(h * DK, (h + 1) * DK)
                        mm = nc.tensor.matmul(bank[:, h, place * P:(place + 1) * P],
                                              kd[rows, n % 2, jt * P:(jt + 1) * P],
                                              qd[rows, n % 2, it * P:(it + 1) * P], start=True, stop=True)
                mm.then_inc(level_mm, 1)
            pe.wait_ge(level_read, len(levels))
            for h in range(H):
                for i in range(ST):
                    for j in range(i + 1):
                        pairs_ij = (near[:, h, i, :] if j == i else att23[:, h, :] if j == 2
                                    else att[:, h, j, i * P:(i + 1) * P])
                        mm = nc.tensor.matmul(acc[0:HD, h, i * P:(i + 1) * P], v[:, j, h * HD:(h + 1) * HD], pairs_ij,
                                              start=(j == 0), stop=(j == i))
            mm.then_inc(o_mm, 1)
            pe.wait_ge(act_done, 5)
            for h in range(H):
                mm = nc.tensor.matmul(acc2[0:HD, h, :], C.ones[0:HD, 0:HD], osq[:, h, :], start=True, stop=True)
            mm.then_inc(rms_mm, 1)

        @block.scalar
        def _(act):
            act.wait_ge(dve_done, 3)
            nc.scalar.activation(tmp[:, :], diff[:, :], ACT.Exp).then_inc(act_done, 1)
            act.wait_ge(act_done, 1)
            nc.scalar.activation(decay[:, :], tmp[:, :], ACT.Ln, bias=1.0).then_inc(act_done, 1)
            for n in range(1, len(levels)):
                act.wait_ge(diffed, 2 * n)
                act.wait_ge(factors, 2 * n)
                nc.scalar.activation(decay[:, :], diff[:, :], ACT.Exp, scale=1 / 16).then_inc(decayed, 1)
            nc.scalar.activation(rs[:, :, :], r[:, :, :], ACT.Silu).then_inc(act_done, 1)
            act.wait_ge(o_mm, 1)
            nc.scalar.activation(o[:, :, :], acc[0:HD, :, :], ACT.Copy).then_inc(act_done, 1)
            nc.scalar.activation(osq[:, :, :], acc[0:HD, :, :], ACT.Square).then_inc(act_done, 1)
            act.wait_ge(rms_mm, 1)
            nc.scalar.activation(oroot[:, :, :], acc2[0:HD, :, :], ACT.Sqrt, bias=C.eps[0:HD, 0:1],
                                 scale=1 / HD).then_inc(act_done, 1)

        @block.vector
        def _(dve):
            dve.wait_ge(z_mm, 1)
            nc.vector.tensor_scalar(b[:, :], acc[:, 0, :], bup[:, 0:1], None, ALU.add).then_inc(dve_done, 1)
            dve.wait_ge(dve_done, 1)
            nc.vector.tensor_scalar(tmp[:, :], b[:, :], -1.0, None, ALU.mult).then_inc(dve_done, 1)
            dve.wait_ge(dve_done, 2)
            nc.vector.tensor_tensor(diff[:, :], b[:, :], tmp[:, :], ALU.min).then_inc(dve_done, 1)
            dve.wait_ge(act_done, 2)
            nc.vector.scalar_tensor_tensor(tmp2[:, :], b[:, :], 0.0, decay[:, :], ALU.min,
                                           ALU.subtract).then_inc(dve_done, 1)
            nc.vector.memset(tmp[:, :], 1.0).then_inc(dve_done, 1)
            dve.wait_ge(dve_done, 5)
            nc.vector.tensor_tensor_scan(b[:, :], tmp[:, :], tmp2[:, :], 0.0, ALU.mult, ALU.add).then_inc(dve_done, 1)
            dve.wait_ge(landed, 128)
            nc.vector.tensor_scalar(q[:, :], q[:, :], DK ** -0.5, None, ALU.mult).then_inc(dve_done, 1)
            dve.wait_ge(dve_done, 7)

            def make_factors(n, s):
                if n >= 2:
                    dve.wait_ge(level_mm, n - 1)
                if s == 1:
                    nc.vector.tensor_copy(qd[:, 0, :], q[:, :]).then_inc(factors, 1)
                    nc.vector.tensor_copy(kd[:, 0, :], k[:, :]).then_inc(factors, 1)
                    return
                if n >= 2:
                    dve.wait_ge(decayed, n - 1)
                half = s // 2
                bv = b[:, :].rearrange("p (n s) -> p n s", s=s)
                dv = diff[:, :].rearrange("p (n s) -> p n s", s=s)
                ref = bv[:, :, half - 1:half].to_broadcast([P, S // s, half])
                nc.vector.tensor_tensor(dv[:, :, half:s], bv[:, :, half:s], ref, ALU.subtract).then_inc(diffed, 1)
                nc.vector.tensor_tensor(dv[:, :, 0:half], ref, bv[:, :, 0:half], ALU.subtract).then_inc(diffed, 1)
                dve.wait_ge(decayed, n)
                nc.vector.tensor_tensor(qd[:, n % 2, :], q[:, :], decay[:, :], ALU.mult).then_inc(factors, 1)
                nc.vector.tensor_tensor(kd[:, n % 2, :], k[:, :], decay[:, :], ALU.mult).then_inc(factors, 1)

            steps = [7]

            def take_level(n, s):
                dve.wait_ge(level_mm, n + 1)
                bank = (acc, acc2)[n % 2]
                if s <= P:
                    mask = C.level_mask[:, n:n + 1, :].unsqueeze(1).to_broadcast([P, H, ST, P])
                    sums = bank[:, :, :].rearrange("p h (t i) -> p h t i", t=ST)
                    if n == 0:
                        nc.vector.tensor_tensor(near[:, :, :, :], sums, mask, ALU.mult).then_inc(level_read, 1)
                    else:
                        nc.vector.tensor_tensor(masked[:, :, :, :], sums, mask, ALU.mult).then_inc(dve_done, 1)
                        steps[0] += 1
                        dve.wait_ge(dve_done, steps[0])
                        dve.wait_ge(level_read, n)
                        nc.vector.tensor_tensor(near[:, :, :, :], near[:, :, :, :], masked[:, :, :, :],
                                                ALU.add).then_inc(level_read, 1)
                elif s == 256:
                    nc.vector.tensor_copy(att[:, :, 0, P:2 * P], bank[:, :, 0:P]).then_inc(dve_done, 1)
                    nc.vector.tensor_copy(att23[:, :, :], bank[:, :, P:2 * P]).then_inc(level_read, 1)
                    steps[0] += 1
                else:
                    nc.vector.tensor_copy(att[:, :, 0, 2 * P:S], bank[:, :, 0:2 * P]).then_inc(dve_done, 1)
                    nc.vector.tensor_copy(att[:, :, 1, 2 * P:S], bank[:, :, 2 * P:S]).then_inc(level_read, 1)
                    steps[0] += 1

            make_factors(0, levels[0])
            for n in range(1, len(levels)):
                make_factors(n, levels[n])
                take_level(n - 1, levels[n - 1])
            take_level(len(levels) - 1, levels[-1])
            dve.wait_ge(act_done, 6)
            nc.vector.reciprocal(oinv[:, :, :], oroot[:, :, :]).then_inc(dve_done, 1)
            dve.wait_ge(dve_done, steps[0] + 1)
            nc.vector.scalar_tensor_tensor(osq[:, :, :], o[:, :, :], norm[:, 0:1], oinv[:, :, :], ALU.mult,
                                           ALU.mult).then_inc(dve_done, 1)
            dve.wait_ge(dve_done, steps[0] + 2)
            nc.vector.tensor_tensor(o[:, :, :], osq[:, :, :], rs[:, :, :], ALU.mult).then_inc(made, 1)


def modulation(nc, C, cvec, weight, bias, mod):
    n, blocks = 6 * KT, 6 * D // S
    with ExitStack() as ctx:
        sem = Sems(nc, ctx)
        w = ctx.enter_context(sbuf(nc, [P, 2, KT * S], F32))
        c, sc = [ctx.enter_context(sbuf(nc, [P, KT, 2], F32)) for _ in range(2)]
        b = ctx.enter_context(sbuf(nc, [P, n], F32))
        rows = ctx.enter_context(sbuf(nc, [2, 6 * D], F32))
        acc = ctx.enter_context(psum(nc, [P, 2, S], F32))
        turned = ctx.enter_context(psum(nc, [P, S], F32))
        c_landed, c_made, all_turned = sem.one("c_landed"), sem.one("silu_made"), sem.one("all_turned")
        w_landed, mm_done, evacuated = sem.two("w_landed"), sem.two("mm_done", 1), sem.two("evacuated", 1)
        block = ctx.enter_context(nc.Block())

        @block.sync
        def _(sp):
            sp.dma_start(c[:, :, :], cvec).then_inc(c_landed, 16)
            sp.dma_start(b[:, :], bias).then_inc(c_landed, 16)

            def body(p, s):
                sp.wait_ge(mm_done[s], p + 1)
                sp.dma_start(w[:, s, :], weight[2 * p + s]).then_inc(w_landed[s], 16)
            paired(sp, blocks, body)

        @block.scalar
        def _(act):
            act.wait_ge(c_landed, 32)
            nc.scalar.activation(sc[:, :, :], c[:, :, :], ACT.Silu).then_inc(c_made, 1)

        @block.tensor
        def _(pe):
            pe.wait_ge(c_made, 1)

            def body(p, s):
                pe.wait_ge(evacuated[s], p + 1)
                pe.wait_ge(w_landed[s], 16 * p + 16)
                for k in range(KT):
                    mm = nc.tensor.matmul(acc[0:2, s, :], sc[:, k, :], w[:, s, k * S:(k + 1) * S],
                                          start=(k == 0), stop=(k == KT - 1))
                mm.then_inc(mm_done[s], 1)
            paired(pe, blocks, body)
            for s in range(2):
                pe.wait_ge(evacuated[s], blocks // 2 + 1)
            for i in range(n):
                mm = nc.tensor.transpose(turned[:, 2 * i:2 * i + 2], rows[:, i * P:(i + 1) * P], C.ident[0:2, 0:2])
            mm.then_inc(all_turned, 1)

        @block.vector
        def _(dve):
            def body(p, s):
                dve.wait_ge(mm_done[s], p + 2)
                nc.vector.tensor_copy(rows[:, bass.ds((2 * p + s) * S, S)], acc[0:2, s, :]).then_inc(evacuated[s], 1)
            paired(dve, blocks, body)
            dve.wait_ge(c_landed, 32)
            dve.wait_ge(all_turned, 1)
            nc.vector.tensor_tensor(mod[:, :, :], turned[:, 0:2 * n].rearrange("p (t v) -> p t v", v=2),
                                    b[:, :].unsqueeze(2).to_broadcast([P, n, 2]), ALU.add)


def block2_scalars(nc, C, mod, n1, n2, lqk, g1x, g1c, g2x, lam):
    with ExitStack() as ctx:
        sem = Sems(nc, ctx)
        sb = lambda shape: ctx.enter_context(sbuf(nc, shape, F32))
        n1s, n2s, l, prod, tot, e = sb([P, KT]), sb([P, KT]), sb([P, 4, HD]), sb([P, 2, HD]), sb([P, 2]), sb([P, 2])
        landed, done, exped = sem.one("landed"), sem.one("dve_done"), sem.one("exp_done")
        block = ctx.enter_context(nc.Block())

        @block.sync
        def _(sp):
            sp.dma_start(n1s[:, :], n1).then_inc(landed, 16)
            sp.dma_start(n2s[:, :], n2).then_inc(landed, 16)
            for i in range(4):
                sp.dma_start(l[:, i, :], lqk[i].to_broadcast([P, HD])).then_inc(landed, 16)

        @block.vector
        def _(dve):
            dve.wait_ge(landed, 96)
            for g, n, at, v in ((g1x, n1s, KT, 0), (g1c, n1s, KT, 1), (g2x, n2s, 4 * KT, 0)):
                nc.vector.scalar_tensor_tensor(g[:, :], mod[:, at:at + KT, v], 1.0, n[:, :], ALU.add,
                                               ALU.mult).then_inc(done, 1)
            nc.vector.tensor_tensor(prod[:, :, :], l[:, 0:2, :], l[:, 2:4, :], ALU.mult).then_inc(done, 1)
            dve.wait_ge(done, 4)
            nc.vector.tensor_reduce(tot[:, :], prod[:, :, :], AX_X, ALU.add).then_inc(done, 1)
            dve.wait_ge(exped, 1)
            nc.vector.tensor_tensor(lam[:, :], e[:, 1:2], e[:, 0:1], ALU.subtract).then_inc(done, 1)
            dve.wait_ge(done, 6)
            nc.vector.tensor_scalar(lam[:, :], lam[:, :], 0.2, None, ALU.subtract).then_inc(done, 1)

        @block.scalar
        def _(act):
            act.wait_ge(done, 5)
            nc.scalar.activation(e[:, :], tot[:, :], ACT.Exp).then_inc(exped, 1)


def diff_combine(nc, C, od, lam, subln, mix):
    n = 4
    with ExitStack() as ctx:
        sem = Sems(nc, ctx)
        sb = lambda shape: ctx.enter_context(sbuf(nc, shape, F32))
        o, d, sq, root, inv, out, g = sb([P, 2 * n, S]), sb([P, n, S]), sb([P, n, S]), sb([P, n, S]), sb([P, n, S]), sb([P, n, S]), sb([P, 1])
        acc = ctx.enter_context(psum(nc, [P, n, S], F32))
        landed, differ, squared, summed, rooted, inverted, made, g_made, stored = [sem.one(x) for x in (
            "landed", "differ", "squared", "summed", "rooted", "inverted", "made", "gain_made", "stored")]
        block = ctx.enter_context(nc.Block())

        @block.sync
        def _(sp):
            sp.dma_start(g[:, :], subln).then_inc(landed, 16)
            sp.dma_start(o[:, :, :], od.rearrange("(n p) s -> p n s", p=P)).then_inc(landed, 16)
            sp.wait_ge(made, n)
            sp.dma_start(mix.rearrange("(n p) s -> p n s", p=P), out[:, :, :]).then_inc(stored, 16)
            sp.wait_ge(stored, 16)

        @block.vector
        def _(dve):
            dve.wait_ge(landed, 32)
            nc.vector.tensor_scalar(g[:, :], g[:, :], 0.8, None, ALU.mult).then_inc(g_made, 1)
            for h in range(n):
                nc.vector.scalar_tensor_tensor(d[:, h, :], o[:, 2 * h + 1, :], lam[:, 0:1], o[:, 2 * h, :], ALU.mult,
                                               ALU.add).then_inc(differ, 1)
            dve.wait_ge(g_made, 1)
            dve.wait_ge(differ, n)
            for h in range(n):
                dve.wait_ge(rooted, h + 1)
                nc.vector.reciprocal(inv[:, h, :], root[:, h, :]).then_inc(inverted, 1)
                dve.wait_ge(inverted, h + 1)
                nc.vector.scalar_tensor_tensor(out[:, h, :], d[:, h, :], g[:, 0:1], inv[:, h, :], ALU.mult,
                                               ALU.mult).then_inc(made, 1)

        @block.scalar
        def _(act):
            for h in range(n):
                act.wait_ge(differ, h + 1)
                nc.scalar.activation(sq[:, h, :], d[:, h, :], ACT.Square).then_inc(squared, 1)
            for h in range(n):
                act.wait_ge(summed, h + 1)
                nc.scalar.activation(root[:, h, :], acc[:, h, :], ACT.Sqrt, bias=C.eps[:, 0:1],
                                     scale=1 / P).then_inc(rooted, 1)

        @block.tensor
        def _(pe):
            for h in range(n):
                pe.wait_ge(squared, h + 1)
                nc.tensor.matmul(acc[:, h, :], C.ones[:, :], sq[:, h, :], start=True, stop=True).then_inc(summed, 1)


def turn(nc, C, count, src, take):
    with ExitStack() as ctx:
        sem = Sems(nc, ctx)
        ps = ctx.enter_context(psum(nc, [P, 4, S], F32))
        turned, taken = sem.one("turned"), sem.one("taken")
        block = ctx.enter_context(nc.Block())

        @block.tensor
        def _(pe):
            for i in range(count):
                if i >= 4:
                    pe.wait_ge(taken, i - 3)
                nc.tensor.transpose(ps[:, i % 4, 0:P], src(i), C.ident[:, :]).then_inc(turned, 1)

        @block.vector
        def _(dve):
            for i in range(count):
                dve.wait_ge(turned, i + 1)
                take(dve, i, ps[:, i % 4, 0:P]).then_inc(taken, 1)


def peer_pick(nc, C, qT, keys, stream, weights):
    T = TOPK
    with ExitStack() as ctx:
        sem = Sems(nc, ctx)
        sb = lambda shape, dt=F32: ctx.enter_context(sbuf(nc, shape, dt))
        q, kk = sb([P, 2, S]), sb([P, 2, NKEY])
        sc, sc2 = sb([P, 2, ST, NKEY]), sb([P, 2, ST, NKEY])
        val, idx, idf = sb([P, 2, ST, T]), sb([P, 2, ST, T], U32), sb([P, 2, ST, T])
        cand, cand2 = sb([P, ST, T * T]), sb([P, ST, T * T])
        best, pos, half, halff = sb([P, ST, T]), sb([P, ST, T], U32), sb([P, 2, ST, T], U32), sb([P, 2, ST, T])
        hot = sb([P, ST * T, T])
        hot2 = sb([P, ST * T, T])
        found, exps, tot, inv, shifted = sb([P, 2, ST * T]), sb([P, ST, T]), sb([P, ST]), sb([P, ST]), sb([P, ST, T])
        ps = ctx.enter_context(psum(nc, [P, 2, S], F32))
        landed, exp_done, dve_done, passed = [sem.one(x) for x in ("landed", "exp_done", "dve_done", "waits_passed")]
        mm_done, copied, topped = [sem.one(x, 1) for x in ("mm_done", "copied", "topped")]
        block = ctx.enter_context(nc.Block())
        SHIFT_AT = 2 * ST * 5 + 1 + ST * 5 + 1
        STEPS = SHIFT_AT + 2 + 1 + 6 + 2 + 3

        @block.sync
        def _(sp):
            with sp.Fori(0, PH) as h:
                sp.wait_ge(mm_done, h + 1)
                for p in range(2):
                    sp.dma_start(q[:, p, :], qT[bass.ds((2 * h + p) * P, P), :]).then_inc(landed, 16)
                    sp.dma_start(kk[:, p, :], keys[2 * h + p]).then_inc(landed, 16)

        @block.tensor
        def _(pe):
            with pe.Fori(0, PH) as h:
                pe.wait_ge(landed, 64 * h + 64)
                pe.wait_ge(copied, 2 * h + 1)
                for p in range(2):
                    for t in range(ST):
                        mm = nc.tensor.matmul(ps[:, p, t * P:(t + 1) * P], q[:, p, t * P:(t + 1) * P], kk[:, p, :],
                                              start=True, stop=True)
                mm.then_inc(mm_done, 1)

        @block.scalar
        def _(act):
            with act.Fori(0, PH) as h:
                act.wait_ge(mm_done, h + 2)
                act.wait_ge(topped, h + 1)
                for p in range(2):
                    nc.scalar.activation(sc[:, p, :, :], ps[:, p, :].rearrange("p (t n) -> p t n", t=ST),
                                         ACT.Copy).then_inc(copied, 1)
                act.wait_ge(dve_done, STEPS * h + SHIFT_AT)
                nc.scalar.activation(exps[:, :, :], shifted[:, :, :], ACT.Exp).then_inc(exp_done, 1)

        @block.vector
        def _(dve):
            nc.vector.memset(stream[:, 2 * ST * PICKS:], 0)
            with dve.Fori(0, PH) as h:
                step = [0]

                def did(op):
                    step[0] += 1
                    op.then_inc(dve_done, 1)

                def after():
                    wait_apart(dve, dve_done, STEPS * h + step[0], passed)

                def top16(rows):
                    for x, x2, v, i in rows:
                        did(nc.vector.max(v[:, 0:8], x))
                    after()
                    for x, x2, v, i in rows:
                        did(nc.vector.max_index(i[:, 0:8], v[:, 0:8], x))
                        did(nc.vector.match_replace(x2, v[:, 0:8], x, -3e38))
                    after()
                    for x, x2, v, i in rows:
                        did(nc.vector.max(v[:, 8:16], x2))
                    after()
                    for x, x2, v, i in rows:
                        did(nc.vector.max_index(i[:, 8:16], v[:, 8:16], x2))

                wait_apart(dve, copied, 2 * h + 3, passed)
                top16([(sc[:, p, t, :], sc2[:, p, t, :], val[:, p, t, :], idx[:, p, t, :])
                       for p in range(2) for t in range(ST)])
                after()
                did(nc.vector.tensor_copy(idf[:, :, :, :], idx[:, :, :, :]))
                after()
                nc.vector.tensor_tensor(cand[:, :, :].rearrange("p t (a b) -> p t a b", a=T),
                                        val[:, 0, :, :].unsqueeze(3).to_broadcast([P, ST, T, T]),
                                        val[:, 1, :, :].unsqueeze(2).to_broadcast([P, ST, T, T]),
                                        ALU.add).then_inc(topped, 1)
                wait_apart(dve, topped, h + 2, passed)
                top16([(cand[:, t, :], cand2[:, t, :], best[:, t, :], pos[:, t, :]) for t in range(ST)])
                after()
                did(nc.vector.tensor_tensor(shifted[:, :, :], best[:, :, :], best[:, :, 0:1].to_broadcast([P, ST, T]),
                                            ALU.subtract))
                did(nc.vector.tensor_scalar(half[:, 0, :, :], pos[:, :, :], 4, None, ALU.logical_shift_right))
                did(nc.vector.tensor_scalar(half[:, 1, :, :], pos[:, :, :], T - 1, None, ALU.bitwise_and))
                after()
                did(nc.vector.tensor_copy(halff[:, :, :, :], half[:, :, :, :]))
                for p in range(2):
                    after()
                    did(nc.vector.tensor_tensor(hot[:, :, :],
                                                halff[:, p, :, :].rearrange("p t k -> p (t k)").unsqueeze(2)
                                                .to_broadcast([P, ST * T, T]),
                                                C.iota[:, :].unsqueeze(1).to_broadcast([P, ST * T, T]), ALU.is_equal))
                    after()
                    did(nc.vector.tensor_tensor(hot2[:, :, :].rearrange("p (t k) a -> p t k a", t=ST),
                                                hot[:, :, :].rearrange("p (t k) a -> p t k a", t=ST),
                                                idf[:, p, :, :].unsqueeze(2).to_broadcast([P, ST, T, T]), ALU.mult))
                    after()
                    did(nc.vector.tensor_reduce(found[:, p, :], hot2[:, :, :], AX_X, ALU.add))
                after()
                cols = bass.ds(h * T, T)
                for f in range(2):
                    did(nc.vector.scalar_tensor_tensor(
                        stream[:, 0:2 * ST * PICKS].rearrange("p (t f k) -> p t f k", f=2, k=PICKS)[:, :, f, cols],
                        found[:, 0, :].rearrange("p (t k) -> p t k", t=ST), float(NKEY),
                        found[:, 1, :].rearrange("p (t k) -> p t k", t=ST), ALU.mult, ALU.add))
                dve.wait_ge(exp_done, h + 1)
                did(nc.vector.tensor_reduce(tot[:, :], exps[:, :, :], AX_X, ALU.add))
                after()
                did(nc.vector.reciprocal(inv[:, :], tot[:, :]))
                after()
                did(nc.vector.tensor_tensor(weights[:, :, cols], exps[:, :, :],
                                            inv[:, :].unsqueeze(2).to_broadcast([P, ST, T]), ALU.mult))
                after()
                assert step[0] == STEPS, (step[0], STEPS)


RING = 8
GROUPS = PICKS // RING


def peer_experts(nc, C, h_tok, stream, weights, u, v, y):
    with ExitStack() as ctx:
        sem = Sems(nc, ctx)
        sb = lambda shape, dt=F32: ctx.enter_context(sbuf(nc, shape, dt))
        rows = sb([P, RING, D])
        h_cur, acc = sb([P, D]), sb([P, D])
        pick = sb([P, 2, RING], U32)
        dots, wcur = sb([P, 2, RING]), sb([P, 2, RING])
        a, ga, wa = sb([P, PICKS]), sb([P, PICKS]), sb([P, PICKS])
        gathered = [sem.one(f"gathered{r}") for r in range(RING)]
        used = [sem.one(f"used{r}", 1) for r in range(RING)]
        picked, tile_set, dots_kept, gelu_done, w_made, w_set = [sem.one(x) for x in (
            "picked", "tile_set", "dots_kept", "gelu_done", "w_made", "w_set")]
        y_kept = sem.one("y_kept", 1)
        passed, passed_pool = sem.one("vector_waits_passed"), sem.one("pool_waits_passed")
        block = ctx.enter_context(nc.Block())

        def steps(eng, t, f, body):
            with eng.Fori(0, GROUPS // 2) as g:
                for b in range(2):
                    body((t * 2 + f) * GROUPS + 2 * g + b, 2 * g + b, b)

        @block.gpsimd
        def _(pool):
            with pool.Fori(0, ST) as t:
                for f, table in ((0, u), (1, v)):
                    def body(n, g, b):
                        for r in range(RING):
                            if r == 0:
                                pool.wait_ge(picked, n + 1)
                            wait_apart(pool, used[r], n + 1, passed_pool)
                            pool.indirect_dma_start(
                                rows[:, r, :], None, table,
                                bass.IndirectOffsetOnAxis(ap=pick[:, b, r:r + 1], axis=0)).then_inc(gathered[r], 16)
                    steps(pool, t, f, body)

        @block.scalar
        def _(act):
            with act.Fori(0, ST) as t:
                act.wait_ge(dots_kept, GROUPS * (t + 1))
                nc.scalar.activation(ga[:, :], a[:, :], ACT.Gelu).then_inc(gelu_done, 1)

        @block.vector
        def _(dve):
            def pick_rows(n, b):
                nc.vector.tensor_copy(pick[:, b, :], stream[:, bass.ds(n * RING, RING)]).then_inc(picked, 1)

            pick_rows(0, 0)
            pick_rows(1, 1)
            with dve.Fori(0, ST) as t:
                nc.vector.tensor_copy(h_cur[:, :], h_tok[:, t, :]).then_inc(tile_set, 1)
                dve.wait_ge(y_kept, t + 1)
                nc.vector.memset(acc[:, :], 0.0).then_inc(tile_set, 1)
                wait_apart(dve, tile_set, 2 * t + 2, passed)

                def dot(n, g, b):
                    for r in range(RING):
                        dve.wait_ge(gathered[r], 16 * n + 16)
                        nc.vector.tensor_tensor_reduce(out=rows[:, r, :], in0=rows[:, r, :], in1=h_cur[:, :], scale=1.0,
                                                       scalar=0.0, op0=ALU.mult, op1=ALU.add,
                                                       accum_out=dots[:, b, r:r + 1]).then_inc(used[r], 1)
                    pick_rows(n + 2, b)
                    for r in range(RING):
                        dve.wait_ge(used[r], n + 2)
                    nc.vector.tensor_copy(a[:, bass.ds(g * RING, RING)], dots[:, b, :]).then_inc(dots_kept, 1)

                steps(dve, t, 0, dot)
                dve.wait_ge(gelu_done, t + 1)
                nc.vector.tensor_tensor(wa[:, :], ga[:, :], weights[:, t, :], ALU.mult).then_inc(w_made, 1)
                wait_apart(dve, w_made, t + 1, passed)

                def add(n, g, b):
                    nc.vector.tensor_copy(wcur[:, b, :], wa[:, bass.ds(g * RING, RING)]).then_inc(w_set, 1)
                    dve.wait_ge(w_set, GROUPS * t + g + 1)
                    for r in range(RING):
                        dve.wait_ge(gathered[r], 16 * n + 16)
                        if r:
                            dve.wait_ge(used[r - 1], n + 2)
                        else:
                            dve.wait_ge(used[RING - 1], n + 1)
                        nc.vector.scalar_tensor_tensor(acc[:, :], rows[:, r, :], wcur[:, b, r:r + 1], acc[:, :],
                                                       ALU.mult, ALU.add).then_inc(used[r], 1)
                    pick_rows(n + 2, b)

                steps(dve, t, 1, add)
                dve.wait_ge(used[RING - 1], 2 * GROUPS * (t + 1) + 1)
                nc.vector.tensor_copy(y[:, t, :], acc[:, :]).then_inc(y_kept, 1)


INPUTS = dict(
    xT=(D, S), gains1=(DEPTH, P, KT), gains2=(DEPTH, P, KT), gain_end=(P, KT),
    w_fm=(DEPTH, Z_ROWS // P, P, D), w_tm=(DEPTH, D, T_COLS), w_small=(DEPTH, P, KT, 40),
    cw1=(DEPTH, 2, P, 16, 256), cw2=(DEPTH, 2, P, 2, HD), cpos=(DEPTH, 2, P, 16),
    gla_up=(DEPTH, 16, P), gla_b=(DEPTH, P, 1), gla_g=(DEPTH, HD, 1),
    sg_w=(DEPTH, P, 4, P), sg_b=(DEPTH, 1, 4 * P), sg_lng=(DEPTH, 1, 256), sg_lnb=(DEPTH, 1, 256),
    w_out=(DEPTH, KT, P, D), w_ffn=(DEPTH, 2, FT, P, D), w_down=(DEPTH, KT, P, FT * P),
    cvec=(P, KT, 2), ctxT=(D, CTX), w_mod=(6 * D // S, P, KT * S), b_mod=(P, 6 * KT), n1=(P, KT), n2=(P, KT), n3=(P, KT),
    w2_fm=(Y_ROWS // P, P, D), w2_tm=(D, Y2_COLS), w2_out=(KT, P, D), lqk=(4, 1, HD), subln=(P, 1),
    gq_g=(P, 1), gk_g=(P, 1), wq=(2 * PH, P, D), keys=(2 * PH, P, NKEY),
    peer_u=(NKEY * NKEY, D), peer_v=(NKEY * NKEY, D),
    c_ident=(P, P), c_ones64=(P, P), c_rot=(P, P), c_rot2=(P, P), c_cos=(P, S), c_sin=(P, S), c_cos2=(P, S),
    c_sin2=(P, S), c_kcos=(HD, 2 * NC_BLK), c_ksin=(HD, 2 * NC_BLK), c_causal=(P, P), c_levels=(P, 8, P),
    c_iota=(P, TOPK), c_mask_q=(P, P), c_mask_k=(P, P), c_cmp_q=(P, ST, 32), c_cmp_k=(32, S),
)


def build(nc, A, out, stop=None):
    with ExitStack() as ctx:
        sb = lambda shape, dt=F32: ctx.enter_context(sbuf(nc, shape, dt))
        dram = lambda name, shape: nc.dram_tensor(name, shape, F32).ap()

        class C:
            pass
        C.ones, C.ident, C.neg_ident, C.ones64 = sb([P, P]), sb([P, P]), sb([P, P]), sb([P, P])
        C.ident_b, C.mask_q, C.mask_k = sb([P, P], BF16), sb([P, P], BF16), sb([P, P], BF16)
        C.eps = sb([P, 1])
        with ExitStack() as c2:
            sem = Sems(nc, c2)
            landed, made = sem.one("consts_landed"), sem.one("consts_made")
            mask_q, mask_k = [c2.enter_context(sbuf(nc, [P, P], F32)) for _ in range(2)]
            block = c2.enter_context(nc.Block())

            @block.sync
            def _(sp):
                for dst, name in ((C.ident, "c_ident"), (C.ones64, "c_ones64"), (mask_q, "c_mask_q"),
                                  (mask_k, "c_mask_k")):
                    sp.dma_start(dst[:, :], A[name]).then_inc(landed, 16)

            @block.vector
            def _(dve):
                nc.vector.memset(C.ones[:, :], 1.0).then_inc(made, 1)
                nc.vector.memset(C.eps[:, :], EPS).then_inc(made, 1)
                dve.wait_ge(landed, 64)
                nc.vector.tensor_copy(C.ident_b[:, :], C.ident[:, :]).then_inc(made, 1)
                nc.vector.tensor_copy(C.mask_q[:, :], mask_q[:, :]).then_inc(made, 1)
                nc.vector.tensor_copy(C.mask_k[:, :], mask_k[:, :]).then_inc(made, 1)
                nc.vector.tensor_scalar(C.neg_ident[:, :], C.ident[:, :], -1.0, None, ALU.mult).then_inc(made, 1)

        xT, hT = sb([P, KT, S]), sb([P, KT, S])
        block1(nc, A, C, xT, hT, stop)
        if stop in (None, "b2"):
            block2(nc, A, C, xT, hT)
        store_x(nc, xT, hT, out, stop)


def store_x(nc, xT, hT, out, stop):
    moves = [(out[k * P:(k + 1) * P, :], (xT if stop == "b1" else hT)[:, k, :]) for k in range(KT)]
    load_all(nc, moves)


def block1(nc, A, C, xT, hT, stop):
    dram = lambda name, shape: nc.dram_tensor(name, shape, F32).ap()
    zT, ztok, mix = dram("zT", (Z_ROWS, S)), dram("ztok", (S, T_COLS)), dram("mix", (D, S))
    roped = dram("roped", (768, S))
    gates_d, rank_d = dram("gates", (24, S)), dram("rank", (16, S))
    kc_d, vc_d = dram("kc", (2, HD, NC_BLK)), dram("vc", (2, NC_BLK, HD))
    load_all(nc, [(xT[:, k, :], A["xT"][k * P:(k + 1) * P, :]) for k in range(KT)])
    with nc.Fori(0, DEPTH) as l:
        with ExitStack() as ctx:
            gain = ctx.enter_context(sbuf(nc, [P, KT], F32))
            load_all(nc, [(gain[:, :], A["gains1"][l])])
            rmsnorm(nc, C, xT, gain, hT)
        project(nc, C, A["w_fm"][l], Z_ROWS // P, lambda k: hT[:, k, :], S, zT)
        project_tokens(nc, C, A["w_tm"][l], T_COLS, ST, lambda k, t: hT[:, k, t * P:(t + 1) * P], ztok)
        gates_and_rank(nc, C, A["w_small"][l], hT, gates_d, rank_d)
        with ExitStack() as ctx:
            sb = lambda shape, dt=F32: ctx.enter_context(sbuf(nc, shape, dt))
            w1s, w1_landed = sb([P, 2, 16, 256]), Sems(nc, ctx).one("w1_landed")
            for j in range(2):
                nc.sync.dma_start(w1s[:, j, :, :], A["cw1"][l, j]).then_inc(w1_landed, 16)
            cos, sin, C.rot, C.kc_cos, C.kc_sin = sb([P, S]), sb([P, S]), sb([P, P]), sb([HD, 2 * NC_BLK]), sb([HD, 2 * NC_BLK])
            load_all(nc, [(cos[:, :], A["c_cos"]), (sin[:, :], A["c_sin"]), (C.rot[:, :], A["c_rot"]),
                          (C.kc_cos[:, :], A["c_kcos"]), (C.kc_sin[:, :], A["c_ksin"])])
            rope(nc, C, zT[Z_Q:Z_Q + 512, :], roped[0:512, :], 4, cos, sin, C.rot)
            rope(nc, C, zT[Z_KS:Z_KW + P, :], roped[512:768, :], 2, cos, sin, C.rot)
            compress(nc, C, zT, w1s, w1_landed, A["cw2"][l], A["cpos"][l], kc_d, vc_d)
        with ExitStack() as ctx:
            sb = lambda shape, dt=F32: ctx.enter_context(sbuf(nc, shape, dt))
            heads, cmp_q, cmp_k = sb([HD, 8, S]), sb([P, ST, 32], BF16), sb([32, S], BF16)
            cast_masks(nc, A["c_cmp_q"], A["c_cmp_k"], cmp_q, cmp_k)
            q_src = lambda g, s: roped[bass.ds(g * 4 * HD + s * HD, HD), :]
            gate = lambda j: (lambda g, s: gates_d[bass.ds(g * 12 + s * 3 + j, 1), :].to_broadcast([HD, S]))
            tokens = lambda c: (lambda g, s: ztok[:, bass.ds(g * HD + c, HD)].rearrange("(t p) d -> p t d", p=P))
            attention(nc, C, 2, q_src, lambda g, s: kc_d[g], lambda g, s: vc_d[g], NC_BLK, False, HD, None,
                      gate=gate(0), acc=heads, first=True, own_mask=(cmp_q, cmp_k))
            for j, krow, vcol in ((1, 512, T_VS), (2, 640, T_VW)):
                attention(nc, C, 2, q_src, lambda g, s, krow=krow: roped[bass.ds(g * HD + krow, HD), :],
                          tokens(vcol), S, True, HD, None, gate=gate(j), acc=heads)
            load_all(nc, [(mix[0:512, :].rearrange("(h p) s -> p h s", p=HD), heads[:, :, :])])
        with ExitStack() as ctx:
            C.level_mask = ctx.enter_context(sbuf(nc, [P, 8, P], F32))
            load_all(nc, [(C.level_mask[:, :, :], A["c_levels"])])
            gla(nc, C, zT, ztok, rank_d, A["gla_up"][l], A["gla_b"][l], A["gla_g"][l], mix)
        with ExitStack() as ctx:
            C.causal = ctx.enter_context(sbuf(nc, [P, P], F32))
            load_all(nc, [(C.causal[:, :], A["c_causal"])])
            spatial_gate(nc, C, zT, ztok, A["sg_w"][l], A["sg_b"][l], A["sg_lng"][l], A["sg_lnb"][l], mix)
        load_all(nc, [(hT[:, k, :], mix[k * P:(k + 1) * P, :]) for k in range(KT)])
        project_add(nc, C, A["w_out"][l], KT, lambda k: hT[:, k, :], xT)
        with ExitStack() as ctx:
            gain = ctx.enter_context(sbuf(nc, [P, KT], F32))
            load_all(nc, [(gain[:, :], A["gains2"][l])])
            rmsnorm(nc, C, xT, gain, hT)
        with ExitStack() as ctx:
            a_high, a_low = [ctx.enter_context(sbuf(nc, [P, FT, S], F32R)) for _ in range(2)]
            ffn_up(nc, C, A["w_ffn"][l], hT, a_high, a_low)
            project_add_split(nc, C, A["w_down"][l], FT, lambda k: a_high[:, k, :], lambda k: a_low[:, k, :], xT)
    with ExitStack() as ctx:
        gain = ctx.enter_context(sbuf(nc, [P, KT], F32))
        load_all(nc, [(gain[:, :], A["gain_end"])])
        rmsnorm(nc, C, xT, gain, hT)
    load_all(nc, [(xT[:, :, :], hT[:, :, :])])


def block2(nc, A, C, xT, hT):
    dram = lambda name, shape: nc.dram_tensor(name, shape, F32).ap()
    N2 = CTX + S
    y, yc = dram("y", (Y_ROWS, S)), dram("yc", (YC_ROWS, CTX))
    ytok = dram("ytok", (N2, Y2_COLS))
    qr, kr = dram("qr", (1024, S)), dram("kr", (YC_ROWS, N2))
    od, mix2, qp = dram("od", (1024, S)), dram("mix2", (1024, S)), dram("qp", (2048, S))
    with ExitStack() as ctx:
        sb = lambda shape, dt=F32: ctx.enter_context(sbuf(nc, shape, dt))
        mod = sb([P, 6 * KT, 2])
        g1x, g1c, g2x, lam = sb([P, KT]), sb([P, KT]), sb([P, KT]), sb([P, 1])
        modulation(nc, C, A["cvec"], A["w_mod"], A["b_mod"], mod)
        block2_scalars(nc, C, mod, A["n1"], A["n2"], A["lqk"], g1x, g1c, g2x, lam)
        part = lambda j, v: mod[:, j * KT:(j + 1) * KT, v]
        rmsnorm(nc, C, xT, g1x, hT, shift=part(0, 0))
        project(nc, C, A["w2_fm"], Y_ROWS // P, lambda k: hT[:, k, :], S, y)
        project_tokens(nc, C, A["w2_tm"], Y2_COLS, ST, lambda k, t: hT[:, k, t * P:(t + 1) * P], ytok[CTX:N2, :])
        with ExitStack() as c2:
            ctxT = c2.enter_context(sbuf(nc, [P, KT, CTX], F32))
            load_all(nc, [(ctxT[:, k, :], A["ctxT"][k * P:(k + 1) * P, :]) for k in range(KT)])
            rmsnorm(nc, C, ctxT, g1c, hT, n=CTX, shift=part(0, 1))
        project(nc, C, A["w2_fm"][8:13], YC_ROWS // P, lambda k: hT[:, k, 0:CTX], CTX, yc)
        project_tokens(nc, C, A["w2_tm"], Y2_COLS, CTX // P, lambda k, t: hT[:, k, t * P:(t + 1) * P], ytok[0:CTX, :])
        with ExitStack() as c2:
            sb2 = lambda shape, dt=F32: c2.enter_context(sbuf(nc, shape, dt))
            cos, sin, rot, gqg, gkg = sb2([P, S]), sb2([P, S]), sb2([P, P]), sb2([P, 1]), sb2([P, 1])
            load_all(nc, [(cos[:, :], A["c_cos2"]), (sin[:, :], A["c_sin2"]), (rot[:, :], A["c_rot2"]),
                          (gqg[:, :], A["gq_g"]), (gkg[:, :], A["gk_g"])])
            rope(nc, C, y[0:512, :], qr[0:512, :], 4, cos, sin, rot)
            rope(nc, C, y[512:1024, :], qr[512:1024, :], 4, cos, sin, rot, head_gain=gqg[:, 0:1])
            rope(nc, C, y[1024:1536, :], kr[0:512, :], 4, cos, sin, rot, col0=CTX)
            rope(nc, C, y[1536:1664, :], kr[512:640, :], 1, cos, sin, rot, col0=CTX, head_gain=gkg[:, 0:1])
            rope(nc, C, yc[512:640, :], kr[512:640, :], 1, None, None, None, cols=CTX, head_gain=gkg[:, 0:1])
        load_all(nc, [(kr[0:512, 0:CTX], yc[0:512, :])])
        attention(nc, C, 2, lambda o, s: qr[bass.ds(o * 2 * P + s * HD, HD), :],
                  lambda o, s: kr[bass.ds(o * 2 * P + s * HD, HD), :],
                  lambda o, s: ytok[:, bass.ds(o * 2 * P + s // 2 * P, P)].rearrange("(t p) d -> p t d", p=P), N2, False,
                  P, lambda o, s: od[bass.ds((o * 4 + s) * P, P), :])
        attention(nc, C, 2, lambda g, s: qr[bass.ds(g * 4 * HD + s * HD + 512, HD), :],
                  lambda g, s: kr[bass.ds(g * HD + 512, HD), :],
                  lambda g, s: ytok[:, bass.ds(g * HD + 512, HD)].rearrange("(t p) d -> p t d", p=P), N2, False, HD,
                  lambda g, s: mix2[bass.ds(g * 4 * HD + s * HD + 512, HD), :])
        diff_combine(nc, C, od, lam, A["subln"], mix2[0:512, :])
        load_all(nc, [(hT[:, k, :], mix2[k * P:(k + 1) * P, :]) for k in range(KT)])
        project_add(nc, C, A["w2_out"], KT, lambda k: hT[:, k, :], xT, gate=part(2, 0))
        rmsnorm(nc, C, xT, g2x, hT, shift=part(3, 0))
        project(nc, C, A["wq"], 2 * PH, lambda k: hT[:, k, :], S, qp)
        with ExitStack() as c2:
            sb2 = lambda shape, dt=F32: c2.enter_context(sbuf(nc, shape, dt))
            stream = sb2([P, 2 * ST * PICKS + 2 * RING], U32)
            weights = sb2([P, ST, PICKS])
            with ExitStack() as c3:
                C.iota = c3.enter_context(sbuf(nc, [P, TOPK], F32))
                load_all(nc, [(C.iota[:, :], A["c_iota"])])
                peer_pick(nc, C, qp, A["keys"], stream, weights)
            h_tok, yt = sb2([P, ST, D]), sb2([P, ST, D])
            at = lambda i: (i // KT, slice(i % KT * P, (i % KT + 1) * P), i % KT, slice(i // KT * P, (i // KT + 1) * P))

            def to_tokens(dve, i, tile):
                t, cols, k, toks = at(i)
                return nc.vector.tensor_copy(h_tok[:, t, cols], tile)
            turn(nc, C, ST * KT, lambda i: hT[:, at(i)[2], at(i)[3]], to_tokens)
            peer_experts(nc, C, h_tok, stream, weights, A["peer_u"], A["peer_v"], yt)

            def add_back(dve, i, tile):
                t, cols, k, toks = at(i)
                return nc.vector.scalar_tensor_tensor(xT[:, k, toks], tile, mod[:, 5 * KT + k, 0:1], xT[:, k, toks],
                                                      ALU.mult, ALU.add)
            turn(nc, C, ST * KT, lambda i: yt[:, at(i)[0], at(i)[1]], add_back)
        with ExitStack() as c2:
            gain = c2.enter_context(sbuf(nc, [P, KT], F32))
            load_all(nc, [(gain[:, :], A["n3"])])
            rmsnorm(nc, C, xT, gain, hT)


def constants():
    f = np.float32
    i = np.arange(P)
    c = {}
    c["c_ident"] = np.eye(P, dtype=f)
    c["c_ones64"] = (i[:, None] // HD == i[None, :] // HD).astype(f)

    def turned(half):
        r = np.zeros((P, P), f)
        for m in range(P):
            if m % (2 * half) < half:
                r[m + half, m] = -1
            else:
                r[m - half, m] = 1
        return r
    c["c_rot"], c["c_rot2"] = turned(32), turned(16)

    def table(pos, half):
        inv = (1.0 / (f(10000.0) ** (np.arange(half, dtype=f) / f(half)))).astype(f)
        ang = (pos.astype(f)[None, :] * inv[:, None]).astype(f)
        return np.concatenate([np.cos(ang)] * 2).astype(f), np.concatenate([np.sin(ang)] * 2).astype(f)
    pos = np.arange(S)
    cos, sin = table(pos, 32)
    c["c_cos"], c["c_sin"] = np.tile(cos, (2, 1)), np.tile(sin, (2, 1))
    cos, sin = table(np.arange(NC_BLK) * 16 + 31, 32)
    c["c_kcos"], c["c_ksin"] = np.tile(cos, (1, 2)), np.tile(sin, (1, 2))
    rc, rs = table(pos // 64, 16)
    cc, cs = table(pos % 64, 16)
    c["c_cos2"], c["c_sin2"] = np.concatenate([rc, cc, rc, cc]), np.concatenate([rs, cs, rs, cs])
    c["c_causal"] = (i[None, :] >= i[:, None]).astype(f)
    lv = np.zeros((P, 8, P), f)
    lv[:, 0] = np.eye(P)
    for n, s in enumerate(GLA_LEVELS[:7]):
        same = i[:, None] // s == i[None, :] // s
        lv[:, n + 1] = same & (i[:, None] % s < s // 2) & (i[None, :] % s >= s // 2)
    c["c_levels"] = lv
    c["c_iota"] = np.tile(np.arange(TOPK, dtype=f), (P, 1))
    c["c_mask_q"] = np.where(i[None, :] > i[:, None], MASK, 0).astype(f)
    c["c_mask_k"] = np.where(i[:, None] > i[None, :], MASK, 0).astype(f)
    end = np.arange(32) * 16 + 31
    t = np.arange(S)
    ck = np.where(end[:, None] > t[None, :], MASK, 0)
    c["c_cmp_k"] = ck.astype(f)
    c["c_cmp_q"] = np.ascontiguousarray(ck.T.reshape(ST, P, 32).transpose(1, 0, 2)).astype(f)
    return c


def tiles(w):
    K, N = w.shape
    return np.ascontiguousarray(w.reshape(K // P, P, N // P, P).transpose(2, 1, 0, 3).reshape(N // P, P, K))


def columns(v):
    return np.ascontiguousarray(v.reshape(-1, P).T)


def laid_out(I):
    L = range(DEPTH)
    a = {}
    a["xT"] = I["x"][0].T
    a["gains1"] = np.stack([columns(I["attn_norm"][l]) for l in L])
    a["gains2"] = np.stack([columns(I["ffn_norm"][l]) for l in L])
    a["gain_end"] = columns(I["final_norm"])
    w = I["w_in"]
    cat = lambda *parts: np.concatenate([w[:, :, s:s + n] for s, n in parts], axis=2)
    fm = cat((0, 512), (512, 128), (640, 128), (768, 128), (1024, 128), (1304, 128), (1432, 128), (1832, 256), (2088, 256))
    a["w_fm"] = np.stack([tiles(fm[l]) for l in L])
    a["w_tm"] = cat((896, 128), (1152, 128), (1560, 256), (2344, 256))
    small = cat((1280, 24), (1816, 16))
    a["w_small"] = small.reshape(DEPTH, KT, P, 40).transpose(0, 2, 1, 3)
    a["cw1"] = np.stack([I["cmp_w1_k"], I["cmp_w1_v"]], 1).reshape(DEPTH, 2, 16, P, 256).transpose(0, 1, 3, 2, 4)
    a["cw2"] = np.stack([I["cmp_w2_k"], I["cmp_w2_v"]], 1).reshape(DEPTH, 2, 2, P, HD).transpose(0, 1, 3, 2, 4)
    a["cpos"] = np.stack([I["cmp_pos_k"], I["cmp_pos_v"]], 1).reshape(DEPTH, 2, 16, P).transpose(0, 1, 3, 2)
    a["gla_up"] = I["gla_w_up"]
    a["gla_b"] = I["gla_b_up"][:, :, None]
    a["gla_g"] = I["gla_norm"][:, :, None]
    a["sg_w"] = I["sg_w"].transpose(0, 3, 1, 2)
    a["sg_b"] = I["sg_b"].reshape(DEPTH, 1, 4 * P)
    a["sg_lng"], a["sg_lnb"] = I["sg_ln_g"][:, None, :], I["sg_ln_b"][:, None, :]
    a["w_out"] = np.stack([tiles(I["w_out"][l]) for l in L])
    a["w_ffn"] = np.stack([np.stack([tiles(I["w_gate"][l]), tiles(I["w_up"][l])]) for l in L])
    a["w_down"] = np.stack([tiles(I["w_down"][l]) for l in L])
    a["cvec"] = np.stack([columns(I["c_2"][0]), columns(I["c_ctx_2"])], 2)
    a["ctxT"] = I["ctx_2"][0].T
    a["w_mod"] = I["w_mod_2"][0].reshape(KT, P, 6 * D // S, S).transpose(2, 1, 0, 3).reshape(6 * D // S, P, KT * S)
    a["b_mod"] = columns(I["b_mod_2"][0])
    a["n1"], a["n2"], a["n3"] = columns(I["norm1_g_2"][0]), columns(I["norm2_g_2"][0]), columns(I["final_norm_g_2"])
    w = I["w_in_2"]
    a["w2_fm"] = tiles(cat((0, 512), (1536, 512), (512, 512), (2048, 128))[0])
    a["w2_tm"] = cat((1024, 512), (2176, 128))[0]
    a["w2_out"] = tiles(I["w_out_2"][0])
    a["lqk"] = np.stack([I["diff_lq1_2"], I["diff_lq2_2"], I["diff_lk1_2"], I["diff_lk2_2"]])
    a["subln"] = I["diff_subln_g_2"][0][:, None]
    a["gq_g"], a["gk_g"] = [np.tile(I[n][0], 2)[:, None] for n in ("gqa_q_norm_g_2", "gqa_k_norm_g_2")]
    a["wq"] = tiles(I["peer_wq_2"][0])
    a["keys"] = I["peer_subkeys_2"][0].reshape(2 * PH, NKEY, P).transpose(0, 2, 1)
    a["peer_u"], a["peer_v"] = I["peer_u_2"][0], I["peer_v_2"][0]
    a.update(constants())
    return {n: np.ascontiguousarray(a[n]) for n in INPUTS}


def kernel(**inputs):
    import concourse.bacc as bacc
    from concourse.bass_utils import run_bass_kernel_spmd
    nc = bacc.Bacc("TRN2", target_bir_lowering=False, num_devices=1)
    arrays = laid_out({n: np.asarray(v) for n, v in inputs.items()})
    args = {}
    for n, shape in INPUTS.items():
        assert arrays[n].shape == tuple(shape), (n, arrays[n].shape, shape)
        args[n] = nc.dram_tensor(n, shape, F32, kind="ExternalInput").ap()
    out = nc.dram_tensor("out_x", (D, S), F32, kind="ExternalOutput").ap()
    build(nc, args, out)
    got = run_bass_kernel_spmd(nc, [arrays], core_ids=[0]).results[0]["out_x"]
    return np.ascontiguousarray(got.T)[None]
```
